# Optimizing a Trainium2 kernel written in Bass

```python
import math
import jax, jax.numpy as jnp
from jax import lax
import numpy as np

D_MODEL = 1024
BATCH = 1
SEQ = 256
DEPTH = 1

CHUNK = 64
Q_BLOCK = 128

MLA_HEADS = 8
QK_NOPE = 64
QK_ROPE = 32
V_DIM = 64
Q_RANK = 256
KV_RANK = 128
ROPE_THETA = 10000.0
MLA_WIDTH = MLA_HEADS * V_DIM

SSM_GROUP = 16
SSM_STATE = 64
SSM_WIDTH = D_MODEL // 2
SSM_GROUPS = SSM_WIDTH // SSM_GROUP
DT_MIN = 1e-3
DT_MAX = 1e-1

MIX_WIDTH = MLA_WIDTH + SSM_WIDTH
IN_WIDTH = Q_RANK + KV_RANK + QK_ROPE + SSM_WIDTH

N_EXPERTS = 64
TOP_K = 8
N_GROUPS = 8
TOP_GROUPS = 4
EXPERT_FF = 256
ROUTED_SCALE = 2.5
MOE_BLOCK = 128

ALPHA = (2.0 * DEPTH) ** 0.25
BETA = (8.0 * DEPTH) ** -0.25
EPS = 1e-5

kernel_name = "hybrid_mla_s5_moe_deepnorm_block"

def layer_norm(x, g, b):
    xf = x.astype(jnp.float32)
    mu = jnp.mean(xf, axis=-1, keepdims=True)
    var = jnp.mean(jnp.square(xf - mu), axis=-1, keepdims=True)
    return ((xf - mu) * lax.rsqrt(var + EPS) * g.astype(jnp.float32) + b.astype(jnp.float32)).astype(x.dtype)

def rms_norm(x, g):
    xf = x.astype(jnp.float32)
    return (xf * lax.rsqrt(jnp.mean(xf * xf, axis=-1, keepdims=True) + EPS) * g.astype(jnp.float32)).astype(x.dtype)

def rope(x, positions):
    half = QK_ROPE // 2
    inv_freq = ROPE_THETA ** (-jnp.arange(half, dtype=jnp.float32) / half)
    ang = positions.astype(jnp.float32)[..., None] * inv_freq
    ang = ang.reshape(ang.shape[:2] + (1,) * (x.ndim - 3) + (half,))
    cos, sin = jnp.cos(ang), jnp.sin(ang)
    xf = x.astype(jnp.float32)
    x1, x2 = xf[..., :half], xf[..., half:]
    return jnp.concatenate([x1 * cos - x2 * sin, x2 * cos + x1 * sin], axis=-1).astype(x.dtype)

def mla(c_q, c_kv, k_rope_raw, positions, q_norm_g, kv_norm_g, w_uq, w_ukv):
    B, S, _ = c_q.shape
    q = jnp.einsum('bsr,rhd->bshd', rms_norm(c_q, q_norm_g), w_uq)
    q_nope, q_rope = q[..., :QK_NOPE], rope(q[..., QK_NOPE:], positions)
    kv = jnp.einsum('bsr,rhd->bshd', rms_norm(c_kv, kv_norm_g), w_ukv)
    k_nope, v = kv[..., :QK_NOPE], kv[..., QK_NOPE:]
    k_rope = rope(k_rope_raw, positions)
    scale = (QK_NOPE + QK_ROPE) ** -0.5
    chunk_id = jnp.arange(S) // CHUNK
    outs = []
    for i in range(S // Q_BLOCK):
        q0, q1 = i * Q_BLOCK, (i + 1) * Q_BLOCK
        s = (jnp.einsum('bqhn,bkhn->bhqk', q_nope[:, q0:q1], k_nope[:, :q1]).astype(jnp.float32)
             + jnp.einsum('bqhr,bkr->bhqk', q_rope[:, q0:q1], k_rope[:, :q1]).astype(jnp.float32)) * scale
        mask = chunk_id[q0:q1, None] >= chunk_id[None, :q1]
        s = jnp.where(mask, s, -jnp.inf)
        p = jax.nn.softmax(s, axis=-1).astype(v.dtype)
        outs.append(jnp.einsum('bhqk,bkhd->bqhd', p, v[:, :q1]))
    return jnp.concatenate(outs, axis=1).reshape(B, S, MLA_WIDTH)

def s5(u, lambda_re, lambda_im, log_step, b_re, b_im, c_re, c_im, d_skip, w_glu, b_glu):
    B, S, _ = u.shape
    uf = u.astype(jnp.float32).reshape(B, S, SSM_GROUPS, SSM_GROUP)
    lam = lax.complex(jnp.minimum(lambda_re.astype(jnp.float32), -1e-4),
                      lambda_im.astype(jnp.float32))
    step = jnp.exp(log_step.astype(jnp.float32))[:, None]
    lam_bar = jnp.exp(lam * step)
    b_mat = lax.complex(b_re.astype(jnp.float32), b_im.astype(jnp.float32))
    b_bar = ((lam_bar - 1.0) / lam)[..., None] * b_mat
    bu = jnp.einsum('gpc,bsgc->sbgp', b_bar, uf.astype(jnp.complex64))
    a = jnp.broadcast_to(lam_bar, (S, 1) + lam_bar.shape)

    def combine(left, right):
        a_l, b_l = left
        a_r, b_r = right
        return a_r * a_l, a_r * b_l + b_r

    _, states = lax.associative_scan(combine, (a, bu), axis=0)
    c_mat = lax.complex(c_re.astype(jnp.float32), c_im.astype(jnp.float32))
    y = jnp.einsum('gcp,sbgp->bsgc', c_mat, states).real + d_skip.astype(jnp.float32) * uf
    y = jax.nn.gelu(y.reshape(B, S, SSM_WIDTH))
    return y * jax.nn.sigmoid(y @ w_glu.astype(jnp.float32) + b_glu.astype(jnp.float32))

def moe(x, w_router, router_bias, w_gate, w_up, w_down, ws_gate, ws_up, ws_down):
    B, S, D = x.shape
    xt = x.reshape(-1, D)
    T = xt.shape[0]
    scores = jax.nn.sigmoid((xt @ w_router).astype(jnp.float32))
    sel = scores + router_bias.astype(jnp.float32)
    grp_score = lax.top_k(sel.reshape(T, N_GROUPS, N_EXPERTS // N_GROUPS), 2)[0].sum(-1)
    _, top_g = lax.top_k(grp_score, TOP_GROUPS)
    gmask = jax.nn.one_hot(top_g, N_GROUPS, dtype=jnp.float32).sum(1)
    emask = jnp.repeat(gmask, N_EXPERTS // N_GROUPS, axis=1) > 0
    _, idx = lax.top_k(jnp.where(emask, sel, -jnp.inf), TOP_K)
    w = jnp.take_along_axis(scores, idx, axis=1)
    w = w / jnp.sum(w, axis=-1, keepdims=True) * ROUTED_SCALE
    gates = jnp.einsum('tk,tke->te', w, jax.nn.one_hot(idx, N_EXPERTS, dtype=jnp.float32))

    def expert_block(args):
        xb, gb = args
        h = jax.nn.silu(jnp.einsum('td,edf->tef', xb, w_gate)) * jnp.einsum('td,edf->tef', xb, w_up)
        return jnp.einsum('tef,efd->td', h * gb[..., None].astype(h.dtype), w_down)

    routed = lax.map(expert_block, (xt.reshape(-1, MOE_BLOCK, D),
                                    gates.reshape(-1, MOE_BLOCK, N_EXPERTS)))
    shared = (jax.nn.silu(xt @ ws_gate) * (xt @ ws_up)) @ ws_down
    return (routed.reshape(T, D) + shared).reshape(B, S, D)

def setup_inputs(seed: int = 0) -> dict:
    key = jax.random.key(seed)
    ks = iter(jax.random.split(key, 40))
    nrm = lambda shape, s: jax.random.normal(next(ks), shape, jnp.float32) * s
    L = DEPTH
    x = nrm((BATCH, SEQ, D_MODEL), 1.0)
    offset = jax.random.randint(next(ks), (BATCH, 1), 0, 4096, dtype=jnp.int32)
    positions = (offset + jnp.arange(SEQ, dtype=jnp.int32)[None, :]).astype(jnp.int32)
    ln_in_g = 1.0 + nrm((D_MODEL,), 0.01)
    ln_in_b = nrm((D_MODEL,), 0.01)
    w_in = nrm((L, D_MODEL, IN_WIDTH), D_MODEL ** -0.5)
    q_norm_g = 1.0 + nrm((L, Q_RANK), 0.01)
    kv_norm_g = 1.0 + nrm((L, KV_RANK), 0.01)
    w_uq = nrm((L, Q_RANK, MLA_HEADS, QK_NOPE + QK_ROPE), Q_RANK ** -0.5)
    w_ukv = nrm((L, KV_RANK, MLA_HEADS, QK_NOPE + V_DIM), KV_RANK ** -0.5)
    w_ukv = w_ukv.at[..., QK_NOPE:].multiply(BETA)
    lambda_re = -0.5 + nrm((L, SSM_GROUPS, SSM_STATE), 0.01)
    lambda_im = math.pi * jnp.arange(SSM_STATE, dtype=jnp.float32) + nrm((L, SSM_GROUPS, SSM_STATE), 0.01)
    log_step = jax.random.uniform(next(ks), (L, SSM_GROUPS), jnp.float32,
                                  math.log(DT_MIN), math.log(DT_MAX))
    b_scale = (2.0 * SSM_GROUP) ** -0.5
    b_re = nrm((L, SSM_GROUPS, SSM_STATE, SSM_GROUP), b_scale)
    b_im = nrm((L, SSM_GROUPS, SSM_STATE, SSM_GROUP), b_scale)
    c_scale = (2.0 * SSM_STATE) ** -0.5
    c_re = nrm((L, SSM_GROUPS, SSM_GROUP, SSM_STATE), c_scale)
    c_im = nrm((L, SSM_GROUPS, SSM_GROUP, SSM_STATE), c_scale)
    d_skip = nrm((L, SSM_GROUPS, SSM_GROUP), 1.0)
    w_glu = nrm((L, SSM_WIDTH, SSM_WIDTH), SSM_WIDTH ** -0.5)
    b_glu = nrm((L, SSM_WIDTH), 0.01)
    attn_out_g = 1.0 + nrm((L, MLA_WIDTH), 0.01)
    ssm_out_g = 1.0 + nrm((L, SSM_WIDTH), 0.01)
    w_o = nrm((L, MIX_WIDTH, D_MODEL), MIX_WIDTH ** -0.5 * BETA)
    ln1_g = 1.0 + nrm((L, D_MODEL), 0.01)
    ln1_b = nrm((L, D_MODEL), 0.01)
    w_router = nrm((L, D_MODEL, N_EXPERTS), D_MODEL ** -0.5)
    router_bias = nrm((L, N_EXPERTS), 0.01)
    w_gate = nrm((L, N_EXPERTS, D_MODEL, EXPERT_FF), D_MODEL ** -0.5)
    w_up = nrm((L, N_EXPERTS, D_MODEL, EXPERT_FF), D_MODEL ** -0.5)
    w_down = nrm((L, N_EXPERTS, EXPERT_FF, D_MODEL), EXPERT_FF ** -0.5 * BETA)
    ws_gate = nrm((L, D_MODEL, EXPERT_FF), D_MODEL ** -0.5)
    ws_up = nrm((L, D_MODEL, EXPERT_FF), D_MODEL ** -0.5)
    ws_down = nrm((L, EXPERT_FF, D_MODEL), EXPERT_FF ** -0.5 * BETA)
    ln2_g = 1.0 + nrm((L, D_MODEL), 0.01)
    ln2_b = nrm((L, D_MODEL), 0.01)
    return {"x": x, "positions": positions, "ln_in_g": ln_in_g, "ln_in_b": ln_in_b,
            "w_in": w_in, "q_norm_g": q_norm_g, "kv_norm_g": kv_norm_g, "w_uq": w_uq, "w_ukv": w_ukv,
            "lambda_re": lambda_re, "lambda_im": lambda_im, "log_step": log_step,
            "b_re": b_re, "b_im": b_im, "c_re": c_re, "c_im": c_im, "d_skip": d_skip,
            "w_glu": w_glu, "b_glu": b_glu, "attn_out_g": attn_out_g, "ssm_out_g": ssm_out_g,
            "w_o": w_o, "ln1_g": ln1_g, "ln1_b": ln1_b, "w_router": w_router, "router_bias": router_bias,
            "w_gate": w_gate, "w_up": w_up, "w_down": w_down,
            "ws_gate": ws_gate, "ws_up": ws_up, "ws_down": ws_down, "ln2_g": ln2_g, "ln2_b": ln2_b}

def reference(x, positions, ln_in_g, ln_in_b, w_in, q_norm_g, kv_norm_g, w_uq, w_ukv,
              lambda_re, lambda_im, log_step, b_re, b_im, c_re, c_im, d_skip, w_glu, b_glu,
              attn_out_g, ssm_out_g, w_o, ln1_g, ln1_b, w_router, router_bias,
              w_gate, w_up, w_down, ws_gate, ws_up, ws_down, ln2_g, ln2_b):
    x = layer_norm(x, ln_in_g, ln_in_b)
    s1 = Q_RANK
    s2 = s1 + KV_RANK
    s3 = s2 + QK_ROPE
    for l in range(DEPTH):
        h = x @ w_in[l]
        c_q, c_kv, k_rope_raw, u = h[..., :s1], h[..., s1:s2], h[..., s2:s3], h[..., s3:]
        att = mla(c_q, c_kv, k_rope_raw, positions, q_norm_g[l], kv_norm_g[l], w_uq[l], w_ukv[l])
        ssm = s5(u, lambda_re[l], lambda_im[l], log_step[l], b_re[l], b_im[l], c_re[l], c_im[l],
                 d_skip[l], w_glu[l], b_glu[l]).astype(att.dtype)
        mix = jnp.concatenate([rms_norm(att, attn_out_g[l]), rms_norm(ssm, ssm_out_g[l])], axis=-1) @ w_o[l]
        x = layer_norm(ALPHA * x + mix, ln1_g[l], ln1_b[l])
        ffn = moe(x, w_router[l], router_bias[l], w_gate[l], w_up[l], w_down[l],
                  ws_gate[l], ws_up[l], ws_down[l])
        x = layer_norm(ALPHA * x + ffn, ln2_g[l], ln2_b[l])
    return x


_drawn_inputs = setup_inputs


def setup_inputs(seed=0):
    import zlib

    import numpy as np

    out = dict(_drawn_inputs(seed))
    spreads = {}
    factors = {'q_norm_g': 4.889,
     'kv_norm_g': 3.341,
     'lambda_re': 8.0,
     'b_glu': 7.143,
     'attn_out_g': 4.111,
     'ssm_out_g': 3.396,
     'ln2_g': 5.484,
     'ln2_b': 5.681}
    for name, (base, spread) in spreads.items():
        noise = np.random.default_rng([zlib.crc32(name.encode()), seed]).standard_normal(out[name].shape)
        drawn = base * np.exp(spread * noise) if base else spread * noise
        out[name] = __import__('jax').numpy.asarray(drawn.astype(out[name].dtype))
    for name, factor in factors.items():
        out[name] = (out[name] * factor).astype(out[name].dtype)
    return out
```

```python
from contextlib import ExitStack

import numpy as np

import concourse.bass as bass
from concourse import mybir

F32 = mybir.dt.float32
I32 = mybir.dt.int32
ALU = mybir.AluOpType
ACT = mybir.ActivationFunctionType
AX = mybir.AxisListType

P = 128
T = 256
TB = T // P
D = 1024
DK = D // P
QR, KVR, ROPE, SSM = 256, 128, 32, 512
CW = QR + KVR + ROPE
H, NOPE, VD = 8, 64, 64
QK = NOPE + ROPE
QKX = QK + TB
HALF = ROPE // 2
G, CH, ST = 32, 16, 64
L = 8
NC = T // L
NPW = 2 * L + 1
E, FF = 64, 256
FK = FF // P
CAP = 64
XU = T * 8 // CAP
NU = E + XU
NUP = NU + 4
SH = TB
PAIR_W = 2 * 3 * DK * FF
ALPHA = 2.0 ** 0.25
EPS = 1e-5
SCALE = float(QK) ** -0.5
ROUND = 12582912.0
NEG = -1e30
FAR = 1000.0
TWO_PI = 2 * np.pi
SIN_SCALE = 6.283185
PI_1 = 6.28125
PI_2 = float(np.floor((TWO_PI - PI_1) * 2.0 ** 21) / 2.0 ** 21)
PI_3 = float(TWO_PI - PI_1 - PI_2)

CONST_COLS = dict(ident=P, nj=P, tri=P, ones=P, iota=CAP, low8=64, invf=HALF, powers=NPW, chunk=NC,
                  qmask=4, kmask=4, eid=1, level=3, thresh=3, jx=XU,
                  eps=1, half_pi=1)


def constant_places():
    at, out = 0, {}
    for name, n in CONST_COLS.items():
        out[name] = (at, at + n)
        at += n
    return out, at


def constants():
    place, n = constant_places()
    c = np.zeros((P, n), np.float32)

    def put(name, value):
        a, b = place[name]
        c[:, a:b] = value

    p = np.arange(P)
    put("ident", np.eye(P))
    nj = np.zeros((P, P))
    nj[p[:ST] + ST, p[:ST]] = 1.0
    nj[p[:ST], p[:ST] + ST] = -1.0
    put("nj", nj)
    put("tri", p[:, None] < p[None, :])
    put("ones", 1.0)
    put("iota", np.arange(CAP))
    g = np.arange(8)
    put("low8", (g[None, :] < g[:, None]).reshape(1, 64))
    put("invf", np.float32(10000.0) ** (-np.arange(HALF, dtype=np.float32) / np.float32(HALF)))
    put("powers", list(range(L - 1, -1, -1)) + list(range(L + 1)))
    put("chunk", np.arange(NC))
    put("qmask", np.where(p < 64, NEG, 0.0)[:, None] * np.eye(TB).reshape(1, -1))
    put("kmask", (p >= 64)[:, None] * np.eye(TB).reshape(1, -1))
    put("eid", p[:, None])
    put("level", [1.0, 2.0, 3.0])
    put("thresh", [CAP * 1.0, CAP * 2.0, CAP * 3.0])
    put("jx", np.arange(XU))
    put("eps", EPS)
    put("half_pi", np.pi / 2)
    return c


def build(nc, A, out):
    place, n_const = constant_places()
    ctx = ExitStack()
    with ctx:
        def sb(name, shape, dt=F32):
            return ctx.enter_context(nc.sbuf_tensor(name, shape, dt))

        def sem(name):
            return ctx.enter_context(nc.semaphore(name))

        const = sb("const", [P, n_const])
        C = {k: const[:, a:b] for k, (a, b) in place.items()}
        ident = C["ident"]

        ring = sb("ring", [P, 2 * PAIR_W])
        keep = sb("keep", [P, 27200])
        ps = ctx.enter_context(nc.psum_tensor("ps", [P, 8, 512], F32))

        def area(base, off, *shape, rows=P):
            n = int(np.prod(shape))
            v = base[0:rows, off:off + n]
            if len(shape) == 1:
                return v
            names = "abcd"[:len(shape)]
            return v.rearrange(f"p ({' '.join(names)}) -> p {' '.join(names)}",
                               **dict(zip(names[1:], shape[1:])))

        x = area(keep, 0, TB, D)
        lnr = area(keep, 2048, 2, D)
        xT = area(keep, 4096, DK, T)
        wb = area(keep, 6144, G, P)
        wc = area(keep, 10240, G, L + 1, CH)
        toep = area(keep, 14848, G, P)
        qf = area(keep, 18944, TB, H, QKX)
        kf = area(keep, 18944 + 1568, TB, H, QKX)
        vv = area(keep, 18944 + 3136, TB, H * VD)
        kT = area(keep, 18944 + 4160, H, T)
        u1 = area(keep, 18944 + 6208, TB, SSM)
        ug = area(keep, 18944 + 7232, G, NC)
        qT = xT[:, :, :]
        att = area(keep, 18944, TB, H * VD)
        mT = xT
        wsg = area(keep, 6144, 2, DK, FF)
        wsd = area(keep, 6144 + 4096, FK, D)
        wr = area(keep, 6144 + 6144, DK, E)
        xp = area(keep, 12800, TB, DK, P)
        xg = area(keep, 14848, 2, DK, P)
        yb = area(keep, 16896, 2, D)
        tt = area(keep, 18944, 2, 512)
        hb = area(keep, 19968, FF)
        sg = area(keep, 20224, FF)
        pm = area(keep, 20480, 2, TB, 2, CAP)
        pg = area(keep, 20992, 2, TB, 2, CAP)
        ru = area(keep, 21504, TB, NUP)
        gu = area(keep, 21704, TB, NUP)
        wpre = area(ring, 0, G, L, CH)
        uc = area(keep, 18944, L, SSM, rows=NC)
        pt1 = area(ring, 0, H, 2, P)
        kall = area(ring, 4096, G, P, rows=CH)
        wtmp = area(ring, 4096, G, L, CH)
        yc = area(ring, 4096, L, G // 4, CH)
        lr = area(ring, 8192, G, NPW)
        li = area(ring, 8736, G, NPW)
        decay = area(ring, 8192, G, NC)
        cosc = area(ring, 9280, G, NC)
        sinc = area(ring, 10304, G, NC)
        wo = area(ring, 0, DK, D)
        R1 = PAIR_W
        w_in = area(ring, R1, DK, CW + SSM)
        wuq = area(ring, R1 + 7424, 2, H * QK)
        wukv = area(ring, R1 + 8960, H * (NOPE + VD))
        wglu = area(ring, R1 + 9984, 4, SSM)
        ucg = area(ring, R1, G, L, CH, rows=NC)
        bt = area(ring, 0, G // 4, P)
        sb_b = area(ring, R1, G, NC)
        sb_w = area(ring, R1 + 1024, G, NC)
        sb_z = area(ring, R1 + 2048, G, NC)
        sb_s = area(ring, R1 + 3072, G, NC + 1)
        prob = area(ring, R1 + 4128, 3072)
        bs = area(keep, 18944, G, CH)
        bbar = area(keep, 18944 + 7232, G, CH)
        jbb = area(keep, 18944 + 1024, G, CH)
        ca = area(keep, 18944 + 1536, G, CH)
        cb = area(keep, 18944 + 2048, G, CH)
        ang = area(keep, 18944 + 2560, G, NPW)
        ang2 = area(keep, 18944 + 3104, G, NPW)
        mag = area(keep, 18944 + 3648, G, NPW)
        cang = area(keep, 18944 + 4192, G, NC)
        cang2 = area(keep, 18944 + 5216, G, NC)
        nbb = area(keep, 18944 + 6272, G, CH)

        hc = area(keep, 2048, TB, CW)
        brow = area(keep, 2880, SSM, rows=1)
        junk = area(keep, 3392, 512)
        junk_mix = area(keep, 18944 + 4160 + 1024, 512)
        par = area(ring, 11328, 24, G)
        rt = area(keep, 22000, 10, TB, E)
        cmp8 = area(keep, 23280, 3, 64)
        ev = area(keep, 23500, 12, XU, rows=E)
        rte = area(keep, 24000, 2, T, rows=E)
        vec = sb("vec", [P, 15])
        drow = sb("drow", [CH, G])
        rbias = sb("rbias", [P, E])
        posi = sb("posi", [P, TB], I32)
        rp = sb("rp", [P, 8, TB, HALF])
        st6 = sb("st6", [P, TB, 2, 6])
        stat = sb("stat", [P, 48])
        sm = sb("sm", [P, 4, 8])
        ids = sb("ids", [1, NUP], I32)
        cnt = sb("cnt", [1, 2], I32)
        ut = nc.dram_tensor("u_time", [T, SSM], F32).ap()
        yt = nc.dram_tensor("y_time", [T, SSM], F32).ap()

        names = """ld_const ld_x ld_ln ld_w_in ld_par ld_attn_w ld_glu ld_wo ld_shared ld_small st_u ld_u st_y ld_y
            st_out j_c j_b j_bbar cbar_done bbar_done bb_signed wc_done wpre_done
            ln_stat ln_rstd x_ready xT_ps xT_sb proj h_sb u_sb kall_ps kall_sb wbt_ps wbt_sb kall_d kall_dma
            toep_zero cn_sq cn_rstd cn_ready cT_ps cT_sb qkv_ps qkv_sb heads_ready hT_ps hT_sb sc_ps
            smax p_sb pT_ps pT_sb pv_ps att_sb ug_ps ug_sb b_ps b_sb nb_ps w_done z_done nz_ps s_done y_ps yg yc_ps
            yc_sb yT_ps yT_sb glu_ps glu_sig ssm_ready mix_sq mix_rstd mix_ready mT_ps mT_sb mix_ps x1_ready x1T_ps
            x1T_sb router_ps sig_sb mask_ready rank_ps rank_sb rt_ps rt_sb tab_ps tab2_ps tables
            ids_ready sh_down zeroed onehot gated gath xg_sb up silu h_ready tps
            tps_sb combined down0 down1 y0 y1 final dve act pool tabs mags tt_ready rope_sin ucg_a ucg_b nbs_sb turns chunks bt_ps bt_sb j_read"""
        S = {n: sem("s_" + n) for n in names.split()}
        wgu_in = [sem(f"s_wgu_in{b}") for b in range(2)]
        wd_in = [sem(f"s_wd_in{b}") for b in range(2)]

        wg, wu, wd = A["w_gate"], A["w_up"], A["w_down"]

        def unit_w(b, u):
            off = b * PAIR_W + u * PAIR_W // 2
            return area(ring, off, 2, DK, FF), area(ring, off + 2 * DK * FF, FK, D)

        block = ctx.enter_context(nc.Block())

        def cT_of(k):
            return area(keep, 18944 + 4160 + 1024 + k * T, T)

        def yT_():
            return area(keep, 18944 + 7232, 4, T)

        def junk2(b):
            return area(keep, 18944 + 4160 + 512 * b, 512)

        def jx_():
            return nbb_wide

        nbb_wide = area(keep, 18944 + 6272, G, NPW)

        def junk3():
            return area(keep, 3392, G, CH, rows=CH)

        def pT0():
            return prob[:, 0:1024]

        def rt64(k):
            return rte[:, k, :]

        @block.sync
        def _(sp):
            sp.dma_start(const[:, :], A["const"]).then_inc(S["ld_const"], 16)
            sp.dma_start(x[:, 0, :], A["x"][0, 0:P, :]).then_inc(S["ld_x"], 16)
            sp.dma_start(x[:, 1, :], A["x"][0, P:T, :]).then_inc(S["ld_x"], 16)
            for n in range(2):
                sp.dma_start(lnr[:, n, :], A[("ln_in_g", "ln_in_b")[n]][:].partition_broadcast(P)
                             ).then_inc(S["ld_ln"], 16)
            for src, dst in (("lam", par[:, 0:3, :]), ("bstack", bs), ("cstack", ca)):
                sp.dma_start(dst, A[src]).then_inc(S["ld_par"], 16)
            sp.dma_start(w_in, A["w_in"][0].rearrange("(k p) n -> p k n", p=P)).then_inc(S["ld_w_in"], 16)
            for src, dst in (("vec", vec[:, :]), ("dskip", drow[:, :]),
                             ("pos", posi[:, :])):
                sp.dma_start(dst, A[src]).then_inc(S["ld_small"], 16)
            sp.dma_start(rbias[:, :], A["router_bias"][0, :].partition_broadcast(P)).then_inc(S["ld_small"], 16)
            sp.dma_start(wuq, A["w_uq"][0].rearrange("(k p) h d -> p k (h d)", p=P)).then_inc(S["ld_attn_w"], 16)
            sp.dma_start(wukv, A["w_ukv"][0].rearrange("p h d -> p (h d)")).then_inc(S["ld_attn_w"], 16)
            sp.dma_start(wglu, A["w_glu"][0].rearrange("(k p) n -> p k n", p=P)).then_inc(S["ld_glu"], 16)
            sp.wait_ge(S["x_ready"], 2)
            sp.dma_start(brow, A["b_glu"]).then_inc(S["ld_glu"], 16)
            sp.wait_ge(S["u_sb"], 2)
            sp.dma_start(ut.rearrange("(b p) n -> p b n", p=P), u1).then_inc(S["st_u"], 16)
            sp.wait_ge(S["st_u"], 16)
            sp.wait_ge(S["wc_done"], 1)
            sp.wait_ge(S["wpre_done"], 1)
            sp.wait_ge(S["chunks"], 1)
            sp.dma_start(uc, ut.rearrange("(c j) n -> c j n", j=L)).then_inc(S["ld_u"], 16)
            sp.wait_ge(S["kall_d"], 1)
            sp.wait_ge(S["toep_zero"], 1)
            for j in range(L):
                sp.dma_start(toep[CH * j:CH * (j + 1), :, CH * j:], kall[:, :, 0:P - CH * j]
                             ).then_inc(S["kall_dma"], 16)
            sp.wait_ge(S["yg"], 2)
            for q in range(4):
                sp.dma_start(yt.rearrange("(c i) (q n) -> q c i n", i=L, q=4)[q],
                             yc[NC * q:NC * (q + 1)].rearrange("c i r o -> c i (r o)")).then_inc(S["st_y"], 16)
            sp.wait_ge(S["st_y"], 64)
            sp.dma_start(u1, yt.rearrange("(b p) n -> p b n", p=P)).then_inc(S["ld_y"], 16)
            sp.wait_ge(S["pv_ps"], 2)
            sp.wait_ge(S["z_done"], 1)
            sp.dma_start(wo, A["w_o"][0].rearrange("(k p) n -> p k n", p=P)).then_inc(S["ld_wo"], 16)
            sp.wait_ge(S["y_ps"], 2)
            for n in range(2):
                sp.dma_start(wsg[:, n, :, :], A[("ws_gate", "ws_up")[n]][0].rearrange("(p k) f -> p k f", k=DK)
                             ).then_inc(S["ld_shared"], 16)
            sp.dma_start(wsd, A["ws_down"][0].rearrange("(p k) n -> p k n", k=FK)).then_inc(S["ld_shared"], 16)
            sp.dma_start(wr, A["w_router"][0].rearrange("(p k) n -> p k n", k=DK)).then_inc(S["ld_shared"], 16)

            def load_gate_up(b, experts):
                for u in range(2):
                    for n, w in enumerate((wg, wu)):
                        sp.dma_start(unit_w(b, u)[0][:, n, :, :],
                                     w[bass.ds(experts[u], 1)].rearrange("a (p k) f -> p (a k) f", k=DK)
                                     ).then_inc(wgu_in[b], 16)

            def load_down(b, experts):
                for u in range(2):
                    sp.dma_start(unit_w(b, u)[1],
                                 wd[bass.ds(experts[u], 1)].rearrange("a (p k) n -> p (a k) n", k=FK)
                                 ).then_inc(wd_in[b], 16)

            sp.wait_ge(S["glu_ps"], 2)
            sp.wait_ge(S["pT_ps"], 3)
            for n in range(2):
                sp.dma_start(lnr[:, n, :], A[("ln1_g", "ln1_b")[n]][0, :].partition_broadcast(P)
                             ).then_inc(S["ld_ln"], 16)
            load_gate_up(1, (2, 3))
            load_down(1, (2, 3))
            sp.wait_ge(S["mix_ps"], 2)
            load_gate_up(0, (0, 1))
            load_down(0, (0, 1))
            sp.wait_ge(S["x1_ready"], 2)
            for n in range(2):
                sp.dma_start(lnr[:, n, :], A[("ln2_g", "ln2_b")[n]][0, :].partition_broadcast(P)
                             ).then_inc(S["ld_ln"], 16)
            sp.wait_ge(S["ids_ready"], 2)
            steps = sp.value_load(cnt[0:1, 0:1], min_val=E // 4, max_val=NU // 4)
            with sp.Fori(1, steps) as s:
                for b in range(2):
                    experts = [sp.value_load(ids[0:1, bass.ds(4 * s + 2 * b + u, 1)], min_val=0, max_val=E - 1)
                               for u in range(2)]
                    sp.wait_ge(S["up"], SH + 2 * s + b - 1)
                    load_gate_up(b, experts)
                    sp.wait_ge(S["down1"], 2 * s + b - 1)
                    load_down(b, experts)
            sp.wait_ge(S["final"], TB)
            sp.dma_start(out[0].rearrange("(b p) n -> p b n", p=P), x).then_inc(S["st_out"], 16)
            sp.wait_ge(S["st_out"], 16)

        def unit_cols(t, i):
            return t[:, :, bass.ds(2 * i, 2)].unsqueeze(3).to_broadcast([P, TB, 2, CAP])

        slots = C["iota"].unsqueeze(1).unsqueeze(1).to_broadcast([P, TB, 2, CAP])

        @block.gpsimd
        def _(pool):
            n = [0]

            def step(ins):
                n[0] += 1
                ins.then_inc(S["pool"], 1)
                pool.wait_ge(S["pool"], n[0])

            def bc(t, rows, k):
                return t[:, :, rows].unsqueeze(3).to_broadcast([P, G, k, CH])

            def over(t, k):
                return t.unsqueeze(2).to_broadcast([P, G, k, CH])

            pool.wait_ge(S["cbar_done"], 1)
            pool.wait_ge(S["tabs"], 1)
            step(nc.gpsimd.tensor_copy(wc[:, :, 0, :], ca))
            step(nc.gpsimd.tensor_tensor(wc[:, :, 1:, :], bc(lr, slice(L + 1, NPW), L), over(ca, L), ALU.mult))
            step(nc.gpsimd.tensor_tensor(wtmp, bc(li, slice(L + 1, NPW), L), over(cb, L), ALU.mult))
            nc.gpsimd.tensor_tensor(wc[:, :, 1:, :], wc[:, :, 1:, :], wtmp, ALU.add).then_inc(S["wc_done"], 1)
            pool.wait_ge(S["wpre_done"], 1)
            nc.gpsimd.memset(toep, 0.0).then_inc(S["toep_zero"], 1)
            pool.wait_ge(S["x1T_ps"], 4)
            pool.wait_ge(S["mT_ps"], 4)
            nc.gpsimd.memset(yb[:, 1, 0:512], 0.0).then_inc(S["y0"], 1)
            nc.gpsimd.memset(yb[:, 1, 512:], 0.0).then_inc(S["y1"], 1)
            nc.gpsimd.memset(tt[:, 1, :], 0.0).then_inc(S["zeroed"], 1)
            pool.wait_ge(S["tables"], 1)
            pool.wait_ge(S["ids_ready"], 2)
            steps = pool.value_load(cnt[0:1, 0:1], min_val=E // 4, max_val=NU // 4)

            with pool.Fori(0, steps) as s:
                for b in range(2):
                    i = 2 * s + b
                    pool.wait_ge(S["onehot"], i + 1)
                    pool.wait_ge(S["tps"], SH + i - 1)
                    nc.gpsimd.tensor_tensor(pg[:, b], pm[:, b], unit_cols(gu, i), ALU.mult).then_inc(S["gated"], 1)

        @block.scalar
        def _(act):
            n = [0]

            def step(ins):
                n[0] += 1
                ins.then_inc(S["act"], 1)
                act.wait_ge(S["act"], n[0])

            def f(out_, in_, func, **k):
                return nc.scalar.activation(out_, in_, func, **k)

            act.wait_ge(S["ld_const"], 16)
            for b in range(TB):
                act.wait_ge(S["ln_stat"], b + 1)
                f(stat[:, 4 + b:5 + b], stat[:, 2 * b + 1:2 * b + 2], ACT.Sqrt, bias=C["eps"]).then_inc(S["ln_rstd"], 1)
            act.wait_ge(S["ld_par"], 48)
            f(par[:, 3, :], par[:, 2, :], ACT.Exp).then_inc(S["mags"], 1)
            act.wait_ge(S["j_b"], 1)
            f(nbb.rearrange("p g c -> p (g c)"), ps[:, 5, :], ACT.Copy).then_inc(S["nbs_sb"], 1)
            act.wait_ge(S["j_c"], 1)
            f(cb.rearrange("p g c -> p (g c)"), ps[:, 4, :], ACT.Copy).then_inc(S["cbar_done"], 1)
            for b in range(TB):
                for q in range(2):
                    act.wait_ge(S["xT_ps"], 2 * b + q + 1)
                    f(xT[:, 4 * q:4 * q + 4, b * P:(b + 1) * P],
                      ps[:, 2 * b + q, :].rearrange("p (k t) -> p k t", k=4), ACT.Copy).then_inc(S["xT_sb"], 1)
            act.wait_ge(S["tt_ready"], 1)
            step(f(par[:, 6, :], par[:, 4, :], ACT.Exp))
            step(f(mag, ang2, ACT.Exp))
            step(f(par[:, 8, :], par[:, 5, :], ACT.Sin))
            f(par[:, 9, :], par[:, 7, :], ACT.Sin, bias=C["half_pi"]).then_inc(S["mags"], 1)
            act.wait_ge(S["turns"], 1)
            step(f(li, ang, ACT.Sin, scale=SIN_SCALE))
            step(f(ang2, ang, ACT.Abs))
            f(lr, ang2, ACT.Sin, scale=-SIN_SCALE, bias=C["half_pi"]).then_inc(S["mags"], 1)
            act.wait_ge(S["turns"], 2)
            step(f(rp[:, 1], rp[:, 0], ACT.Sin))
            step(f(rp[:, 2], rp[:, 0], ACT.Abs))
            f(rp[:, 3], rp[:, 2], ACT.Sin, scale=-1.0, bias=C["half_pi"]).then_inc(S["rope_sin"], 1)
            act.wait_ge(S["turns"], 3)
            step(f(sinc, cang, ACT.Sin, scale=SIN_SCALE))
            step(f(cang2, cang, ACT.Abs))
            f(cosc, cang2, ACT.Sin, scale=-SIN_SCALE, bias=C["half_pi"]).then_inc(S["chunks"], 1)
            act.wait_ge(S["proj"], 4)
            act.wait_ge(S["chunks"], 1)
            for b in range(TB):
                f(hc[:, b, :], ps[:, 4 + 2 * b, 0:CW], ACT.Copy).then_inc(S["h_sb"], 1)
                f(u1[:, b, :], ps[:, 5 + 2 * b, :], ACT.Copy).then_inc(S["u_sb"], 1)
            for b in range(TB):
                act.wait_ge(S["h_sb"], b + 1)
                step(f(junk[:, 0:QR], hc[:, b, 0:QR], ACT.Square, scale=QR ** -0.5,
                       accum_out=stat[:, 8 + 2 * b:9 + 2 * b]))
                step(f(junk[:, 0:KVR], hc[:, b, QR:QR + KVR], ACT.Square, scale=KVR ** -0.5,
                       accum_out=stat[:, 9 + 2 * b:10 + 2 * b]))
            f(stat[:, 12:16], stat[:, 8:12], ACT.Sqrt, bias=C["eps"]).then_inc(S["cn_sq"], 1)
            act.wait_ge(S["cT_ps"], 1)
            act.wait_ge(S["ld_small"], 64)
            for k in range(3):
                f(cT_of(k), ps[:, 4 + k, 0:T], ACT.Copy, scale=vec[:, k:k + 1]).then_inc(S["cT_sb"], 1)
            for r in range(8):
                act.wait_ge(S["wbt_ps"], r + 1)
                f(wb[:, 4 * r:4 * r + 4, :], ps[:, r % 4, :].rearrange("p (g n) -> p g n", g=4),
                  ACT.Copy).then_inc(S["wbt_sb"], 1)
            for r in range(2):
                act.wait_ge(S["kall_ps"], r + 1)
                f(kall[:, 16 * r:16 * r + 16, :], ps[0:CH, 0:4, :].rearrange("p a (g n) -> p (a g) n", g=4),
                  ACT.Copy).then_inc(S["kall_sb"], 1)
            act.wait_ge(S["ld_u"], 16)
            uv = uc.rearrange("p j (g c) -> p g j c", g=G)
            f(ucg[:, 0:G // 2], uv[:, 0:G // 2], ACT.Copy).then_inc(S["ucg_a"], 1)
            def qkv_out(b):
                if b == 0:
                    act.wait_ge(S["ucg_a"], 1)
                    act.wait_ge(S["ucg_b"], 1)
                act.wait_ge(S["qkv_ps"], 2 * b + 1)
                f(qf[:, b, :, 0:QK].rearrange("p (a h) d -> p a h d", a=2),
                  ps[:, 4:6, 0:4 * QK].rearrange("p a (h d) -> p a h d", h=4), ACT.Copy).then_inc(S["qkv_sb"], 1)
                act.wait_ge(S["qkv_ps"], 2 * b + 2)
                kv = ps[:, 6:8, :].rearrange("p a (h d) -> p (a h) d", h=4)
                f(kf[:, b, :, 0:NOPE], kv[:, :, 0:NOPE], ACT.Copy).then_inc(S["qkv_sb"], 1)
                f(vv[:, b, :].rearrange("p (h d) -> p h d", h=H), kv[:, :, NOPE:], ACT.Copy).then_inc(S["qkv_sb"], 1)

            qkv_out(0)
            for r in range(2):
                act.wait_ge(S["ug_ps"], r + 1)
                f(ug[:, 16 * r:16 * r + 16, :], ps[:, r, :].rearrange("p (g c) -> p g c", g=16),
                  ACT.Copy).then_inc(S["ug_sb"], 1)
            qkv_out(1)
            for r in range(2):
                act.wait_ge(S["bt_ps"], r + 1)
                f(bt[:, 4 * r:4 * r + 4, :], ps[:, 2 + r, :].rearrange("p (r n) -> p r n", r=4),
                  ACT.Copy).then_inc(S["bt_sb"], 1)
            for r in range(2):
                act.wait_ge(S["b_ps"], r + 1)
                f(sb_b.rearrange("p (q r) c -> p r q c", q=4)[:, 4 * r:4 * r + 4],
                  ps[:, r, :].rearrange("p (r q c) -> p r q c", r=4, q=4), ACT.Copy).then_inc(S["b_sb"], 1)
            for t in range(2):
                dst = (qT, kT)[t]
                act.wait_ge(S["hT_ps"], t + 1)
                f(dst[0:QKX, :, :], ps[0:QKX, 4:8, :].rearrange("p a (h t) -> p (a h) t", h=2),
                  ACT.Copy).then_inc(S["hT_sb"], 1)
            def exps(r):
                act.wait_ge(S["smax"], r + 1)
                if r == 0:
                    w, heads, off = P, range(8), 0
                else:
                    w, heads, off = T, range(4 * (r - 1), 4 * r), 1024 + 1024 * (r - 1)
                bank = (4, 6, 4)[r]
                for m, h in enumerate(heads):
                    col = 16 + 8 * min(r, 1) + h
                    src = ps[:, bank:bank + 2, :].rearrange("p a n -> p (a n)")[:, m * w:(m + 1) * w]
                    last = f(prob[:, off + m * w:off + (m + 1) * w], src, ACT.Exp, scale=SCALE,
                             bias=stat[:, col:col + 1], accum_out=stat[:, col + 16:col + 17])
                    if m < len(heads) - 1:
                        last.then_inc(S["act"], 1)
                        n[0] += 1
                last.then_inc(S["p_sb"], 1)
                act.wait_ge(S["act"], n[0])

            for r in range(3):
                exps(r)
            for r in range(2):
                act.wait_ge(S["y_ps"], r + 1)
                f(yc[:, :, 4 * r:4 * r + 4, :], ps[:, r, :].rearrange("p (r i o) -> p i r o", r=4, i=L),
                  ACT.Gelu_apprx_tanh).then_inc(S["yg"], 1)
            act.wait_ge(S["yT_ps"], 1)
            f(yT_(), ps[:, 0:2, :].rearrange("p a (k t) -> p (a k) t", k=2), ACT.Copy).then_inc(S["yT_sb"], 1)
            for b in range(TB):
                act.wait_ge(S["glu_ps"], b + 1)
                f(junk2(b), ps[:, 2 + b, :], ACT.Sigmoid).then_inc(S["glu_sig"], 1)
            act.wait_ge(S["att_sb"], 2)
            for b in range(TB):
                step(f(junk_mix, att[:, b, :], ACT.Square, scale=SSM ** -0.5, accum_out=stat[:, 8 + b:9 + b]))
            act.wait_ge(S["ssm_ready"], 2)
            for b in range(TB):
                step(f(junk_mix, u1[:, b, :], ACT.Square, scale=SSM ** -0.5, accum_out=stat[:, 10 + b:11 + b]))
            f(stat[:, 12:16], stat[:, 8:12], ACT.Sqrt, bias=C["eps"]).then_inc(S["mix_sq"], 1)
            act.wait_ge(S["mT_ps"], 4)
            for k in range(8):
                f(mT[:, k, :], ps[:, k // 2, (k % 2) * T:(k % 2 + 1) * T], ACT.Copy,
                  scale=vec[:, 3 + k:4 + k]).then_inc(S["mT_sb"], 1)
            for b in range(TB):
                act.wait_ge(S["ln_stat"], 3 + b)
                f(stat[:, 4 + b:5 + b], stat[:, 2 * b + 1:2 * b + 2], ACT.Sqrt, bias=C["eps"]).then_inc(S["ln_rstd"], 1)
            for b in range(TB):
                for q in range(2):
                    act.wait_ge(S["x1T_ps"], 2 * b + q + 1)
                    f(xT[:, 4 * q:4 * q + 4, b * P:(b + 1) * P],
                      ps[:, 2 * b + q, :].rearrange("p (k t) -> p k t", k=4), ACT.Copy).then_inc(S["x1T_sb"], 1)
            act.wait_ge(S["router_ps"], 1)
            f(rt[:, 0, :, :], ps[:, 4, 0:TB * E].rearrange("p (b e) -> p b e", b=TB), ACT.Sigmoid
              ).then_inc(S["sig_sb"], 1)
            for b in range(TB):
                act.wait_ge(S["up"], b + 1)
                if b:
                    act.wait_ge(S["h_ready"], b)
                f(sg, ps[:, 6, 0:FF], ACT.Silu).then_inc(S["silu"], 1)
            act.wait_ge(S["ids_ready"], 2)
            steps = act.value_load(cnt[0:1, 0:1], min_val=E // 4, max_val=NU // 4)

            def evac_gather(b, wait_half):
                for q in range(2):
                    act.wait_ge(S["gath"], wait_half(q))
                    f(xg[:, b, 4 * q:4 * q + 4, :], ps[:, 4 + q, :].rearrange("p (k s) -> p k s", k=4),
                      ACT.Copy).then_inc(S["xg_sb"], 1)

            evac_gather(0, lambda q: q + 1)
            with act.Fori(0, steps) as s:
                for b in range(2):
                    i = 2 * s + b
                    act.wait_ge(S["up"], SH + i + 1)
                    act.wait_ge(S["h_ready"], SH + i)
                    f(sg, ps[:, 6, 0:FF], ACT.Silu).then_inc(S["silu"], 1)
                    evac_gather(1 - b, lambda q: 2 * (i + 1) + q + 1)
                    act.wait_ge(S["down0"], i + 1)
                    f(yb[:, b, 0:512], ps[:, 6, :], ACT.Copy).then_inc(S["y0"], 1)
                    act.wait_ge(S["down1"], i + 1)
                    f(yb[:, b, 512:D], ps[:, 7, :], ACT.Copy).then_inc(S["y1"], 1)
            for b in range(TB):
                act.wait_ge(S["ln_stat"], 5 + b)
                f(stat[:, 4 + b:5 + b], stat[:, 2 * b + 1:2 * b + 2], ACT.Sqrt, bias=C["eps"]).then_inc(S["ln_rstd"], 1)

        @block.vector
        def _(dve):
            n = [0]

            def step(ins):
                n[0] += 1
                ins.then_inc(S["dve"], 1)
                dve.wait_ge(S["dve"], n[0])

            def ts(o, i, a, b, op0, op1=ALU.bypass):
                if b is None:
                    return nc.vector.tensor_scalar(o, i, a, None, op0)
                return nc.vector.tensor_scalar(o, i, a, b, op0, op1)

            def tt2(o, a, b, op):
                return nc.vector.tensor_tensor(o, a, b, op)

            def layer_norm(b, k, ready):
                for q in range(2):
                    step(nc.vector.bn_stats(st6[:, b, q, :], x[:, b, 512 * q:512 * q + 512]))
                nc.vector.bn_aggr(stat[:, 2 * b:2 * b + 2], st6[:, b, :, :]).then_inc(S["ln_stat"], 1)

            def layer_norm_end(b, k, ready):
                dve.wait_ge(S["ln_rstd"], k + 1)
                step(nc.vector.reciprocal(stat[:, 6 + b:7 + b], stat[:, 4 + b:5 + b]))
                step(ts(x[:, b, :], x[:, b, :], stat[:, 2 * b:2 * b + 1], stat[:, 6 + b:7 + b], ALU.subtract, ALU.mult))
                step(tt2(x[:, b, :], x[:, b, :], lnr[:, 0, :], ALU.mult))
                tt2(x[:, b, :], x[:, b, :], lnr[:, 1, :], ALU.add).then_inc(ready, 1)

            dve.wait_ge(S["ld_x"], 32)
            for b in range(TB):
                layer_norm(b, b, S["x_ready"])
            dve.wait_ge(S["ld_par"], 48)
            ts(ca[ST:P], ca[ST:P], -1.0, None, ALU.mult).then_inc(S["bb_signed"], 1)
            dve.wait_ge(S["ld_ln"], 32)
            for b in range(TB):
                layer_norm_end(b, b, S["x_ready"])

            pr = lambda k: par[:, k, :]
            dve.wait_ge(S["ld_par"], 48)
            dve.wait_ge(S["mags"], 1)
            step(ts(pr(0), pr(0), -1e-4, None, ALU.min))
            step(tt2(pr(4), pr(0), pr(3), ALU.mult))
            step(tt2(pr(10), pr(1), pr(3), ALU.mult))
            step(ts(pr(11), pr(10), 1.0 / TWO_PI, ROUND, ALU.mult, ALU.add))
            step(ts(pr(11), pr(11), ROUND, None, ALU.subtract))
            for c in (PI_1, PI_2, PI_3):
                step(nc.vector.scalar_tensor_tensor(pr(10), pr(11), -c, pr(10), ALU.mult, ALU.add))
            step(ts(pr(5), pr(10), 3.1415925, -3.1415925, ALU.min, ALU.max))
            step(nc.vector.scalar_tensor_tensor(pr(7), pr(5), -1.0, pr(5), ALU.mult, ALU.min))
            powers = C["powers"].unsqueeze(1).to_broadcast([P, G, NPW])
            tt2(ang2, pr(4).unsqueeze(2).to_broadcast([P, G, NPW]), powers, ALU.mult).then_inc(S["tt_ready"], 1)
            dve.wait_ge(S["mags"], 2)
            re, im = pr(0), pr(1)
            step(tt2(pr(16), pr(6), pr(9), ALU.mult))
            step(ts(pr(16), pr(16), -1.0, None, ALU.add))
            step(tt2(pr(17), pr(6), pr(8), ALU.mult))
            step(tt2(pr(18), re, re, ALU.mult))
            step(tt2(pr(19), im, im, ALU.mult))
            step(tt2(pr(18), pr(18), pr(19), ALU.add))
            step(nc.vector.reciprocal(pr(18), pr(18)))
            step(tt2(pr(19), pr(16), re, ALU.mult))
            step(tt2(pr(20), pr(17), im, ALU.mult))
            step(tt2(pr(19), pr(19), pr(20), ALU.add))
            step(tt2(pr(19), pr(19), pr(18), ALU.mult))
            step(tt2(pr(20), pr(17), re, ALU.mult))
            step(tt2(pr(21), pr(16), im, ALU.mult))
            step(tt2(pr(20), pr(20), pr(21), ALU.subtract))
            step(tt2(pr(20), pr(20), pr(18), ALU.mult))
            dve.wait_ge(S["nbs_sb"], 1)
            col = lambda k: pr(k).unsqueeze(2).to_broadcast([P, G, CH])
            step(tt2(bbar, col(19), bs, ALU.mult))
            step(tt2(jbb, col(20), nbb, ALU.mult))
            tt2(bbar, bbar, jbb, ALU.subtract).then_inc(S["bbar_done"], 1)
            dve.wait_ge(S["bbar_done"], 1)
            step(ts(pr(12), pr(10), 1.0 / TWO_PI, None, ALU.mult))
            step(tt2(ang, pr(12).unsqueeze(2).to_broadcast([P, G, NPW]), powers, ALU.mult))
            step(ts(jx_(), ang, ROUND, ROUND, ALU.add, ALU.subtract))
            tt2(ang, ang, jx_(), ALU.subtract).then_inc(S["turns"], 1)
            dve.wait_ge(S["ld_small"], 64)
            step(nc.vector.tensor_copy(stat[:, 46:48], posi[:, :]))
            for b in range(TB):
                step(ts(rp[:, 4, b, :], C["invf"], stat[:, 46 + b:47 + b], None, ALU.mult))
            step(ts(rp[:, 5], rp[:, 4], 1.0 / TWO_PI, ROUND, ALU.mult, ALU.add))
            step(ts(rp[:, 5], rp[:, 5], ROUND, None, ALU.subtract))
            for c in (PI_1, PI_2, PI_3):
                step(nc.vector.scalar_tensor_tensor(rp[:, 4], rp[:, 5], -c, rp[:, 4], ALU.mult, ALU.add))
            ts(rp[:, 0], rp[:, 4], 3.1415925, -3.1415925, ALU.min, ALU.max).then_inc(S["turns"], 1)
            step(ts(pr(13), pr(12), float(L), None, ALU.mult))
            step(ts(pr(14), pr(13), ROUND, ROUND, ALU.add, ALU.subtract))
            step(tt2(pr(13), pr(13), pr(14), ALU.subtract))
            step(ts(pr(14), pr(13), 4096.0, ROUND, ALU.mult, ALU.add))
            step(ts(pr(14), pr(14), ROUND, 1.0 / 4096.0, ALU.subtract, ALU.mult))
            step(tt2(pr(15), pr(13), pr(14), ALU.subtract))
            chunks = C["chunk"].unsqueeze(1).to_broadcast([P, G, NC])
            wide = lambda k: pr(k).unsqueeze(2).to_broadcast([P, G, NC])
            step(tt2(cang, wide(14), chunks, ALU.mult))
            step(ts(cang2, cang, ROUND, ROUND, ALU.add, ALU.subtract))
            step(tt2(cang, cang, cang2, ALU.subtract))
            step(tt2(cang2, wide(15), chunks, ALU.mult))
            step(tt2(cang, cang, cang2, ALU.add))
            step(ts(cang2, cang, ROUND, ROUND, ALU.add, ALU.subtract))
            tt2(cang, cang, cang2, ALU.subtract).then_inc(S["turns"], 1)
            dve.wait_ge(S["mags"], 3)
            step(nc.vector.tensor_copy(pr(22), mag[:, :, NPW - 1]))
            step(tt2(lr, lr, mag, ALU.mult))
            tt2(li, li, mag, ALU.mult).then_inc(S["tabs"], 1)
            dve.wait_ge(S["tabs"], 1)
            dve.wait_ge(S["j_bbar"], 1)
            nc.vector.tensor_copy(jbb, ps[:, 0, :].rearrange("p (g c) -> p g c", g=G)).then_inc(S["j_read"], 1)
            dve.wait_ge(S["j_read"], 1)
            pb = lambda t: t[:, :, 0:L].unsqueeze(3).to_broadcast([P, G, L, CH])
            step(tt2(wpre, pb(lr), bbar.unsqueeze(2).to_broadcast([P, G, L, CH]), ALU.mult))
            t4 = toep.rearrange("p g (j c) -> p g j c", j=L)
            step(tt2(t4, pb(li), jbb.unsqueeze(2).to_broadcast([P, G, L, CH]), ALU.mult))
            tt2(wpre, wpre, t4, ALU.subtract).then_inc(S["wpre_done"], 1)
            dve.wait_ge(S["cn_sq"], 1)
            step(nc.vector.reciprocal(stat[:, 12:16], stat[:, 12:16]))
            for b in range(TB):
                step(ts(hc[:, b, 0:QR], hc[:, b, 0:QR], stat[:, 12 + 2 * b:13 + 2 * b], None, ALU.mult))
                ts(hc[:, b, QR:QR + KVR], hc[:, b, QR:QR + KVR], stat[:, 13 + 2 * b:14 + 2 * b], None,
                   ALU.mult).then_inc(S["cn_ready"], 1)
            dve.wait_ge(S["wc_done"], 1)
            step(nc.vector.tensor_copy(decay, pr(22).unsqueeze(2).to_broadcast([P, G, NC])))
            step(nc.vector.memset(decay[:, :, 0:1], 0.0))
            dve.wait_ge(S["kall_sb"], 2)
            step(tt2(junk3(), ident[0:CH, 0:CH].unsqueeze(1).to_broadcast([CH, G, CH]),
                     drow[:, :].unsqueeze(2).to_broadcast([CH, G, CH]), ALU.mult))
            tt2(kall[:, :, 0:CH], kall[:, :, 0:CH], junk3(), ALU.add).then_inc(S["kall_d"], 1)

            dve.wait_ge(S["ld_u"], 16)
            uv = uc.rearrange("p j (g c) -> p g j c", g=G)
            nc.vector.tensor_copy(ucg[:, G // 2:], uv[:, G // 2:]).then_inc(S["ucg_b"], 1)

            dve.wait_ge(S["rope_sin"], 1)
            def rotate(x1, x2, shape, c, s, t):
                step(tt2(t[0], x1, s, ALU.mult))
                step(tt2(t[1], x2, s, ALU.mult))
                step(tt2(t[2], x2, c, ALU.mult))
                step(tt2(t[3], x1, c, ALU.mult))
                step(tt2(x1, t[3], t[1], ALU.subtract))
                step(tt2(x2, t[2], t[0], ALU.add))

            rotate(hc[:, :, QR + KVR:QR + KVR + HALF], hc[:, :, QR + KVR + HALF:CW], None, rp[:, 3], rp[:, 1],
                   [rp[:, k] for k in (4, 5, 6, 7)])
            dve.wait_ge(S["qkv_sb"], 6)
            tmp = [area(ring, R1 + 7200 - 4 * 256 + 256 * k, TB, H, HALF) for k in range(4)]
            spread = lambda t: t.unsqueeze(2).to_broadcast([P, TB, H, HALF])
            rotate(qf[:, :, :, NOPE:NOPE + HALF], qf[:, :, :, NOPE + HALF:QK], None, spread(rp[:, 3]), spread(rp[:, 1]), tmp)
            for b in range(TB):
                step(nc.vector.tensor_copy(kf[:, b, :, NOPE:QK],
                                           hc[:, b, QR + KVR:CW].unsqueeze(1).to_broadcast([P, H, ROPE])))
            for t, m in ((qf, "qmask"), (kf, "kmask")):
                last = nc.vector.tensor_copy(t[:, :, :, QK:QKX], C[m].rearrange("p (b m) -> p b m", b=TB)
                                             .unsqueeze(2).to_broadcast([P, TB, H, TB]))
                if t is qf:
                    step(last)
            last.then_inc(S["heads_ready"], 1)

            dve.wait_ge(S["nb_ps"], 2)
            dve.wait_ge(S["b_sb"], 2)
            flat = lambda t: t.rearrange("p g c -> p (g c)")
            two = ps[:, 0:2, :].rearrange("p a n -> p (a n)")
            step(tt2(flat(sb_w), flat(sinc), two, ALU.mult))
            step(tt2(sb_z, cosc, sb_b, ALU.mult))
            step(tt2(sb_w, sb_w, sb_z, ALU.add))
            nc.vector.tensor_tensor_scan(flat(sb_z), flat(decay), flat(sb_w), 0.0, ALU.mult, ALU.add).then_inc(S["z_done"], 1)
            dve.wait_ge(S["z_done"], 1)
            dve.wait_ge(S["nz_ps"], 2)
            two = ps[:, 2:4, :].rearrange("p a n -> p (a n)")
            step(tt2(flat(sb_w), flat(sinc), two, ALU.mult))
            step(tt2(sb_b, cosc, sb_z, ALU.mult))
            step(nc.vector.memset(sb_s[:, :, 0:1], 0.0))
            tt2(sb_s[:, :, 1:], sb_b, sb_w, ALU.subtract).then_inc(S["s_done"], 1)

            for r in range(3):
                dve.wait_ge(S["sc_ps"], r + 1)
                w, m, c = ((P, 8, 16), (T, 4, 24), (T, 4, 28))[r]
                bank = (4, 6, 4)[r]
                src = ps[:, bank:bank + 2, :].rearrange("p a n -> p (a n)").rearrange("p (h k) -> p h k", h=m)
                step(nc.vector.tensor_reduce(stat[:, c:c + m], src, AX.X, ALU.max))
                ts(stat[:, c:c + m], stat[:, c:c + m], -SCALE, None, ALU.mult).then_inc(S["smax"], 1)
            dve.wait_ge(S["pT_ps"], 1)
            nc.vector.tensor_copy(pT0(), ps[:, 6:8, :].rearrange("p a n -> p (a n)")).then_inc(S["pT_sb"], 1)
            for r in range(2):
                dve.wait_ge(S["pT_ps"], 2 + r)
                bank = (4, 6)[r]
                nc.vector.tensor_copy(pt1[:, 4 * r:4 * r + 4].rearrange("p h k q -> p (h k q)"),
                                      ps[:, bank:bank + 2, :].rearrange("p a n -> p (a n)")).then_inc(S["pT_sb"], 1)
            step(nc.vector.reciprocal(stat[:, 32:48 - 2], stat[:, 32:48 - 2]) if False else
                 nc.vector.reciprocal(stat[:, 32:48], stat[:, 32:48]))
            for b in range(TB):
                dve.wait_ge(S["pv_ps"], b + 1)
                tt2(att[:, b, :].rearrange("p (h d) -> p h d", h=H), ps[:, 4 + b, :].rearrange("p (h d) -> p h d", h=H),
                    stat[:, 32 + 8 * b:40 + 8 * b].unsqueeze(2).to_broadcast([P, H, VD]), ALU.mult).then_inc(S["att_sb"], 1)
            dve.wait_ge(S["ld_y"], 16)
            for b in range(TB):
                dve.wait_ge(S["glu_sig"], b + 1)
                tt2(u1[:, b, :], u1[:, b, :], junk2(b), ALU.mult).then_inc(S["ssm_ready"], 1)
            dve.wait_ge(S["mix_sq"], 1)
            step(nc.vector.reciprocal(stat[:, 12:16], stat[:, 12:16]))
            for b in range(TB):
                ts(att[:, b, :], att[:, b, :], stat[:, 12 + b:13 + b], None, ALU.mult).then_inc(S["mix_ready"], 1)
                ts(u1[:, b, :], u1[:, b, :], stat[:, 14 + b:15 + b], None, ALU.mult).then_inc(S["mix_ready"], 1)
            for b in range(TB):
                dve.wait_ge(S["mix_ps"], b + 1)
                step(nc.vector.scalar_tensor_tensor(x[:, b, :], x[:, b, :], ALPHA,
                                                    ps[:, 4 + 2 * b:6 + 2 * b, :].rearrange("p a n -> p (a n)"),
                                                    ALU.mult, ALU.add))
                layer_norm(b, 2 + b, None)
            dve.wait_ge(S["ld_ln"], 64)
            for b in range(TB):
                layer_norm_end(b, 2 + b, S["x1_ready"])
                dve.wait_ge(S["x1_ready"], b + 1)
                step(nc.vector.tensor_copy(xp[:, b].rearrange("p k q -> p q k"),
                                           x[:, b, :].rearrange("p (q k) -> p q k", k=DK)))
                nc.vector.tensor_copy(stat[:, 8:9], stat[:, 8:9]).then_inc(S["mask_ready"], 1)

            r_ = lambda k: rt[:, k, :, :]
            dve.wait_ge(S["sig_sb"], 1)
            step(tt2(r_(1), r_(0), rbias[:, :].unsqueeze(1).to_broadcast([P, TB, E]), ALU.add))
            for b in range(TB):
                for g in range(8):
                    step(nc.vector.max(rt[:, 2, b, 8 * g:8 * g + 8], rt[:, 1, b, 8 * g:8 * g + 8]))
                top = rt[:, 2, b, :].rearrange("p (g k) -> p g k", g=8)
                gs, gn, keepg = sm[:, 0, :], sm[:, 1, :], sm[:, 2, :]
                step(tt2(gs, top[:, :, 0], top[:, :, 1], ALU.add))
                mine = gs.unsqueeze(2).to_broadcast([P, 8, 8])
                other = gs.unsqueeze(1).to_broadcast([P, 8, 8])
                c3 = lambda k: cmp8[:, k, :].rearrange("p (a c) -> p a c", a=8)
                step(tt2(c3(0), other, mine, ALU.is_gt))
                step(tt2(c3(1), other, mine, ALU.is_equal))
                step(tt2(cmp8[:, 1, :], cmp8[:, 1, :], C["low8"], ALU.mult))
                step(tt2(c3(0), c3(0), c3(1), ALU.add))
                step(nc.vector.tensor_reduce(gn, c3(0), AX.X, ALU.add))
                step(ts(keepg, gn, 4.0, None, ALU.is_lt))
                gm = keepg.unsqueeze(2).to_broadcast([P, 8, 8])
                sel = rt[:, 1, b, :].rearrange("p (g k) -> p g k", g=8)
                step(tt2(sel, sel, gm, ALU.mult))
                step(ts(sm[:, 3, :], keepg, 1e30, -1e30, ALU.mult, ALU.add))
                step(tt2(sel, sel, sm[:, 3, :].unsqueeze(2).to_broadcast([P, 8, 8]), ALU.add))
                step(nc.vector.max(sm[:, 0, :], rt[:, 1, b, :]))
                step(nc.vector.match_replace(rt[:, 2, b, :], sm[:, 0, :], rt[:, 1, b, :], -3e30))
                step(ts(rt[:, 3, b, :], rt[:, 2, b, :], -2e30, None, ALU.is_lt))
                step(tt2(rt[:, 4, b, :], rt[:, 0, b, :], rt[:, 3, b, :], ALU.mult))
                step(nc.vector.tensor_reduce(sm[:, 1, 0:1], rt[:, 4, b, :], AX.X, ALU.add))
                step(nc.vector.reciprocal(sm[:, 1, 1:2], sm[:, 1, 0:1]))
                ts(gu[:, b, 0:E], rt[:, 4, b, :], sm[:, 1, 1:2], 2.5, ALU.mult, ALU.mult).then_inc(S["mask_ready"], 1)
            dve.wait_ge(S["rank_ps"], 1)
            step(ts(r_(5), r_(3), -FAR, FAR, ALU.mult, ALU.add))
            dve.wait_ge(S["mask_ready"], 4)
            tt2(ru[:, :, 0:E], r_(5), ps[:, 5, 0:TB * E].rearrange("p (b e) -> p b e", b=TB), ALU.add).then_inc(S["rank_sb"], 1)
            ex = lambda k, w=XU: ev[:, k, 0:w]
            step(tt2(ex(0, 3), ps[0:E, 5, 128:129].to_broadcast([E, 3]), C["thresh"][0:E], ALU.is_gt))
            nc.vector.tensor_reduce(ex(1, 1), ex(0, 3), AX.X, ALU.add).then_inc(S["tables"], 1)
            dve.wait_ge(S["rt_ps"], 1)
            step(nc.vector.tensor_copy(rt64(0), ps[0:E, 7, 0:T]))
            nc.vector.tensor_copy(rt64(1), ps[0:E, 7, T:2 * T]).then_inc(S["rt_sb"], 1)
            dve.wait_ge(S["tab_ps"], 1)
            step(tt2(ex(2, 3), C["level"][0:E], ps[0:E, 5, 130:131].to_broadcast([E, 3]), ALU.add))
            step(tt2(ex(2, 3), ex(2, 3), ex(0, 3), ALU.mult))
            step(ts(ex(2, 3), ex(2, 3), -1.0, None, ALU.add))
            for l in range(3):
                step(ts(ex(3 + l), C["jx"][0:E], ev[:, 2, l:l + 1], None, ALU.is_equal))
            step(tt2(ex(6), ex(3), ex(4), ALU.add))
            step(tt2(ex(6), ex(6), ex(5), ALU.add))
            step(ts(ex(7), ex(6), -FAR, None, ALU.mult))
            for l in range(3):
                step(nc.vector.scalar_tensor_tensor(ex(7), ex(3 + l), -float(CAP * (l + 1)), ex(7), ALU.mult, ALU.add))
            nc.vector.tensor_copy(ex(8), ex(6)).then_inc(S["rt_sb"], 1)
            step(nc.vector.memset(ru[:, :, NU:], FAR))
            step(nc.vector.memset(gu[:, :, NU:], 0.0))
            dve.wait_ge(S["tab2_ps"], 1)
            step(ts(ru[:, :, E:NU], ps[:, 5, 192:192 + TB * XU].rearrange("p (b j) -> p b j", b=TB), FAR, None, ALU.add))
            step(nc.vector.tensor_copy(gu[:, :, E:NU], ps[:, 5, 256:256 + TB * XU].rearrange("p (b j) -> p b j", b=TB)))
            nc.vector.tensor_copy(ids[:, E:NU], ps[0:1, 5, 320:320 + XU]).then_inc(S["ids_ready"], 1)
            step(nc.vector.tensor_copy(ids[:, 0:E], C["iota"][0:1, :]))
            step(ts(ev[0:1, 9, 0:1], ps[0:1, 5, 352:353], 0.25, 0.75 - 0.375 + E // 4, ALU.mult, ALU.add))
            step(ts(ev[0:1, 9, 0:1], ev[0:1, 9, 0:1], ROUND, ROUND, ALU.add, ALU.subtract))
            nc.vector.tensor_copy(cnt[:, 0:1], ev[0:1, 9, 0:1]).then_inc(S["ids_ready"], 1)
            for b in range(TB):
                dve.wait_ge(S["silu"], b + 1)
                if b:
                    dve.wait_ge(S["tps"], b)
                tt2(hb, sg, ps[:, 6, FF:2 * FF], ALU.mult).then_inc(S["h_ready"], 1)
                dve.wait_ge(S["tps"], b + 1)
                nc.vector.tensor_copy(tt[:, 0, 0:FF], ps[:, 7, 0:FF]).then_inc(S["tps_sb"], 1)
                if b == 0:
                    dve.wait_ge(S["sh_down"], 1)
            dve.wait_ge(S["ids_ready"], 2)
            steps = dve.value_load(cnt[0:1, 0:1], min_val=E // 4, max_val=NU // 4)
            tt2(pm[:, 0], slots, unit_cols(ru, 0), ALU.is_equal).then_inc(S["onehot"], 1)
            with dve.Fori(0, steps) as s:
                for b in range(2):
                    i = 2 * s + b
                    dve.wait_ge(S["gath"], 2 * (i + 1))
                    dve.wait_ge(S["gated"], i + 1)
                    tt2(pm[:, 1 - b], slots, unit_cols(ru, i + 1), ALU.is_equal).then_inc(S["onehot"], 1)
                    dve.wait_ge(S["silu"], SH + i + 1)
                    dve.wait_ge(S["tps"], SH + i)
                    tt2(hb, sg, ps[:, 6, FF:2 * FF], ALU.mult).then_inc(S["h_ready"], 1)
                    dve.wait_ge(S["tps"], SH + i + 1)
                    nc.vector.tensor_copy(tt[:, b, :], ps[:, 7, :]).then_inc(S["tps_sb"], 1)
            dve.wait_ge(S["combined"], 2 * steps + 1)
            for b in range(TB):
                step(nc.vector.scalar_tensor_tensor(x[:, b, :], x[:, b, :], ALPHA,
                                                    ps[:, 2 * b:2 * b + 2, :].rearrange("p a n -> p (a n)"),
                                                    ALU.mult, ALU.add))
                layer_norm(b, 4 + b, None)
            dve.wait_ge(S["ld_ln"], 96)
            for b in range(TB):
                layer_norm_end(b, 4 + b, S["final"])

        @block.tensor
        def _(pe):
            def mm(o, l, r, start=True, stop=True, **k):
                return nc.tensor.matmul(o, l, r, start=start, stop=stop, **k)

            fl = lambda t: t.rearrange("p g c -> p (g c)")
            nj = C["nj"]
            pe.wait_ge(S["ld_const"], 16)
            pe.wait_ge(S["ld_par"], 48)
            pe.wait_ge(S["bb_signed"], 1)
            mm(ps[:, 5, :], nj, fl(bs)).then_inc(S["j_b"], 1)
            mm(ps[:, 4, :], nj, fl(ca)).then_inc(S["j_c"], 1)
            for b in range(TB):
                pe.wait_ge(S["x_ready"], b + 1)
                for q in range(2):
                    for k in range(4):
                        c = (4 * q + k) * P
                        last = nc.tensor.transpose(ps[:, 2 * b + q, k * P:(k + 1) * P], x[:, b, c:c + P], ident)
                    last.then_inc(S["xT_ps"], 1)
            pe.wait_ge(S["xT_sb"], 4)
            pe.wait_ge(S["ld_w_in"], 16)
            pe.wait_ge(S["cbar_done"], 1)
            pe.wait_ge(S["nbs_sb"], 1)
            for b in range(TB):
                if b:
                    pe.wait_ge(S["bbar_done"], 1)
                    mm(ps[:, 0, :], nj, fl(bbar)).then_inc(S["j_bbar"], 1)
                for k in range(DK):
                    l = xT[:, k, b * P:(b + 1) * P]
                    m0 = mm(ps[:, 4 + 2 * b, 0:CW], l, w_in[:, k, 0:CW], start=(k == 0), stop=(k == DK - 1))
                    m1 = mm(ps[:, 5 + 2 * b, :], l, w_in[:, k, CW:], start=(k == 0), stop=(k == DK - 1))
                m0.then_inc(S["proj"], 1)
                m1.then_inc(S["proj"], 1)
            pe.wait_ge(S["cn_ready"], 2)
            pe.wait_ge(S["u_sb"], 2)
            pe.wait_ge(S["h_sb"], 2)
            for k in range(3):
                for b in range(TB):
                    last = nc.tensor.transpose(ps[:, 4 + k, b * P:(b + 1) * P], hc[:, b, k * P:(k + 1) * P], ident)
            last.then_inc(S["cT_ps"], 1)
            pe.wait_ge(S["cT_sb"], 3)
            pe.wait_ge(S["ld_attn_w"], 32)

            def qkv(b):
                if b:
                    pe.wait_ge(S["qkv_sb"], 3)
                for a in range(2):
                    for k in range(2):
                        last = mm(ps[:, 4 + a, 0:4 * QK], cT_of(k)[:, b * P:(b + 1) * P],
                                  wuq[:, k, a * 4 * QK:(a + 1) * 4 * QK], start=(k == 0), stop=(k == 1))
                last.then_inc(S["qkv_ps"], 1)
                for a in range(2):
                    last = mm(ps[:, 6 + a, :], cT_of(2)[:, b * P:(b + 1) * P], wukv[:, a * 512:(a + 1) * 512])
                last.then_inc(S["qkv_ps"], 1)

            qkv(0)
            pe.wait_ge(S["wpre_done"], 1)
            pe.wait_ge(S["j_read"], 1)
            for r in range(8):
                if r >= 4:
                    pe.wait_ge(S["wbt_sb"], r - 3)
                for g in range(4):
                    last = nc.tensor.transpose(ps[:, r % 4, g * P:(g + 1) * P],
                                               wpre[:, 4 * r + g, :, :].rearrange("p j c -> p (j c)"), ident)
                last.then_inc(S["wbt_ps"], 1)
            pe.wait_ge(S["wc_done"], 1)
            for r in range(2):
                pe.wait_ge(S["kall_sb"], 1) if r else pe.wait_ge(S["wbt_sb"], 8)
                for g in range(16):
                    gg = 16 * r + g
                    last = mm(ps[0:CH, g // 4, (g % 4) * P:(g % 4 + 1) * P], bbar[:, gg, :],
                              wc[:, gg, 0:L, :].rearrange("p i c -> p (i c)"))
                last.then_inc(S["kall_ps"], 1)
            pe.wait_ge(S["ucg_a"], 1)
            pe.wait_ge(S["ucg_b"], 1)
            pe.wait_ge(S["kall_sb"], 2)
            for r in range(2):
                for g in range(16):
                    last = nc.tensor.transpose(ps[:, r, g * NC:(g + 1) * NC],
                                               ucg[:, 16 * r + g].rearrange("p j c -> p (j c)"), ident[0:NC, 0:NC])
                last.then_inc(S["ug_ps"], 1)
            qkv(1)
            pe.wait_ge(S["ug_sb"], 2)
            for r in range(G // 4):
                for q in range(4):
                    g = q * (G // 4) + r
                    last = mm(ps[NC * q:NC * (q + 1), 2 + r // 4, (r % 4) * P:(r % 4 + 1) * P], ug[:, g, :], wb[:, g, :])
                if r % 4 == 3:
                    last.then_inc(S["bt_ps"], 1)
            for r in range(G // 4):
                pe.wait_ge(S["bt_sb"], r // 4 + 1)
                last = nc.tensor.transpose(ps[:, r // 4, (r % 4) * P:(r % 4 + 1) * P], bt[:, r, :], ident)
                if r % 4 == 3:
                    last.then_inc(S["b_ps"], 1)
            pe.wait_ge(S["b_sb"], 2)
            for r in range(2):
                mm(ps[:, r, :], nj, sb_b[:, 16 * r:16 * r + 16, :].rearrange("p g c -> p (g c)")).then_inc(S["nb_ps"], 1)
            pe.wait_ge(S["heads_ready"], 1)
            pe.wait_ge(S["qkv_sb"], 6)
            for t in range(2):
                if t:
                    pe.wait_ge(S["hT_sb"], 1)
                for h in range(H):
                    for b in range(TB):
                        c = (h % 2) * T + b * P
                        last = nc.tensor.transpose(ps[0:QKX, 4 + h // 2, c:c + P], (qf, kf)[t][:, b, h, :], ident)
                last.then_inc(S["hT_ps"], 1)
            pe.wait_ge(S["z_done"], 1)
            for r in range(2):
                mm(ps[:, 2 + r, :], nj, sb_z[:, 16 * r:16 * r + 16, :].rearrange("p g c -> p (g c)")).then_inc(S["nz_ps"], 1)
            pe.wait_ge(S["hT_sb"], 2)

            def scores(r):
                heads = range(8) if r == 0 else range(4 * (r - 1), 4 * r)
                bank = (4, 6, 4)[r]
                w = P if r == 0 else T
                flat = ps[:, bank:bank + 2, :].rearrange("p a n -> p (a n)")
                for m, h in enumerate(heads):
                    q0 = 0 if r == 0 else P
                    last = mm(flat[:, m * w:(m + 1) * w], qT[0:QKX, h, q0:q0 + P], kT[0:QKX, h, 0:w])
                last.then_inc(S["sc_ps"], 1)

            scores(0)
            scores(1)
            pe.wait_ge(S["p_sb"], 1)
            scores(2)
            pe.wait_ge(S["s_done"], 1)
            pe.wait_ge(S["kall_dma"], 16 * L)
            for r in range(G // 4):
                spot = [ps[NC * q:NC * (q + 1), r // 4, (r % 4) * P:(r % 4 + 1) * P] for q in range(4)]
                for q in range(4):
                    mm(spot[q], ug[:, q * (G // 4) + r, :], toep[:, q * (G // 4) + r, :], stop=False)
                for q in range(4):
                    g = q * (G // 4) + r
                    last = mm(spot[q], sb_s[:, g, 0:NC], wc[:, g, 1:, :].rearrange("p i c -> p (i c)"), start=False)
                if r % 4 == 3:
                    last.then_inc(S["y_ps"], 1)
            pe.wait_ge(S["p_sb"], 2)
            for h in range(H):
                last = nc.tensor.transpose(ps[:, 6 + h // 4, (h % 4) * P:(h % 4 + 1) * P], prob[:, h * P:(h + 1) * P], ident)
            last.then_inc(S["pT_ps"], 1)
            pe.wait_ge(S["p_sb"], 3)
            for r in range(2):
                if r:
                    pe.wait_ge(S["pT_sb"], 1)
                for m in range(4):
                    for k in range(2):
                        c = 1024 + (4 * r + m) * T + k * P
                        j = 2 * m + k
                        last = nc.tensor.transpose(ps[:, (4, 6)[r] + j // 4, (j % 4) * P:(j % 4 + 1) * P],
                                                   prob[:, c:c + P], ident)
                last.then_inc(S["pT_ps"], 1)
            pe.wait_ge(S["pT_sb"], 3)
            for b in range(TB):
                for h in range(H):
                    for k in range(b + 1):
                        l = pT0()[:, h * P:(h + 1) * P] if b == 0 else pt1[:, h, k, :]
                        last = mm(ps[:, 4 + b, h * VD:(h + 1) * VD], l, vv[:, k, h * VD:(h + 1) * VD],
                                  start=(k == 0), stop=(k == b))
                last.then_inc(S["pv_ps"], 1)
            pe.wait_ge(S["ld_y"], 16)
            pe.wait_ge(S["yg"], 2)
            for k in range(4):
                for b in range(TB):
                    c = (k % 2) * T + b * P
                    last = nc.tensor.transpose(ps[:, k // 2, c:c + P], u1[:, b, k * P:(k + 1) * P], ident)
            last.then_inc(S["yT_ps"], 1)
            pe.wait_ge(S["yT_sb"], 1)
            pe.wait_ge(S["ld_glu"], 32)
            for b in range(TB):
                mm(ps[:, 2 + b, :], C["ones"][0:1, :], brow[0:1, :], stop=False)
                for k in range(4):
                    last = mm(ps[:, 2 + b, :], yT_()[:, k, b * P:(b + 1) * P], wglu[:, k, :], start=False, stop=(k == 3))
                last.then_inc(S["glu_ps"], 1)
            pe.wait_ge(S["mix_ready"], 4)
            for q in range(4):
                for k in range(2 * q, 2 * q + 2):
                    for b in range(TB):
                        src = att[:, b, k * P:(k + 1) * P] if k < 4 else u1[:, b, (k - 4) * P:(k - 3) * P]
                        last = nc.tensor.transpose(ps[:, q, (k % 2) * T + b * P:(k % 2) * T + (b + 1) * P], src, ident)
                last.then_inc(S["mT_ps"], 1)
            pe.wait_ge(S["mT_sb"], 8)
            pe.wait_ge(S["att_sb"], 2)
            pe.wait_ge(S["ld_wo"], 16)
            for b in range(TB):
                for k in range(8):
                    for c in range(2):
                        last = mm(ps[:, 4 + 2 * b + c, :], mT[:, k, b * P:(b + 1) * P], wo[:, k, c * 512:(c + 1) * 512],
                                  start=(k == 0), stop=(k == 7))
                last.then_inc(S["mix_ps"], 1)
            for b in range(TB):
                pe.wait_ge(S["mask_ready"], b + 1)
                for q in range(2):
                    for k in range(4):
                        last = nc.tensor.transpose(ps[:, 2 * b + q, k * P:(k + 1) * P], xp[:, b, 4 * q + k, :], ident)
                    last.then_inc(S["x1T_ps"], 1)
            pe.wait_ge(S["x1T_sb"], 4)
            pe.wait_ge(S["ld_shared"], 64)
            pe.wait_ge(S["x1_ready"], 2)
            for b in range(TB):
                for k in range(DK):
                    last = mm(ps[:, 4, b * E:(b + 1) * E], xT[:, k, b * P:(b + 1) * P], wr[:, k, :],
                              start=(k == 0), stop=(k == DK - 1))
            last.then_inc(S["router_ps"], 1)

            def shared_up(b):
                for k in range(DK):
                    last = mm(ps[:, 6, :], xT[:, k, b * P:(b + 1) * P], wsg[:, :, k, :], start=(k == 0), stop=(k == DK - 1))
                last.then_inc(S["up"], 1)

            def shared_down(b):
                pe.wait_ge(S["h_ready"], b + 1)
                for k in range(FK):
                    last = nc.tensor.transpose(ps[:, 7, k * P:(k + 1) * P], hb[:, k:FF:FK], ident)
                last.then_inc(S["tps"], 1)
                pe.wait_ge(S["tps_sb"], b + 1)
                for c in range(2):
                    for k in range(FK):
                        last = mm(ps[:, 2 * b + c, :], tt[:, 0, k * P:(k + 1) * P], wsd[:, k, c * 512:(c + 1) * 512],
                                  start=(k == 0), stop=False, skip_group_check=True)
                last.then_inc(S["sh_down"], 1)

            shared_up(0)
            pe.wait_ge(S["mask_ready"], 4)
            ch = rt[:, 3, :, :]
            mm(ps[:, 5, 0:E], C["tri"], ch[:, 0, :])
            mm(ps[:, 5, E:2 * E], C["ones"], ch[:, 0, :], stop=False)
            mm(ps[:, 5, E:2 * E], C["tri"], ch[:, 1, :], start=False)
            mm(ps[0:E, 5, 128:129], ch[:, 0, :], C["ones"][:, 0:1], stop=False)
            mm(ps[0:E, 5, 128:129], ch[:, 1, :], C["ones"][:, 0:1], start=False).then_inc(S["rank_ps"], 1)
            pe.wait_ge(S["tables"], 1)
            mm(ps[0:E, 5, 130:131], C["tri"][0:E, 0:E], ev[:, 1, 0:1])
            mm(ps[0:1, 5, 352:353], C["ones"][0:E, 0:1], ev[:, 1, 0:1]).then_inc(S["tab_ps"], 1)
            pe.wait_ge(S["rank_sb"], 1)
            for k, t in enumerate((ru, gu)):
                for b in range(TB):
                    last = mm(ps[0:E, 7, k * T + b * P:k * T + (b + 1) * P], t[:, b, 0:E], ident)
            last.then_inc(S["rt_ps"], 1)
            pe.wait_ge(S["rt_sb"], 2)
            for b in range(TB):
                o = ps[:, 5, 192 + b * XU:192 + (b + 1) * XU]
                mm(o, rt64(0)[:, b * P:(b + 1) * P], ev[:, 6, :], stop=False)
                mm(o, C["ones"][0:E, :], ev[:, 7, :], start=False)
                mm(ps[:, 5, 256 + b * XU:256 + (b + 1) * XU], rt64(1)[:, b * P:(b + 1) * P], ev[:, 6, :])
            mm(ps[0:1, 5, 320:320 + XU], C["eid"][0:E, :], ev[:, 6, :]).then_inc(S["tab2_ps"], 1)
            shared_down(0)
            shared_up(1)
            shared_down(1)

            pe.wait_ge(S["ids_ready"], 2)
            steps = pe.value_load(cnt[0:1, 0:1], min_val=E // 4, max_val=NU // 4)

            def gather(b):
                for q in range(2):
                    for k in range(4):
                        for t in range(TB):
                            last = mm(ps[:, 4 + q, k * P:(k + 1) * P], xp[:, t, 4 * q + k, :],
                                      pm[:, b, t].rearrange("p u s -> p (u s)"), start=(t == 0), stop=(t == TB - 1))
                    last.then_inc(S["gath"], 1)

            def combine(b):
                for t in range(TB):
                    for c in range(2):
                        last = mm(ps[:, 2 * t + c, :], tt[:, b, FF + t * P:FF + (t + 1) * P],
                                  yb[:, b, c * 512:(c + 1) * 512], start=False, stop=False, skip_group_check=True)
                last.then_inc(S["combined"], 1)

            pe.wait_ge(S["onehot"], 1)
            pe.wait_ge(S["zeroed"], 1)
            gather(0)
            with pe.Fori(0, steps) as s:
                for b in range(2):
                    i = 2 * s + b
                    pe.wait_ge(wgu_in[b], 64 * (s + 1))
                    pe.wait_ge(S["xg_sb"], 2 * (i + 1))
                    pe.wait_ge(S["y0"], i + 1)
                    for k in range(DK):
                        for u in range(2):
                            last = mm(ps[CAP * u:CAP * (u + 1), 6, :], xg[:, b, k, CAP * u:CAP * (u + 1)],
                                      unit_w(b, u)[0][:, :, k, :], start=(k == 0), stop=(k == DK - 1))
                    last.then_inc(S["up"], 1)
                    pe.wait_ge(S["onehot"], i + 2)
                    gather(1 - b)
                    pe.wait_ge(S["h_ready"], SH + i + 1)
                    pe.wait_ge(S["gated"], i + 1)
                    pe.wait_ge(S["y1"], i + 1)
                    for k in range(FK):
                        nc.tensor.transpose(ps[:, 7, k * P:(k + 1) * P], hb[:, k:FF:FK], ident)
                    for t in range(TB):
                        last = nc.tensor.transpose(ps[:, 7, FF + t * P:FF + (t + 1) * P],
                                                   pg[:, b, t].rearrange("p u s -> p (u s)"), ident)
                    last.then_inc(S["tps"], 1)
                    combine(1 - b)
                    pe.wait_ge(S["tps_sb"], SH + i + 1)
                    pe.wait_ge(wd_in[b], 32 * (s + 1))
                    for c in range(2):
                        for k in range(FK):
                            for u in range(2):
                                last = mm(ps[CAP * u:CAP * (u + 1), 6 + c, :],
                                          tt[:, b, k * P + CAP * u:k * P + CAP * (u + 1)],
                                          unit_w(b, u)[1][:, k, c * 512:(c + 1) * 512],
                                          start=(k == 0), stop=(k == FK - 1))
                        last.then_inc(S[f"down{c}"], 1)
            pe.wait_ge(S["y0"], 2 * steps + 1)
            pe.wait_ge(S["y1"], 2 * steps + 1)
            combine(1)


def kernel(**inputs):
    import concourse.bacc as bacc
    from concourse.bass_utils import run_bass_kernel_spmd

    a = {k: np.asarray(v) for k, v in inputs.items()}

    def states(re, im):
        return np.ascontiguousarray(np.concatenate([re.transpose(1, 0, 2), im.transpose(1, 0, 2)]))

    def twice(t):
        return np.concatenate([t.T, t.T])

    arrays = {"const": constants()}
    for name in ("x", "ln_in_g", "ln_in_b", "w_in", "w_uq", "w_ukv", "w_glu", "b_glu", "w_o", "ln1_g", "ln1_b",
                 "w_router", "router_bias", "ws_gate", "ws_up", "ws_down", "ln2_g", "ln2_b"):
        arrays[name] = np.ascontiguousarray(a[name])
    for name in ("w_gate", "w_up", "w_down"):
        arrays[name] = np.ascontiguousarray(a[name][0])
    step = np.broadcast_to(a["log_step"][0][None, :], (P, G))
    arrays["lam"] = np.ascontiguousarray(np.stack([twice(a["lambda_re"][0]), twice(a["lambda_im"][0]), step], 1))
    arrays["bstack"] = states(a["b_re"][0], a["b_im"][0])
    arrays["cstack"] = states(a["c_re"][0].transpose(0, 2, 1), a["c_im"][0].transpose(0, 2, 1))
    rows = [a["q_norm_g"][0], a["kv_norm_g"][0], a["attn_out_g"][0], a["ssm_out_g"][0]]
    vec = np.concatenate([r.reshape(-1, P) for r in rows])
    arrays["vec"] = np.ascontiguousarray(np.concatenate([vec, vec[:4]]).T)
    arrays["dskip"] = np.ascontiguousarray(a["d_skip"][0].T)
    arrays["pos"] = np.ascontiguousarray(a["positions"].reshape(TB, P).T)

    nc = bacc.Bacc("TRN2", target_bir_lowering=False, num_devices=1)
    A, sent = {}, {}
    for name, v in arrays.items():
        sent[f"in_{name}"] = v
        A[name] = nc.dram_tensor(f"in_{name}", v.shape, mybir.dt.from_np(v.dtype), kind="ExternalInput").ap()
    out = nc.dram_tensor("out_x", (1, T, D), F32, kind="ExternalOutput").ap()
    build(nc, A, out)
    r = run_bass_kernel_spmd(nc, [sent], core_ids=[0])
    return r.results[0]["out_x"]
```

```python
from contextlib import ExitStack

import numpy as np

import concourse.bass as bass
from concourse import mybir

F32 = mybir.dt.float32
I32 = mybir.dt.int32
ALU = mybir.AluOpType
ACT = mybir.ActivationFunctionType
AX = mybir.AxisListType

P = 128
T = 256
TB = T // P
D = 1024
DK = D // P
QR, KVR, ROPE, SSM = 256, 128, 32, 512
CW = QR + KVR + ROPE
H, NOPE, VD = 8, 64, 64
QK = NOPE + ROPE
QKX = QK + TB
HALF = ROPE // 2
G, CH, ST = 32, 16, 64
L = 8
NC = T // L
NPW = 2 * L + 1
E, FF = 64, 256
FK = FF // P
CAP = 64
XU = T * 8 // CAP
NU = E + XU
NUP = NU + 4
STEPS = E // 4
SHARED_BANK = (6, 4)
SH = TB
KEEP = 25152
PAIR_W = 2 * 3 * DK * FF
ALPHA = 2.0 ** 0.25
EPS = 1e-5
SCALE = float(QK) ** -0.5
ROUND = 12582912.0
NEG = -1e30
FAR = 1000.0
TWO_PI = 2 * np.pi
SIN_SCALE = 6.283185
PI_1 = 6.28125
PI_2 = float(np.floor((TWO_PI - PI_1) * 2.0 ** 21) / 2.0 ** 21)
PI_3 = float(TWO_PI - PI_1 - PI_2)

CONST_COLS = dict(ident=P, nj=P, tri=P, ones=P, iota=CAP, invf=HALF, powers=NPW,
                  qmask=4, kmask=4, eid=1, level=3, thresh=3,
                  eps=1, half_pi=1)


def constant_places():
    at, out = 0, {}
    for name, n in CONST_COLS.items():
        out[name] = (at, at + n)
        at += n
    return out, at


def constants():
    place, n = constant_places()
    c = np.zeros((P, n), np.float32)

    def put(name, value):
        a, b = place[name]
        c[:, a:b] = value

    p = np.arange(P)
    put("ident", np.eye(P))
    nj = np.zeros((P, P))
    nj[p[:ST] + ST, p[:ST]] = 1.0
    nj[p[:ST], p[:ST] + ST] = -1.0
    put("nj", nj)
    put("tri", p[:, None] < p[None, :])
    put("ones", 1.0)
    put("iota", np.arange(CAP))
    put("invf", np.float32(10000.0) ** (-np.arange(HALF, dtype=np.float32) / np.float32(HALF)))
    put("powers", list(range(L - 1, -1, -1)) + list(range(L + 1)))
    put("qmask", np.where(p < 64, NEG, 0.0)[:, None] * np.eye(TB).reshape(1, -1))
    put("kmask", (p >= 64)[:, None] * np.eye(TB).reshape(1, -1))
    put("eid", p[:, None])
    put("level", [1.0, 2.0, 3.0])
    put("thresh", [CAP * 1.0, CAP * 2.0, CAP * 3.0])
    put("eps", EPS)
    put("half_pi", np.pi / 2)
    g = np.arange(8)
    low8 = np.broadcast_to((g[None, :] < g[:, None]).reshape(1, 64), (P, 64)).astype(np.float32)
    return c, low8


def build(nc, A, out):
    place, n_const = constant_places()
    ctx = ExitStack()
    with ctx:
        def sb(name, shape, dt=F32):
            return ctx.enter_context(nc.sbuf_tensor(name, shape, dt))

        def sem(name):
            return ctx.enter_context(nc.semaphore(name))

        const = sb("const", [P, n_const])
        C = {k: const[:, a:b] for k, (a, b) in place.items()}
        ident = C["ident"]

        ring = sb("ring", [P, 2 * PAIR_W])
        keep = sb("keep", [P, KEEP])
        ps = ctx.enter_context(nc.psum_tensor("ps", [P, 8, 512], F32))

        def area(base, off, *shape, rows=P):
            n = int(np.prod(shape))
            v = base[0:rows, off:off + n]
            if len(shape) == 1:
                return v
            names = "abcd"[:len(shape)]
            return v.rearrange(f"p ({' '.join(names)}) -> p {' '.join(names)}",
                               **dict(zip(names[1:], shape[1:])))

        x = area(keep, 0, TB, D)
        lnr = area(keep, 2048, 2, D)
        xT = area(keep, 4096, DK, T)
        wb = area(keep, 6144, G, P)
        wc = area(keep, 10240, G, L + 1, CH)
        toep = area(keep, 14848, G, P)
        M = 18944
        qf = area(keep, M, TB, H, QKX)
        kf = area(keep, M + 1568, TB, H, QKX)
        vv = area(keep, M + 3136, TB, H * VD)
        u1 = area(keep, M + 4160, TB, SSM)
        ug = area(keep, M + 5184, G, NC)
        uc = area(keep, M, L, SSM, rows=NC)
        att = area(keep, M, TB, H * VD)
        yT = area(keep, M + 5184, 4, T)
        hc = area(keep, 2048, TB, CW)
        brow = area(keep, 2880, SSM, rows=1)
        bbar = area(keep, 3392, G, CH)
        cT = area(keep, 4096, 3, T)
        qT = xT
        mT = xT
        gate = area(keep, 4096 + 1024, TB, SSM)
        wsg = area(keep, 6144, 2, DK, FF)
        wsd = area(keep, 6144 + 4096, FK, D)
        wr = area(keep, 6144 + 6144, DK, E)
        xp = area(keep, 12800, TB, DK, P)
        xg = area(keep, 14848, 2, DK, P)
        hT = area(keep, 16896, 2, FF)
        hb = area(keep, 17408, 2, FF)
        sg = area(keep, 17920, 2, FF)
        pm = area(keep, 18432, 2, TB, 2, CAP)
        pg = area(keep, M, 2, TB, 2, CAP)
        ru = area(keep, 19456, TB, NUP)
        gu = area(keep, 19656, TB, NUP)
        rt = area(keep, 20000, 5, TB, E)
        cmp8 = area(keep, 20640, 2, TB, 64)
        ev = area(keep, 20900, 12, XU, rows=E)
        rte = area(keep, 21300, 2, T, rows=E)
        rbias = area(keep, 21812, E)
        low8 = area(keep, 21876, 64)
        wpre = area(ring, 0, G, L, CH)
        pt1 = area(ring, 0, H, 2, P)
        bt = area(ring, 0, G // 4, P)
        kT = area(ring, 2048, H, T)
        dterm = area(ring, 1024, G, CH, rows=CH)
        kall = area(ring, 4096, G, P, rows=CH)
        wtmp = area(ring, 4096, G, L, CH)
        yc = area(ring, 4096, L, G // 4, CH)
        lr = area(ring, 8192, G, NPW)
        li = area(ring, 8736, G, NPW)
        decay = area(ring, 8192, G, NC)
        cosc = area(ring, 9280, G, NC)
        sinc = area(ring, 10304, G, NC)
        par = area(ring, 11328, 24, G)
        drow = area(ring, 12096, G, rows=CH)
        wo = area(ring, 0, DK, D)
        R1 = PAIR_W
        w_in = area(ring, R1, DK, CW + SSM)
        wuq = area(ring, R1 + 7424, 2, H * QK)
        wukv = area(ring, R1 + 8960, H * (NOPE + VD))
        wglu = area(ring, R1 + 9984, 4, SSM)
        rp = area(ring, R1 + 12032, 8, TB, HALF)
        ucg = area(ring, R1, G, L, CH, rows=NC)
        sb_b = area(ring, R1, G, NC)
        sb_w = area(ring, R1 + 1024, G, NC)
        sb_z = area(ring, R1 + 2048, G, NC)
        sb_s = area(ring, R1 + 3072, G, NC + 1)
        prob = area(ring, R1 + 4128, 3072)
        pt0 = area(ring, R1 + 4128, H, P)
        rtmp = [area(ring, R1 + 6176 + 256 * k, TB, H, HALF) for k in range(4)]
        bs = area(keep, M, G, CH)
        jbb = area(keep, M + 1024, G, CH)
        ca = area(keep, M + 5184, G, CH)
        cb = area(keep, M + 5696, G, CH)
        ang = area(keep, M + 2560, G, NPW)
        ang2 = area(keep, M + 3104, G, NPW)
        mag = area(keep, M + 3648, G, NPW)
        nbb = area(keep, M + 4192, G, CH)
        whole = area(keep, 16896, G, NPW)
        cang = area(keep, 14848, G, NC)
        cang2 = area(keep, 14848 + 1024, G, NC)

        F32R = mybir.dt.float32r
        y_hi = sb("y_hi", [P, D], F32R)
        y_lo = sb("y_lo", [P, D], F32R)
        oneT = sb("oneT", [P, 2, T], F32R)
        gslot = sb("gslot", [P, 1])
        vec = sb("vec", [P, 15])
        posi = sb("posi", [P, TB], I32)
        st6 = sb("st6", [P, TB, 2, 6])
        stat = sb("stat", [P, 48])
        sm = sb("sm", [P, 4, TB, 8])
        ids = sb("ids", [1, XU], I32)
        cnt = sb("cnt", [1, 2], I32)
        ut = nc.dram_tensor("u_time", [T, SSM], F32).ap()
        yt = nc.dram_tensor("y_time", [T, SSM], F32).ap()

        names = """ld_const ld_x ld_ln ld_w_in ld_par ld_attn_w ld_glu ld_wo ld_shared ld_small st_u ld_u st_y ld_y
            st_out j_c j_b j_bbar cbar_done bbar_done bb_signed wc_done wpre_done
            ln_stat ln_rstd x_ready xT_ps xT_sb proj h_sb u_sb kall_ps kall_sb wbt_ps wbt_sb kall_d kall_dma
            toep_zero cn_sq cn_rstd cn_ready cT_ps cT_sb qkv_ps qkv_sb heads_ready hT_ps hT_sb sc_ps
            smax p_sb pT_ps pT_sb pv_ps att_sb ug_ps ug_sb b_ps b_sb nb_ps w_done z_done nz_ps s_done y_ps yg yc_ps
            yc_sb yT_ps yT_sb glu_ps glu_sig ssm_ready mix_sq mix_rstd mix_ready mT_ps mT_sb mix_ps x1_ready xp_ready chosen att_ready x1T_ps
            x1T_sb router_ps sig_sb mask_ready rank_ps rank_sb rt_ps rt_sb tab_ps tab2_ps tables
            ids_ready sh_down zeroed onehot gated gath xg_sb up silu h_ready tps
            tps_sb combined down_left y_hi0 y_hi1 y0 y1 final dve act pool tabs mags tt_ready rope_sin ucg_a ucg_b nbs_sb turns chunks bt_ps bt_sb j_read ld_route one_sb gate_sb over_ready attT_ps att_sq ssmT_ps ssm_sq"""
        S = {n: sem("s_" + n) for n in names.split()}
        up = [sem(f"s_up{b}") for b in range(2)]
        down = [sem(f"s_down{b}") for b in range(2)]
        wgu_in = [sem(f"s_wgu_in{b}") for b in range(2)]
        wd_in = [sem(f"s_wd_in{b}") for b in range(2)]

        wg, wu, wd = A["w_gate"], A["w_up"], A["w_down"]

        def unit_w(b, u):
            off = b * PAIR_W + u * PAIR_W // 2
            return area(ring, off, 2, DK, FF), area(ring, off + 2 * DK * FF, FK, D)

        block = ctx.enter_context(nc.Block())

        @block.sync
        def _(sp):
            sp.dma_start(const[:, :], A["const"]).then_inc(S["ld_const"], 16)
            sp.dma_start(x[:, 0, :], A["x"][0, 0:P, :]).then_inc(S["ld_x"], 16)
            sp.dma_start(x[:, 1, :], A["x"][0, P:T, :]).then_inc(S["ld_x"], 16)
            for n in range(2):
                sp.dma_start(lnr[:, n, :], A[("ln_in_g", "ln_in_b")[n]][:].partition_broadcast(P)
                             ).then_inc(S["ld_ln"], 16)
            for src, dst in (("lam", par[:, 0:3, :]), ("bstack", bs), ("cstack", ca)):
                sp.dma_start(dst, A[src]).then_inc(S["ld_par"], 16)
            sp.dma_start(w_in, A["w_in"][0].rearrange("(k p) n -> p k n", p=P)).then_inc(S["ld_w_in"], 16)
            for src, dst in (("vec", vec[:, :]), ("dskip", drow[:, :]),
                             ("pos", posi[:, :])):
                sp.dma_start(dst, A[src]).then_inc(S["ld_small"], 16)
            sp.dma_start(wuq, A["w_uq"][0].rearrange("(k p) h d -> p k (h d)", p=P)).then_inc(S["ld_attn_w"], 16)
            sp.dma_start(wukv, A["w_ukv"][0].rearrange("p h d -> p (h d)")).then_inc(S["ld_attn_w"], 16)
            sp.dma_start(wglu, A["w_glu"][0].rearrange("(k p) n -> p k n", p=P)).then_inc(S["ld_glu"], 16)
            sp.wait_ge(S["x_ready"], 2)
            sp.dma_start(brow, A["b_glu"]).then_inc(S["ld_glu"], 16)
            sp.wait_ge(S["u_sb"], 2)
            sp.dma_start(ut.rearrange("(b p) n -> p b n", p=P), u1).then_inc(S["st_u"], 16)
            sp.wait_ge(S["st_u"], 16)
            sp.wait_ge(S["wpre_done"], 1)
            sp.dma_start(uc, ut.rearrange("(c j) n -> c j n", j=L)).then_inc(S["ld_u"], 16)
            sp.wait_ge(S["kall_d"], 1)
            sp.wait_ge(S["toep_zero"], 1)
            for j in range(L):
                sp.dma_start(toep[CH * j:CH * (j + 1), :, CH * j:], kall[:, :, 0:P - CH * j]
                             ).then_inc(S["kall_dma"], 16)
            sp.wait_ge(S["yg"], 2)
            for q in range(4):
                sp.dma_start(yt.rearrange("(c i) (q n) -> q c i n", i=L, q=4)[q],
                             yc[NC * q:NC * (q + 1)].rearrange("c i r o -> c i (r o)")).then_inc(S["st_y"], 16)
            sp.wait_ge(S["st_y"], 64)
            sp.dma_start(u1, yt.rearrange("(b p) n -> p b n", p=P)).then_inc(S["ld_y"], 16)
            sp.wait_ge(S["pv_ps"], 2)
            sp.wait_ge(S["z_done"], 1)
            sp.dma_start(wo, A["w_o"][0].rearrange("(k p) n -> p k n", p=P)).then_inc(S["ld_wo"], 16)
            sp.wait_ge(S["hT_ps"], 2)
            sp.dma_start(rbias, A["router_bias"][0, :].partition_broadcast(P)).then_inc(S["ld_route"], 16)
            sp.dma_start(low8, A["low8"]).then_inc(S["ld_route"], 16)
            sp.wait_ge(S["y_ps"], 2)
            for n in range(2):
                sp.dma_start(wsg[:, n, :, :], A[("ws_gate", "ws_up")[n]][0].rearrange("(p k) f -> p k f", k=DK)
                             ).then_inc(S["ld_shared"], 16)
            sp.dma_start(wsd, A["ws_down"][0].rearrange("(p k) n -> p k n", k=FK)).then_inc(S["ld_shared"], 16)
            sp.dma_start(wr, A["w_router"][0].rearrange("(p k) n -> p k n", k=DK)).then_inc(S["ld_shared"], 16)

            def load_gate_up(b, experts):
                for u in range(2):
                    for n, w in enumerate((wg, wu)):
                        sp.dma_start(unit_w(b, u)[0][:, n, :, :],
                                     w[bass.ds(experts[u], 1)].rearrange("a (p k) f -> p (a k) f", k=DK)
                                     ).then_inc(wgu_in[b], 16)

            def load_down(b, experts):
                for u in range(2):
                    sp.dma_start(unit_w(b, u)[1],
                                 wd[bass.ds(experts[u], 1)].rearrange("a (p k) n -> p (a k) n", k=FK)
                                 ).then_inc(wd_in[b], 16)

            sp.wait_ge(S["glu_ps"], 2)
            sp.wait_ge(S["pT_ps"], 3)
            for n in range(2):
                sp.dma_start(lnr[:, n, :], A[("ln1_g", "ln1_b")[n]][0, :].partition_broadcast(P)
                             ).then_inc(S["ld_ln"], 16)
            load_gate_up(1, (2, 3))
            load_down(1, (2, 3))
            sp.wait_ge(S["mix_ps"], 2)
            load_gate_up(0, (0, 1))
            load_down(0, (0, 1))
            sp.wait_ge(S["x1_ready"], 2)
            for n in range(2):
                sp.dma_start(lnr[:, n, :], A[("ln2_g", "ln2_b")[n]][0, :].partition_broadcast(P)
                             ).then_inc(S["ld_ln"], 16)
            with sp.Fori(1, STEPS) as s:
                for b in range(2):
                    experts = [4 * s + 2 * b + u for u in range(2)]
                    sp.wait_ge(up[b], s + 1)
                    load_gate_up(b, experts)
                    sp.wait_ge(down[b], s)
                    load_down(b, experts)
            sp.wait_ge(S["over_ready"], 2)
            over = sp.value_load(cnt[0:1, 0:1], min_val=1, max_val=XU // 2)
            with sp.Fori(0, over) as j:
                experts = [sp.value_load(ids[0:1, bass.ds(2 * j + u, 1)], min_val=0, max_val=E - 1)
                           for u in range(2)]
                sp.wait_ge(up[0], j + STEPS + 1)
                load_gate_up(0, experts)
                sp.wait_ge(down[0], j + STEPS)
                load_down(0, experts)
            for b in range(TB):
                sp.wait_ge(S["final"], b + 1)
                sp.dma_start(out[0, b * P:(b + 1) * P, :], x[:, b, :]).then_inc(S["st_out"], 16)
            sp.wait_ge(S["st_out"], 16 * TB)

        def unit_cols(t, i):
            return t[:, :, bass.ds(2 * i, 2)].unsqueeze(3).to_broadcast([P, TB, 2, CAP])

        slots = C["iota"].unsqueeze(1).unsqueeze(1).to_broadcast([P, TB, 2, CAP])

        @block.gpsimd
        def _(pool):
            n = [0]

            def step(ins):
                n[0] += 1
                ins.then_inc(S["pool"], 1)
                pool.wait_ge(S["pool"], n[0])

            def bc(t, rows, k):
                return t[:, :, rows].unsqueeze(3).to_broadcast([P, G, k, CH])

            def each(t, k):
                return t.unsqueeze(2).to_broadcast([P, G, k, CH])

            pool.wait_ge(S["cbar_done"], 1)
            pool.wait_ge(S["tabs"], 1)
            step(nc.gpsimd.tensor_copy(wc[:, :, 0, :], ca))
            step(nc.gpsimd.tensor_tensor(wc[:, :, 1:, :], bc(lr, slice(L + 1, NPW), L), each(ca, L), ALU.mult))
            step(nc.gpsimd.tensor_tensor(wtmp, bc(li, slice(L + 1, NPW), L), each(cb, L), ALU.mult))
            nc.gpsimd.tensor_tensor(wc[:, :, 1:, :], wc[:, :, 1:, :], wtmp, ALU.add).then_inc(S["wc_done"], 1)
            pool.wait_ge(S["wpre_done"], 1)
            pool.wait_ge(S["chunks"], 1)
            nc.gpsimd.memset(toep, 0.0).then_inc(S["toep_zero"], 1)
            nc.gpsimd.memset(y_hi[:, :].bitcast(F32), 0.0).then_inc(S["y0"], 1)
            nc.gpsimd.memset(y_lo[:, :].bitcast(F32), 0.0).then_inc(S["y1"], 1)
            nc.gpsimd.memset(oneT[:, 1, :].bitcast(F32), 0.0).then_inc(S["zeroed"], 1)

            def gated(i, b, transposed):
                pool.wait_ge(S["onehot"], i + 1)
                pool.wait_ge(S["tps"], transposed)
                nc.gpsimd.tensor_tensor(pg[:, b], pm[:, b], unit_cols(gu, i), ALU.mult).then_inc(S["gated"], 1)

            with pool.Fori(0, STEPS) as s:
                for b in range(2):
                    i = 2 * s + b
                    gated(i, b, SH + i - 1)
            pool.wait_ge(S["over_ready"], 2)
            over = pool.value_load(cnt[0:1, 0:1], min_val=1, max_val=XU // 2)
            with pool.Fori(0, over) as j:
                i = j + 2 * STEPS
                gated(i, 0, i + SH)

        @block.scalar
        def _(act):
            n = [0]

            def step(ins):
                n[0] += 1
                ins.then_inc(S["act"], 1)
                act.wait_ge(S["act"], n[0])

            def f(out_, in_, func, **k):
                return nc.scalar.activation(out_, in_, func, **k)

            act.wait_ge(S["ld_const"], 16)
            for b in range(TB):
                act.wait_ge(S["ln_stat"], b + 1)
                f(stat[:, 4 + b:5 + b], stat[:, 2 * b + 1:2 * b + 2], ACT.Sqrt, bias=C["eps"]).then_inc(S["ln_rstd"], 1)
            act.wait_ge(S["ld_par"], 48)
            f(par[:, 3, :], par[:, 2, :], ACT.Exp).then_inc(S["mags"], 1)
            act.wait_ge(S["j_b"], 1)
            f(nbb.rearrange("p g c -> p (g c)"), ps[:, 5, :], ACT.Copy).then_inc(S["nbs_sb"], 1)
            act.wait_ge(S["j_c"], 1)
            f(cb.rearrange("p g c -> p (g c)"), ps[:, 4, :], ACT.Copy).then_inc(S["cbar_done"], 1)
            for b in range(TB):
                for q in range(2):
                    act.wait_ge(S["xT_ps"], 2 * b + q + 1)
                    f(xT[:, 4 * q:4 * q + 4, b * P:(b + 1) * P],
                      ps[:, 2 * b + q, :].rearrange("p (k t) -> p k t", k=4), ACT.Copy).then_inc(S["xT_sb"], 1)
            act.wait_ge(S["tt_ready"], 1)
            step(f(par[:, 6, :], par[:, 4, :], ACT.Exp))
            step(f(mag, ang2, ACT.Exp))
            step(f(par[:, 8, :], par[:, 5, :], ACT.Sin))
            f(par[:, 9, :], par[:, 7, :], ACT.Sin, bias=C["half_pi"]).then_inc(S["mags"], 1)
            act.wait_ge(S["turns"], 1)
            step(f(li, ang, ACT.Sin, scale=SIN_SCALE))
            step(f(ang2, ang, ACT.Abs))
            f(lr, ang2, ACT.Sin, scale=-SIN_SCALE, bias=C["half_pi"]).then_inc(S["mags"], 1)
            act.wait_ge(S["turns"], 2)
            step(f(rp[:, 1], rp[:, 0], ACT.Sin))
            step(f(rp[:, 2], rp[:, 0], ACT.Abs))
            f(rp[:, 3], rp[:, 2], ACT.Sin, scale=-1.0, bias=C["half_pi"]).then_inc(S["rope_sin"], 1)
            act.wait_ge(S["proj"], 4)
            act.wait_ge(S["mags"], 3)
            act.wait_ge(S["tabs"], 1)
            for b in range(TB):
                f(hc[:, b, :], ps[:, 4 + 2 * b, 0:CW], ACT.Copy).then_inc(S["h_sb"], 1)
                f(u1[:, b, :], ps[:, 5 + 2 * b, :], ACT.Copy).then_inc(S["u_sb"], 1)
            act.wait_ge(S["xT_sb"], 4)
            for b in range(TB):
                act.wait_ge(S["h_sb"], b + 1)
                step(f(ps[:, 1, 0:QR], hc[:, b, 0:QR], ACT.Square, scale=QR ** -0.5,
                       accum_out=stat[:, 8 + 2 * b:9 + 2 * b]))
                step(f(ps[:, 1, 0:KVR], hc[:, b, QR:QR + KVR], ACT.Square, scale=KVR ** -0.5,
                       accum_out=stat[:, 9 + 2 * b:10 + 2 * b]))
            f(stat[:, 12:16], stat[:, 8:12], ACT.Sqrt, bias=C["eps"]).then_inc(S["cn_sq"], 1)
            act.wait_ge(S["cT_ps"], 1)
            act.wait_ge(S["ld_small"], 48)
            for k in range(3):
                f(cT[:, k, :], ps[:, 4 + k, 0:T], ACT.Copy, scale=vec[:, k:k + 1]).then_inc(S["cT_sb"], 1)
            for r in range(8):
                act.wait_ge(S["wbt_ps"], r + 1)
                f(wb[:, 4 * r:4 * r + 4, :], ps[:, r % 4, :].rearrange("p (g n) -> p g n", g=4),
                  ACT.Copy).then_inc(S["wbt_sb"], 1)
            act.wait_ge(S["ld_u"], 16)
            uv = uc.rearrange("p j (g c) -> p g j c", g=G)
            f(ucg[:, 0:G // 2], uv[:, 0:G // 2], ACT.Copy).then_inc(S["ucg_a"], 1)
            def qkv_out(b):
                if b == 0:
                    act.wait_ge(S["ucg_a"], 1)
                    act.wait_ge(S["ucg_b"], 1)
                act.wait_ge(S["qkv_ps"], 2 * b + 1)
                f(qf[:, b, :, 0:QK].rearrange("p (a h) d -> p a h d", a=2),
                  ps[:, 4:6, 0:4 * QK].rearrange("p a (h d) -> p a h d", h=4), ACT.Copy).then_inc(S["qkv_sb"], 1)
                act.wait_ge(S["qkv_ps"], 2 * b + 2)
                kv = ps[:, 6:8, :].rearrange("p a (h d) -> p (a h) d", h=4)
                f(kf[:, b, :, 0:NOPE], kv[:, :, 0:NOPE], ACT.Copy).then_inc(S["qkv_sb"], 1)
                f(vv[:, b, :].rearrange("p (h d) -> p h d", h=H), kv[:, :, NOPE:], ACT.Copy).then_inc(S["qkv_sb"], 1)

            qkv_out(0)
            act.wait_ge(S["wc_done"], 1)
            for r in range(2):
                act.wait_ge(S["ug_ps"], r + 1)
                f(ug[:, 16 * r:16 * r + 16, :], ps[:, r, :].rearrange("p (g c) -> p g c", g=16),
                  ACT.Copy).then_inc(S["ug_sb"], 1)
            act.wait_ge(S["turns"], 3)
            step(f(sinc, cang, ACT.Sin, scale=SIN_SCALE))
            step(f(cang2, cang, ACT.Abs))
            f(cosc, cang2, ACT.Sin, scale=-SIN_SCALE, bias=C["half_pi"]).then_inc(S["chunks"], 1)
            qkv_out(1)
            for r in range(2):
                act.wait_ge(S["bt_ps"], r + 1)
                f(bt[:, 4 * r:4 * r + 4, :], ps[:, 2 + r, :].rearrange("p (r n) -> p r n", r=4),
                  ACT.Copy).then_inc(S["bt_sb"], 1)
            for r in range(2):
                act.wait_ge(S["b_ps"], r + 1)
                f(sb_b.rearrange("p (q r) c -> p r q c", q=4)[:, 4 * r:4 * r + 4],
                  ps[:, r, :].rearrange("p (r q c) -> p r q c", r=4, q=4), ACT.Copy).then_inc(S["b_sb"], 1)
            def kall_out(r):
                act.wait_ge(S["kall_ps"], r + 1)
                f(kall[:, 8 * r:8 * r + 8, :], ps[0:CH, 2:4, :].rearrange("p a (g n) -> p (a g) n", g=4),
                  ACT.Copy).then_inc(S["kall_sb"], 1)

            kall_out(0)
            kall_out(1)
            for t in range(2):
                dst = (qT, kT)[t]
                act.wait_ge(S["hT_ps"], t + 1)
                f(dst[0:QKX, :, :], ps[0:QKX, 4:8, :].rearrange("p a (h t) -> p (a h) t", h=2),
                  ACT.Copy).then_inc(S["hT_sb"], 1)
                kall_out(2 + t)
            def exps(r):
                act.wait_ge(S["smax"], r + 1)
                if r == 0:
                    w, heads, off = P, range(8), 0
                else:
                    w, heads, off = T, range(4 * (r - 1), 4 * r), 1024 + 1024 * (r - 1)
                bank = (4, 6, 4)[r]
                for m, h in enumerate(heads):
                    col = 16 + 8 * min(r, 1) + h
                    src = ps[:, bank:bank + 2, :].rearrange("p a n -> p (a n)")[:, m * w:(m + 1) * w]
                    last = f(prob[:, off + m * w:off + (m + 1) * w], src, ACT.Exp, scale=SCALE,
                             bias=stat[:, col:col + 1], accum_out=stat[:, col + 16:col + 17])
                    if m < len(heads) - 1:
                        last.then_inc(S["act"], 1)
                        n[0] += 1
                last.then_inc(S["p_sb"], 1)
                act.wait_ge(S["act"], n[0])

            for r in range(3):
                exps(r)
            for r in range(2):
                act.wait_ge(S["y_ps"], r + 1)
                f(yc[:, :, 4 * r:4 * r + 4, :], ps[:, r, :].rearrange("p (r i o) -> p i r o", r=4, i=L),
                  ACT.Gelu_apprx_tanh).then_inc(S["yg"], 1)
            act.wait_ge(S["yT_ps"], 1)
            f(yT, ps[:, 0:2, :].rearrange("p a (k t) -> p (a k) t", k=2), ACT.Copy).then_inc(S["yT_sb"], 1)
            for b in range(TB):
                act.wait_ge(S["att_sb"], b + 1)
                act.wait_ge(S["pT_sb"], 3)
                step(f(ps[:, 7, :], att[:, b, :], ACT.Square, scale=SSM ** -0.5, accum_out=stat[:, 8 + b:9 + b]))
            f(stat[:, 12:14], stat[:, 8:10], ACT.Sqrt, bias=C["eps"]).then_inc(S["att_sq"], 1)
            for b in range(TB):
                act.wait_ge(S["glu_ps"], b + 1)
                f(gate[:, b, :], ps[:, 2 + b, :], ACT.Sigmoid).then_inc(S["glu_sig"], 1)
            for k in range(4):
                act.wait_ge(S["attT_ps"], k // 2 + 1)
                f(mT[:, k, :], ps[:, 6 + k // 2, (k % 2) * T:(k % 2 + 1) * T], ACT.Copy,
                  scale=vec[:, 3 + k:4 + k]).then_inc(S["mT_sb"], 1)
            act.wait_ge(S["glu_sig"], 2)
            for b in range(TB):
                act.wait_ge(S["ssm_ready"], b + 1)
                step(f(ps[:, 2 + b, :], u1[:, b, :], ACT.Square, scale=SSM ** -0.5, accum_out=stat[:, 10 + b:11 + b]))
            f(stat[:, 14:16], stat[:, 10:12], ACT.Sqrt, bias=C["eps"]).then_inc(S["ssm_sq"], 1)
            for k in range(4, 8):
                act.wait_ge(S["ssmT_ps"], k // 2 - 1)
                f(mT[:, k, :], ps[:, k // 2 - 2, (k % 2) * T:(k % 2 + 1) * T], ACT.Copy,
                  scale=vec[:, 3 + k:4 + k]).then_inc(S["mT_sb"], 1)
            for b in range(TB):
                act.wait_ge(S["ln_stat"], 3 + b)
                f(stat[:, 4 + b:5 + b], stat[:, 2 * b + 1:2 * b + 2], ACT.Sqrt, bias=C["eps"]).then_inc(S["ln_rstd"], 1)
            for b in range(TB):
                for q in range(2):
                    act.wait_ge(S["x1T_ps"], 2 * b + q + 1)
                    f(xT[:, 4 * q:4 * q + 4, b * P:(b + 1) * P],
                      ps[:, 2 * b + q, :].rearrange("p (k t) -> p k t", k=4), ACT.Copy).then_inc(S["x1T_sb"], 1)
            act.wait_ge(S["router_ps"], 1)
            f(rt[:, 0, :, :], ps[:, 5, 0:TB * E].rearrange("p (b e) -> p b e", b=TB), ACT.Sigmoid
              ).then_inc(S["sig_sb"], 1)
            for b in range(TB):
                act.wait_ge(up[b], 1)
                f(sg[:, b], ps[:, SHARED_BANK[b], 0:FF], ACT.Silu).then_inc(S["silu"], 1)

            def evac_gather(b, i):
                for q in range(2):
                    act.wait_ge(S["gath"], 2 * i + q + 1)
                    f(xg[:, b, 4 * q:4 * q + 4, :], ps[:, 4 + q, :].rearrange("p (k s) -> p k s", k=4),
                      ACT.Copy).then_inc(S["xg_sb"], 1)

            def pair(i, b, nb, use, sg_read):
                act.wait_ge(up[b], use + 1)
                act.wait_ge(S["h_ready"], sg_read)
                f(sg[:, b], ps[:, 6, 0:FF], ACT.Silu).then_inc(S["silu"], 1)
                evac_gather(nb, i + 1)
                act.wait_ge(S["gate_sb"], i + 1)
                for c in range(2):
                    act.wait_ge(S["down_left"], i + 1) if c == 0 else act.wait_ge(down[b], use)
                    f(y_hi[:, c * 512:(c + 1) * 512], ps[:, 6 + c, :], ACT.Copy, scale=gslot[:, 0:1]
                      ).then_inc(S[f"y_hi{c}"], 1)

            evac_gather(0, 0)
            with act.Fori(0, STEPS) as s:
                for b in range(2):
                    i = 2 * s + b
                    pair(i, b, 1 - b, s + 1, SH + i - 1)
            act.wait_ge(S["over_ready"], 2)
            over = act.value_load(cnt[0:1, 0:1], min_val=1, max_val=XU // 2)
            with act.Fori(0, over) as j:
                i = j + 2 * STEPS
                pair(i, 0, 0, j + STEPS + 1, i + SH)
            for b in range(TB):
                act.wait_ge(S["ln_stat"], 5 + b)
                f(stat[:, 4 + b:5 + b], stat[:, 2 * b + 1:2 * b + 2], ACT.Sqrt, bias=C["eps"]).then_inc(S["ln_rstd"], 1)

        @block.vector
        def _(dve):
            n = [0]

            def step(ins):
                n[0] += 1
                ins.then_inc(S["dve"], 1)
                dve.wait_ge(S["dve"], n[0])

            def ts(o, i, a, b, op0, op1=ALU.bypass):
                if b is None:
                    return nc.vector.tensor_scalar(o, i, a, None, op0)
                return nc.vector.tensor_scalar(o, i, a, b, op0, op1)

            def tt2(o, a, b, op):
                return nc.vector.tensor_tensor(o, a, b, op)

            def layer_norm(b, k, ready):
                for q in range(2):
                    step(nc.vector.bn_stats(st6[:, b, q, :], x[:, b, 512 * q:512 * q + 512]))
                nc.vector.bn_aggr(stat[:, 2 * b:2 * b + 2], st6[:, b, :, :]).then_inc(S["ln_stat"], 1)

            def layer_norm_end(b, k, ready):
                dve.wait_ge(S["ln_rstd"], k + 1)
                step(nc.vector.reciprocal(stat[:, 6 + b:7 + b], stat[:, 4 + b:5 + b]))
                step(ts(x[:, b, :], x[:, b, :], stat[:, 2 * b:2 * b + 1], stat[:, 6 + b:7 + b], ALU.subtract, ALU.mult))
                step(tt2(x[:, b, :], x[:, b, :], lnr[:, 0, :], ALU.mult))
                tt2(x[:, b, :], x[:, b, :], lnr[:, 1, :], ALU.add).then_inc(ready, 1)

            dve.wait_ge(S["ld_x"], 32)
            for b in range(TB):
                layer_norm(b, b, S["x_ready"])
            dve.wait_ge(S["ld_par"], 48)
            ts(ca[ST:P], ca[ST:P], -1.0, None, ALU.mult).then_inc(S["bb_signed"], 1)
            dve.wait_ge(S["ld_ln"], 32)
            for b in range(TB):
                layer_norm_end(b, b, S["x_ready"])

            pr = lambda k: par[:, k, :]
            dve.wait_ge(S["ld_par"], 48)
            dve.wait_ge(S["mags"], 1)
            step(ts(pr(0), pr(0), -1e-4, None, ALU.min))
            step(tt2(pr(4), pr(0), pr(3), ALU.mult))
            step(tt2(pr(10), pr(1), pr(3), ALU.mult))
            step(ts(pr(11), pr(10), 1.0 / TWO_PI, ROUND, ALU.mult, ALU.add))
            step(ts(pr(11), pr(11), ROUND, None, ALU.subtract))
            for c in (PI_1, PI_2, PI_3):
                step(nc.vector.scalar_tensor_tensor(pr(10), pr(11), -c, pr(10), ALU.mult, ALU.add))
            step(ts(pr(5), pr(10), 3.1415925, -3.1415925, ALU.min, ALU.max))
            step(nc.vector.scalar_tensor_tensor(pr(7), pr(5), -1.0, pr(5), ALU.mult, ALU.min))
            powers = C["powers"].unsqueeze(1).to_broadcast([P, G, NPW])
            tt2(ang2, pr(4).unsqueeze(2).to_broadcast([P, G, NPW]), powers, ALU.mult).then_inc(S["tt_ready"], 1)
            dve.wait_ge(S["mags"], 2)
            re, im = pr(0), pr(1)
            step(tt2(pr(16), pr(6), pr(9), ALU.mult))
            step(ts(pr(16), pr(16), -1.0, None, ALU.add))
            step(tt2(pr(17), pr(6), pr(8), ALU.mult))
            step(tt2(pr(18), re, re, ALU.mult))
            step(tt2(pr(19), im, im, ALU.mult))
            step(tt2(pr(18), pr(18), pr(19), ALU.add))
            step(nc.vector.reciprocal(pr(18), pr(18)))
            step(tt2(pr(19), pr(16), re, ALU.mult))
            step(tt2(pr(20), pr(17), im, ALU.mult))
            step(tt2(pr(19), pr(19), pr(20), ALU.add))
            step(tt2(pr(19), pr(19), pr(18), ALU.mult))
            step(tt2(pr(20), pr(17), re, ALU.mult))
            step(tt2(pr(21), pr(16), im, ALU.mult))
            step(tt2(pr(20), pr(20), pr(21), ALU.subtract))
            step(tt2(pr(20), pr(20), pr(18), ALU.mult))
            dve.wait_ge(S["nbs_sb"], 1)
            col = lambda k: pr(k).unsqueeze(2).to_broadcast([P, G, CH])
            step(tt2(bbar, col(19), bs, ALU.mult))
            step(tt2(jbb, col(20), nbb, ALU.mult))
            tt2(bbar, bbar, jbb, ALU.subtract).then_inc(S["bbar_done"], 1)
            dve.wait_ge(S["bbar_done"], 1)
            step(ts(pr(12), pr(10), 1.0 / TWO_PI, None, ALU.mult))
            step(tt2(ang, pr(12).unsqueeze(2).to_broadcast([P, G, NPW]), powers, ALU.mult))
            step(ts(whole, ang, ROUND, ROUND, ALU.add, ALU.subtract))
            tt2(ang, ang, whole, ALU.subtract).then_inc(S["turns"], 1)
            dve.wait_ge(S["ld_small"], 48)
            step(nc.vector.tensor_copy(stat[:, 46:48], posi[:, :]))
            for b in range(TB):
                step(ts(rp[:, 4, b, :], C["invf"], stat[:, 46 + b:47 + b], None, ALU.mult))
            step(ts(rp[:, 5], rp[:, 4], 1.0 / TWO_PI, ROUND, ALU.mult, ALU.add))
            step(ts(rp[:, 5], rp[:, 5], ROUND, None, ALU.subtract))
            for c in (PI_1, PI_2, PI_3):
                step(nc.vector.scalar_tensor_tensor(rp[:, 4], rp[:, 5], -c, rp[:, 4], ALU.mult, ALU.add))
            ts(rp[:, 0], rp[:, 4], 3.1415925, -3.1415925, ALU.min, ALU.max).then_inc(S["turns"], 1)
            dve.wait_ge(S["mags"], 3)
            step(nc.vector.tensor_copy(pr(22), mag[:, :, NPW - 1]))
            step(tt2(lr, lr, mag, ALU.mult))
            tt2(li, li, mag, ALU.mult).then_inc(S["tabs"], 1)
            dve.wait_ge(S["tabs"], 1)
            dve.wait_ge(S["j_bbar"], 1)
            nc.vector.tensor_copy(jbb, ps[:, 0, :].rearrange("p (g c) -> p g c", g=G)).then_inc(S["j_read"], 1)
            dve.wait_ge(S["j_read"], 1)
            pb = lambda t: t[:, :, 0:L].unsqueeze(3).to_broadcast([P, G, L, CH])
            step(tt2(wpre, pb(lr), bbar.unsqueeze(2).to_broadcast([P, G, L, CH]), ALU.mult))
            t4 = toep.rearrange("p g (j c) -> p g j c", j=L)
            step(tt2(t4, pb(li), jbb.unsqueeze(2).to_broadcast([P, G, L, CH]), ALU.mult))
            dve.wait_ge(S["cn_sq"], 1)
            step(nc.vector.reciprocal(stat[:, 12:16], stat[:, 12:16]))
            for b in range(TB):
                step(ts(hc[:, b, 0:QR], hc[:, b, 0:QR], stat[:, 12 + 2 * b:13 + 2 * b], None, ALU.mult))
                ts(hc[:, b, QR:QR + KVR], hc[:, b, QR:QR + KVR], stat[:, 13 + 2 * b:14 + 2 * b], None,
                   ALU.mult).then_inc(S["cn_ready"], 1)
            tt2(wpre, wpre, t4, ALU.subtract).then_inc(S["wpre_done"], 1)
            dve.wait_ge(S["wpre_done"], 1)
            step(ts(pr(13), pr(12), float(L), None, ALU.mult))
            step(ts(pr(14), pr(13), ROUND, ROUND, ALU.add, ALU.subtract))
            step(tt2(pr(13), pr(13), pr(14), ALU.subtract))
            step(ts(pr(14), pr(13), 4096.0, ROUND, ALU.mult, ALU.add))
            step(ts(pr(14), pr(14), ROUND, 1.0 / 4096.0, ALU.subtract, ALU.mult))
            step(tt2(pr(15), pr(13), pr(14), ALU.subtract))
            chunks = C["iota"][:, 0:NC].unsqueeze(1).to_broadcast([P, G, NC])
            wide = lambda k: pr(k).unsqueeze(2).to_broadcast([P, G, NC])
            step(tt2(cang, wide(14), chunks, ALU.mult))
            dve.wait_ge(S["ld_u"], 16)
            uv = uc.rearrange("p j (g c) -> p g j c", g=G)
            nc.vector.tensor_copy(ucg[:, G // 2:], uv[:, G // 2:]).then_inc(S["ucg_b"], 1)
            step(ts(cang2, cang, ROUND, ROUND, ALU.add, ALU.subtract))
            step(tt2(cang, cang, cang2, ALU.subtract))
            step(tt2(cang2, wide(15), chunks, ALU.mult))
            step(tt2(cang, cang, cang2, ALU.add))
            step(ts(cang2, cang, ROUND, ROUND, ALU.add, ALU.subtract))
            tt2(cang, cang, cang2, ALU.subtract).then_inc(S["turns"], 1)
            dve.wait_ge(S["wc_done"], 1)
            step(nc.vector.tensor_copy(decay, pr(22).unsqueeze(2).to_broadcast([P, G, NC])))
            step(nc.vector.memset(decay[:, :, 0:1], 0.0))
            dve.wait_ge(S["wbt_ps"], 8)
            step(tt2(dterm, ident[0:CH, 0:CH].unsqueeze(1).to_broadcast([CH, G, CH]),
                     drow[:, :].unsqueeze(2).to_broadcast([CH, G, CH]), ALU.mult))

            dve.wait_ge(S["rope_sin"], 1)
            def rotate(x1, x2, shape, c, s, t):
                step(tt2(t[0], x1, s, ALU.mult))
                step(tt2(t[1], x2, s, ALU.mult))
                step(tt2(t[2], x2, c, ALU.mult))
                step(tt2(t[3], x1, c, ALU.mult))
                step(tt2(x1, t[3], t[1], ALU.subtract))
                step(tt2(x2, t[2], t[0], ALU.add))

            rotate(hc[:, :, QR + KVR:QR + KVR + HALF], hc[:, :, QR + KVR + HALF:CW], None, rp[:, 3], rp[:, 1],
                   [rp[:, k] for k in (4, 5, 6, 7)])
            dve.wait_ge(S["qkv_sb"], 6)
            tmp = [area(ring, R1 + 7200 - 4 * 256 + 256 * k, TB, H, HALF) for k in range(4)]
            spread = lambda t: t.unsqueeze(2).to_broadcast([P, TB, H, HALF])
            rotate(qf[:, :, :, NOPE:NOPE + HALF], qf[:, :, :, NOPE + HALF:QK], None, spread(rp[:, 3]), spread(rp[:, 1]), tmp)
            for b in range(TB):
                step(nc.vector.tensor_copy(kf[:, b, :, NOPE:QK],
                                           hc[:, b, QR + KVR:CW].unsqueeze(1).to_broadcast([P, H, ROPE])))
            for t, m in ((qf, "qmask"), (kf, "kmask")):
                last = nc.vector.tensor_copy(t[:, :, :, QK:QKX], C[m].rearrange("p (b m) -> p b m", b=TB)
                                             .unsqueeze(2).to_broadcast([P, TB, H, TB]))
                if t is qf:
                    step(last)
            last.then_inc(S["heads_ready"], 1)

            dve.wait_ge(S["nb_ps"], 2)
            dve.wait_ge(S["b_sb"], 2)
            dve.wait_ge(S["chunks"], 1)
            flat = lambda t: t.rearrange("p g c -> p (g c)")
            two = ps[:, 0:2, :].rearrange("p a n -> p (a n)")
            step(tt2(flat(sb_w), flat(sinc), two, ALU.mult))
            step(tt2(sb_z, cosc, sb_b, ALU.mult))
            step(tt2(sb_w, sb_w, sb_z, ALU.add))
            nc.vector.tensor_tensor_scan(flat(sb_z), flat(decay), flat(sb_w), 0.0, ALU.mult, ALU.add).then_inc(S["z_done"], 1)
            dve.wait_ge(S["z_done"], 1)
            dve.wait_ge(S["kall_sb"], 4)
            tt2(kall[:, :, 0:CH], kall[:, :, 0:CH], dterm, ALU.add).then_inc(S["kall_d"], 1)
            dve.wait_ge(S["nz_ps"], 2)
            two = ps[:, 2:4, :].rearrange("p a n -> p (a n)")
            step(tt2(flat(sb_w), flat(sinc), two, ALU.mult))
            step(tt2(sb_b, cosc, sb_z, ALU.mult))
            step(nc.vector.memset(sb_s[:, :, 0:1], 0.0))
            tt2(sb_s[:, :, 1:], sb_b, sb_w, ALU.subtract).then_inc(S["s_done"], 1)

            for r in range(3):
                dve.wait_ge(S["sc_ps"], r + 1)
                w, m, c = ((P, 8, 16), (T, 4, 24), (T, 4, 28))[r]
                bank = (4, 6, 4)[r]
                src = ps[:, bank:bank + 2, :].rearrange("p a n -> p (a n)").rearrange("p (h k) -> p h k", h=m)
                step(nc.vector.tensor_reduce(stat[:, c:c + m], src, AX.X, ALU.max))
                ts(stat[:, c:c + m], stat[:, c:c + m], -SCALE, None, ALU.mult).then_inc(S["smax"], 1)
            dve.wait_ge(S["pT_ps"], 1)
            nc.vector.tensor_copy(pt0.rearrange("p h q -> p (h q)"), ps[:, 6:8, :].rearrange("p a n -> p (a n)")).then_inc(S["pT_sb"], 1)
            for r in range(2):
                dve.wait_ge(S["pT_ps"], 2 + r)
                bank = (4, 6)[r]
                nc.vector.tensor_copy(pt1[:, 4 * r:4 * r + 4].rearrange("p h k q -> p (h k q)"),
                                      ps[:, bank:bank + 2, :].rearrange("p a n -> p (a n)")).then_inc(S["pT_sb"], 1)
            step(nc.vector.reciprocal(stat[:, 32:48], stat[:, 32:48]))
            for b in range(TB):
                dve.wait_ge(S["pv_ps"], b + 1)
                tt2(att[:, b, :].rearrange("p (h d) -> p h d", h=H), ps[:, 4 + b, :].rearrange("p (h d) -> p h d", h=H),
                    stat[:, 32 + 8 * b:40 + 8 * b].unsqueeze(2).to_broadcast([P, H, VD]), ALU.mult).then_inc(S["att_sb"], 1)
            dve.wait_ge(S["att_sq"], 1)
            step(nc.vector.reciprocal(stat[:, 12:14], stat[:, 12:14]))
            for b in range(TB):
                ts(att[:, b, :], att[:, b, :], stat[:, 12 + b:13 + b], None, ALU.mult).then_inc(S["att_ready"], 1)
            dve.wait_ge(S["ld_y"], 16)
            for b in range(TB):
                dve.wait_ge(S["glu_sig"], b + 1)
                tt2(u1[:, b, :], u1[:, b, :], gate[:, b, :], ALU.mult).then_inc(S["ssm_ready"], 1)
            dve.wait_ge(S["ssm_sq"], 1)
            step(nc.vector.reciprocal(stat[:, 14:16], stat[:, 14:16]))
            for b in range(TB):
                ts(u1[:, b, :], u1[:, b, :], stat[:, 14 + b:15 + b], None, ALU.mult).then_inc(S["mix_ready"], 1)
            for b in range(TB):
                dve.wait_ge(S["mix_ps"], b + 1)
                step(nc.vector.scalar_tensor_tensor(x[:, b, :], x[:, b, :], ALPHA,
                                                    ps[:, 4 + 2 * b:6 + 2 * b, :].rearrange("p a n -> p (a n)"),
                                                    ALU.mult, ALU.add))
                layer_norm(b, 2 + b, None)
                dve.wait_ge(S["ld_ln"], 64)
                layer_norm_end(b, 2 + b, S["x1_ready"])
                dve.wait_ge(S["x1_ready"], b + 1)
                nc.vector.tensor_copy(xp[:, b].rearrange("p k q -> p q k"),
                                      x[:, b, :].rearrange("p (q k) -> p q k", k=DK)).then_inc(S["xp_ready"], 1)

            r_ = lambda k: rt[:, k, :, :]
            grouped = lambda k: r_(k).rearrange("p b (g k) -> p b g k", g=8)
            gs, gn, kept, shut = [sm[:, k] for k in range(4)]
            step(nc.vector.memset(ru[:, :, NU:], FAR))
            step(nc.vector.memset(gu[:, :, NU:], 0.0))
            dve.wait_ge(S["sig_sb"], 1)
            dve.wait_ge(S["ld_route"], 32)
            step(tt2(r_(1), r_(0), rbias.unsqueeze(1).to_broadcast([P, TB, E]), ALU.add))
            for b in range(TB):
                for g in range(8):
                    last = nc.vector.max(rt[:, 2, b, 8 * g:8 * g + 8], rt[:, 1, b, 8 * g:8 * g + 8])
                    last.then_inc(S["dve"], 1)
                    n[0] += 1
            dve.wait_ge(S["dve"], n[0])
            step(tt2(gs, grouped(2)[:, :, :, 0], grouped(2)[:, :, :, 1], ALU.add))
            mine = gs.unsqueeze(3).to_broadcast([P, TB, 8, 8])
            other = gs.unsqueeze(2).to_broadcast([P, TB, 8, 8])
            c4 = lambda k: cmp8[:, k].rearrange("p b (a c) -> p b a c", a=8)
            step(tt2(c4(0), other, mine, ALU.is_gt))
            step(tt2(c4(1), other, mine, ALU.is_equal))
            step(tt2(cmp8[:, 1], cmp8[:, 1], low8.unsqueeze(1).to_broadcast([P, TB, 64]), ALU.mult))
            step(tt2(cmp8[:, 0], cmp8[:, 0], cmp8[:, 1], ALU.add))
            step(nc.vector.tensor_reduce(gn, c4(0), AX.X, ALU.add))
            step(ts(kept, gn, 4.0, None, ALU.is_lt))
            step(ts(shut, kept, -NEG, NEG, ALU.mult, ALU.add))
            spread8 = lambda t: t.unsqueeze(3).to_broadcast([P, TB, 8, 8])
            step(tt2(grouped(1), grouped(1), spread8(kept), ALU.mult))
            step(tt2(grouped(1), grouped(1), spread8(shut), ALU.add))
            for b in range(TB):
                step(nc.vector.max(gs[:, b, :], rt[:, 1, b, :]))
                step(nc.vector.match_replace(rt[:, 2, b, :], gs[:, b, :], rt[:, 1, b, :], 3 * NEG))
            ts(r_(3), r_(2), 2 * NEG, None, ALU.is_lt).then_inc(S["chosen"], 1)
            dve.wait_ge(S["chosen"], 1)
            step(tt2(r_(4), r_(0), r_(3), ALU.mult))
            step(nc.vector.tensor_reduce(gn[:, :, 0], r_(4), AX.X, ALU.add))
            step(nc.vector.reciprocal(gn[:, :, 1], gn[:, :, 0]))
            for b in range(TB):
                step(ts(gu[:, b, 0:E], rt[:, 4, b, :], gn[:, b, 1:2], 2.5, ALU.mult, ALU.mult))
            def hidden(b, bank):
                tt2(hb[:, b], sg[:, b], ps[:, bank, FF:2 * FF], ALU.mult).then_inc(S["h_ready"], 1)

            def shared_hidden(b):
                dve.wait_ge(S["silu"], b + 1)
                hidden(b, SHARED_BANK[b])

            def shared_transposed(b):
                dve.wait_ge(S["tps"], b + 1)
                nc.vector.tensor_copy(hT[:, b], ps[:, 7, 0:FF]).then_inc(S["tps_sb"], 1)

            def one_hot(i, b):
                tt2(pm[:, b], slots, unit_cols(ru, i), ALU.is_equal).then_inc(S["onehot"], 1)

            step(ts(r_(2), r_(3), -FAR, FAR, ALU.mult, ALU.add))
            dve.wait_ge(S["rank_ps"], 1)
            tt2(ru[:, :, 0:E], r_(2), ps[:, 5, 0:TB * E].rearrange("p (b e) -> p b e", b=TB), ALU.add).then_inc(S["rank_sb"], 1)
            ex = lambda k, w=XU: ev[:, k, 0:w]
            step(tt2(ex(0, 3), ps[0:E, 5, 128:129].to_broadcast([E, 3]), C["thresh"][0:E], ALU.is_gt))
            nc.vector.tensor_reduce(ex(1, 1), ex(0, 3), AX.X, ALU.add).then_inc(S["tables"], 1)
            dve.wait_ge(S["rank_sb"], 1)
            one_hot(0, 0)
            shared_hidden(0)
            shared_hidden(1)
            shared_transposed(0)
            dve.wait_ge(S["rt_ps"], 1)
            step(nc.vector.tensor_copy(rte[:, :, :], ps[0:E, 6, :].rearrange("p (a t) -> p a t", a=2)))
            dve.wait_ge(S["tab_ps"], 1)
            step(tt2(ex(2, 3), C["level"][0:E], ps[0:E, 5, 130:131].to_broadcast([E, 3]), ALU.add))
            step(tt2(ex(2, 3), ex(2, 3), ex(0, 3), ALU.mult))
            step(ts(ex(2, 3), ex(2, 3), -1.0, None, ALU.add))
            for l in range(3):
                step(ts(ex(3 + l), C["iota"][0:E, 0:XU], ev[:, 2, l:l + 1], None, ALU.is_equal))
            step(tt2(ex(6), ex(3), ex(4), ALU.add))
            step(tt2(ex(6), ex(6), ex(5), ALU.add))
            step(ts(ex(7), ex(6), -FAR, None, ALU.mult))
            for l in range(2):
                step(nc.vector.scalar_tensor_tensor(ex(7), ex(3 + l), -float(CAP * (l + 1)), ex(7), ALU.mult, ALU.add))
            nc.vector.scalar_tensor_tensor(ex(7), ex(5), -3.0 * CAP, ex(7), ALU.mult, ALU.add).then_inc(S["rt_sb"], 1)
            shared_transposed(1)
            dve.wait_ge(S["tab2_ps"], 1)
            step(ts(ru[:, :, E:NU], ps[:, 5, 192:192 + TB * XU].rearrange("p (b j) -> p b j", b=TB), FAR, None, ALU.add))
            step(nc.vector.tensor_copy(gu[:, :, E:NU], ps[:, 5, 256:256 + TB * XU].rearrange("p (b j) -> p b j", b=TB)))
            nc.vector.tensor_copy(ids[:, :], ps[0:1, 5, 320:320 + XU]).then_inc(S["over_ready"], 1)
            step(ts(ev[0:1, 9, 0:1], ps[0:1, 5, 352:353], 0.5, 0.25, ALU.mult, ALU.add))
            step(ts(ev[0:1, 9, 0:1], ev[0:1, 9, 0:1], ROUND, ROUND, ALU.add, ALU.subtract))
            step(ts(ev[0:1, 9, 0:1], ev[0:1, 9, 0:1], 1.0, None, ALU.max))
            nc.vector.tensor_copy(cnt[:, 0:1], ev[0:1, 9, 0:1]).then_inc(S["over_ready"], 1)

            def pair(i, b, nb, hb_read):
                dve.wait_ge(S["gath"], 2 * (i + 1))
                dve.wait_ge(S["gated"], i + 1)
                one_hot(i + 1, nb)
                dve.wait_ge(S["silu"], SH + i + 1)
                dve.wait_ge(S["tps"], hb_read)
                hidden(b, 6)
                dve.wait_ge(S["tps"], SH + i + 1)
                nc.vector.tensor_copy(hT[:, b], ps[:, 7, 0:FF]).then_inc(S["tps_sb"], 1)
                turned = b if nb != b else 1
                if nb == b:
                    dve.wait_ge(S["combined"], i + 1)
                ts(oneT[:, turned], ps[:, 7, FF:], 0.0, None, ALU.is_gt).then_inc(S["one_sb"], 1)
                nc.vector.tensor_reduce(gslot[:, :], ps[:, 7, FF:], AX.X, ALU.add).then_inc(S["gate_sb"], 1)
                dve.wait_ge(S["gate_sb"], i + 1)
                for c in range(2):
                    half = slice(c * 512, (c + 1) * 512)
                    dve.wait_ge(S[f"y_hi{c}"], i + 1)
                    nc.vector.scalar_tensor_tensor(y_lo[:, half], ps[:, 6 + c, :], gslot[:, 0:1],
                                                   y_hi[:, half].bitcast(F32), ALU.mult, ALU.subtract
                                                   ).then_inc(S[f"y{c}"], 1)

            with dve.Fori(0, STEPS) as s:
                for b in range(2):
                    i = 2 * s + b
                    pair(i, b, 1 - b, SH + i - 1)
            over = dve.value_load(cnt[0:1, 0:1], min_val=1, max_val=XU // 2)
            with dve.Fori(0, over) as j:
                i = j + 2 * STEPS
                pair(i, 0, 0, i + SH)
            for b in range(TB):
                dve.wait_ge(S["combined"], over + 2 * STEPS + 1 + b)
                step(nc.vector.scalar_tensor_tensor(x[:, b, :], x[:, b, :], ALPHA,
                                                    ps[:, 2 * b:2 * b + 2, :].rearrange("p a n -> p (a n)"),
                                                    ALU.mult, ALU.add))
                layer_norm(b, 4 + b, None)
                dve.wait_ge(S["ld_ln"], 96)
                layer_norm_end(b, 4 + b, S["final"])

        @block.tensor
        def _(pe):
            def mm(o, l, r, start=True, stop=True, **k):
                return nc.tensor.matmul(o, l, r, start=start, stop=stop, **k)

            fl = lambda t: t.rearrange("p g c -> p (g c)")
            nj = C["nj"]
            pe.wait_ge(S["ld_const"], 16)
            pe.wait_ge(S["ld_par"], 48)
            pe.wait_ge(S["bb_signed"], 1)
            mm(ps[:, 5, :], nj, fl(bs)).then_inc(S["j_b"], 1)
            mm(ps[:, 4, :], nj, fl(ca)).then_inc(S["j_c"], 1)
            for b in range(TB):
                pe.wait_ge(S["x_ready"], b + 1)
                for q in range(2):
                    for k in range(4):
                        c = (4 * q + k) * P
                        last = nc.tensor.transpose(ps[:, 2 * b + q, k * P:(k + 1) * P], x[:, b, c:c + P], ident)
                    last.then_inc(S["xT_ps"], 1)
            pe.wait_ge(S["xT_sb"], 4)
            pe.wait_ge(S["ld_w_in"], 16)
            pe.wait_ge(S["cbar_done"], 1)
            pe.wait_ge(S["nbs_sb"], 1)
            for b in range(TB):
                if b:
                    pe.wait_ge(S["bbar_done"], 1)
                    mm(ps[:, 0, :], nj, fl(bbar)).then_inc(S["j_bbar"], 1)
                for k in range(DK):
                    l = xT[:, k, b * P:(b + 1) * P]
                    m0 = mm(ps[:, 4 + 2 * b, 0:CW], l, w_in[:, k, 0:CW], start=(k == 0), stop=(k == DK - 1))
                    m1 = mm(ps[:, 5 + 2 * b, :], l, w_in[:, k, CW:], start=(k == 0), stop=(k == DK - 1))
                m0.then_inc(S["proj"], 1)
                m1.then_inc(S["proj"], 1)
            pe.wait_ge(S["cn_ready"], 2)
            pe.wait_ge(S["u_sb"], 2)
            pe.wait_ge(S["h_sb"], 2)
            for k in range(3):
                for b in range(TB):
                    last = nc.tensor.transpose(ps[:, 4 + k, b * P:(b + 1) * P], hc[:, b, k * P:(k + 1) * P], ident)
            last.then_inc(S["cT_ps"], 1)
            pe.wait_ge(S["cT_sb"], 3)
            pe.wait_ge(S["ld_attn_w"], 32)

            def qkv(b):
                if b:
                    pe.wait_ge(S["qkv_sb"], 3)
                for a in range(2):
                    for k in range(2):
                        last = mm(ps[:, 4 + a, 0:4 * QK], cT[:, k, :][:, b * P:(b + 1) * P],
                                  wuq[:, k, a * 4 * QK:(a + 1) * 4 * QK], start=(k == 0), stop=(k == 1))
                last.then_inc(S["qkv_ps"], 1)
                for a in range(2):
                    last = mm(ps[:, 6 + a, :], cT[:, 2, :][:, b * P:(b + 1) * P], wukv[:, a * 512:(a + 1) * 512])
                last.then_inc(S["qkv_ps"], 1)

            qkv(0)
            pe.wait_ge(S["wpre_done"], 1)
            pe.wait_ge(S["j_read"], 1)
            for r in range(8):
                if r >= 4:
                    pe.wait_ge(S["wbt_sb"], r - 3)
                for g in range(4):
                    last = nc.tensor.transpose(ps[:, r % 4, g * P:(g + 1) * P],
                                               wpre[:, 4 * r + g, :, :].rearrange("p j c -> p (j c)"), ident)
                last.then_inc(S["wbt_ps"], 1)
            pe.wait_ge(S["ucg_a"], 1)
            pe.wait_ge(S["ucg_b"], 1)
            pe.wait_ge(S["wbt_sb"], 8)
            for r in range(2):
                for g in range(16):
                    last = nc.tensor.transpose(ps[:, r, g * NC:(g + 1) * NC],
                                               ucg[:, 16 * r + g].rearrange("p j c -> p (j c)"), ident[0:NC, 0:NC])
                last.then_inc(S["ug_ps"], 1)
            qkv(1)
            pe.wait_ge(S["ug_sb"], 2)
            for r in range(G // 4):
                for q in range(4):
                    g = q * (G // 4) + r
                    last = mm(ps[NC * q:NC * (q + 1), 2 + r // 4, (r % 4) * P:(r % 4 + 1) * P], ug[:, g, :], wb[:, g, :])
                if r % 4 == 3:
                    last.then_inc(S["bt_ps"], 1)
            for r in range(G // 4):
                pe.wait_ge(S["bt_sb"], r // 4 + 1)
                last = nc.tensor.transpose(ps[:, r // 4, (r % 4) * P:(r % 4 + 1) * P], bt[:, r, :], ident)
                if r % 4 == 3:
                    last.then_inc(S["b_ps"], 1)

            def kall_taps(r):
                pe.wait_ge(S["kall_sb"], r) if r else pe.wait_ge(S["wc_done"], 1)
                for g in range(8):
                    last = mm(ps[0:CH, 2 + g // 4, (g % 4) * P:(g % 4 + 1) * P], bbar[:, 8 * r + g, :],
                              wc[:, 8 * r + g, 0:L, :].rearrange("p i c -> p (i c)"))
                last.then_inc(S["kall_ps"], 1)

            kall_taps(0)
            pe.wait_ge(S["b_sb"], 2)
            for r in range(2):
                mm(ps[:, r, :], nj, sb_b[:, 16 * r:16 * r + 16, :].rearrange("p g c -> p (g c)")).then_inc(S["nb_ps"], 1)
            kall_taps(1)
            pe.wait_ge(S["heads_ready"], 1)
            pe.wait_ge(S["qkv_sb"], 6)
            for t in range(2):
                if t:
                    pe.wait_ge(S["hT_sb"], 1)
                for h in range(H):
                    for b in range(TB):
                        c = (h % 2) * T + b * P
                        last = nc.tensor.transpose(ps[0:QKX, 4 + h // 2, c:c + P], (qf, kf)[t][:, b, h, :], ident)
                last.then_inc(S["hT_ps"], 1)
                kall_taps(2 + t)
            pe.wait_ge(S["z_done"], 1)
            pe.wait_ge(S["kall_sb"], 4)
            for r in range(2):
                mm(ps[:, 2 + r, :], nj, sb_z[:, 16 * r:16 * r + 16, :].rearrange("p g c -> p (g c)")).then_inc(S["nz_ps"], 1)
            pe.wait_ge(S["hT_sb"], 2)

            def scores(r):
                heads = range(8) if r == 0 else range(4 * (r - 1), 4 * r)
                bank = (4, 6, 4)[r]
                w = P if r == 0 else T
                flat = ps[:, bank:bank + 2, :].rearrange("p a n -> p (a n)")
                for m, h in enumerate(heads):
                    q0 = 0 if r == 0 else P
                    last = mm(flat[:, m * w:(m + 1) * w], qT[0:QKX, h, q0:q0 + P], kT[0:QKX, h, 0:w])
                last.then_inc(S["sc_ps"], 1)

            scores(0)
            scores(1)
            pe.wait_ge(S["p_sb"], 1)
            scores(2)
            pe.wait_ge(S["s_done"], 1)
            pe.wait_ge(S["kall_dma"], 16 * L)
            for r in range(G // 4):
                spot = [ps[NC * q:NC * (q + 1), r // 4, (r % 4) * P:(r % 4 + 1) * P] for q in range(4)]
                for q in range(4):
                    mm(spot[q], ug[:, q * (G // 4) + r, :], toep[:, q * (G // 4) + r, :], stop=False)
                for q in range(4):
                    g = q * (G // 4) + r
                    last = mm(spot[q], sb_s[:, g, 0:NC], wc[:, g, 1:, :].rearrange("p i c -> p (i c)"), start=False)
                if r % 4 == 3:
                    last.then_inc(S["y_ps"], 1)
            pe.wait_ge(S["p_sb"], 2)
            for h in range(H):
                last = nc.tensor.transpose(ps[:, 6 + h // 4, (h % 4) * P:(h % 4 + 1) * P], prob[:, h * P:(h + 1) * P], ident)
            last.then_inc(S["pT_ps"], 1)
            pe.wait_ge(S["p_sb"], 3)
            for r in range(2):
                if r:
                    pe.wait_ge(S["pT_sb"], 1)
                for m in range(4):
                    for k in range(2):
                        c = 1024 + (4 * r + m) * T + k * P
                        j = 2 * m + k
                        last = nc.tensor.transpose(ps[:, (4, 6)[r] + j // 4, (j % 4) * P:(j % 4 + 1) * P],
                                                   prob[:, c:c + P], ident)
                last.then_inc(S["pT_ps"], 1)
            pe.wait_ge(S["pT_sb"], 3)
            for b in range(TB):
                for h in range(H):
                    for k in range(b + 1):
                        l = pt0[:, h, :] if b == 0 else pt1[:, h, k, :]
                        last = mm(ps[:, 4 + b, h * VD:(h + 1) * VD], l, vv[:, k, h * VD:(h + 1) * VD],
                                  start=(k == 0), stop=(k == b))
                last.then_inc(S["pv_ps"], 1)
            pe.wait_ge(S["ld_y"], 16)
            pe.wait_ge(S["yg"], 2)
            for k in range(4):
                for b in range(TB):
                    c = (k % 2) * T + b * P
                    last = nc.tensor.transpose(ps[:, k // 2, c:c + P], u1[:, b, k * P:(k + 1) * P], ident)
            last.then_inc(S["yT_ps"], 1)
            pe.wait_ge(S["yT_sb"], 1)
            pe.wait_ge(S["ld_glu"], 32)
            for b in range(TB):
                mm(ps[:, 2 + b, :], C["ones"][0:1, :], brow[0:1, :], stop=False)
                for k in range(4):
                    last = mm(ps[:, 2 + b, :], yT[:, k, b * P:(b + 1) * P], wglu[:, k, :], start=False, stop=(k == 3))
                last.then_inc(S["glu_ps"], 1)
            pe.wait_ge(S["att_ready"], 2)
            for q in range(2):
                for k in range(2 * q, 2 * q + 2):
                    for b in range(TB):
                        c = (k % 2) * T + b * P
                        last = nc.tensor.transpose(ps[:, 6 + q, c:c + P], att[:, b, k * P:(k + 1) * P], ident)
                last.then_inc(S["attT_ps"], 1)

            def project(half):
                pe.wait_ge(S["mT_sb"], 4 * half + 4)
                for b in range(TB):
                    for k in range(4 * half, 4 * half + 4):
                        for c in range(2):
                            last = mm(ps[:, 4 + 2 * b + c, :], mT[:, k, b * P:(b + 1) * P], wo[:, k, c * 512:(c + 1) * 512],
                                      start=(k == 0), stop=(k == 7))
                    if half:
                        last.then_inc(S["mix_ps"], 1)

            pe.wait_ge(S["ld_wo"], 16)
            project(0)
            pe.wait_ge(S["mix_ready"], 2)
            for q in range(2):
                for k in range(2 * q, 2 * q + 2):
                    for b in range(TB):
                        c = (k % 2) * T + b * P
                        last = nc.tensor.transpose(ps[:, q, c:c + P], u1[:, b, k * P:(k + 1) * P], ident)
                last.then_inc(S["ssmT_ps"], 1)
            project(1)
            for b in range(TB):
                pe.wait_ge(S["xp_ready"], b + 1)
                for q in range(2):
                    for k in range(4):
                        last = nc.tensor.transpose(ps[:, 2 * b + q, k * P:(k + 1) * P], xp[:, b, 4 * q + k, :], ident)
                    last.then_inc(S["x1T_ps"], 1)
            pe.wait_ge(S["x1T_sb"], 4)
            pe.wait_ge(S["ld_shared"], 64)
            pe.wait_ge(S["x1_ready"], 2)
            for b in range(TB):
                for k in range(DK):
                    last = mm(ps[:, 5, b * E:(b + 1) * E], xT[:, k, b * P:(b + 1) * P], wr[:, k, :],
                              start=(k == 0), stop=(k == DK - 1))
            last.then_inc(S["router_ps"], 1)

            def shared_up(b):
                for k in range(DK):
                    last = mm(ps[:, SHARED_BANK[b], :], xT[:, k, b * P:(b + 1) * P], wsg[:, :, k, :],
                              start=(k == 0), stop=(k == DK - 1))
                last.then_inc(up[b], 1)

            def shared_turn(b):
                pe.wait_ge(S["h_ready"], b + 1)
                if b:
                    pe.wait_ge(S["tps_sb"], b)
                for k in range(FK):
                    last = nc.tensor.transpose(ps[:, 7, k * P:(k + 1) * P], hb[:, b, k:FF:FK], ident)
                last.then_inc(S["tps"], 1)

            def shared_down(b):
                pe.wait_ge(S["tps_sb"], b + 1)
                for c in range(2):
                    for k in range(FK):
                        mm(ps[:, 2 * b + c, :], hT[:, b, k * P:(k + 1) * P], wsd[:, k, c * 512:(c + 1) * 512],
                           start=(k == 0), stop=False, skip_group_check=True)

            shared_up(0)
            shared_up(1)
            pe.wait_ge(S["chosen"], 1)
            ch = rt[:, 3, :, :]
            mm(ps[:, 5, 0:E], C["tri"], ch[:, 0, :])
            mm(ps[:, 5, E:2 * E], C["ones"], ch[:, 0, :], stop=False)
            mm(ps[:, 5, E:2 * E], C["tri"], ch[:, 1, :], start=False)
            mm(ps[0:E, 5, 128:129], ch[:, 0, :], C["ones"][:, 0:1], stop=False)
            mm(ps[0:E, 5, 128:129], ch[:, 1, :], C["ones"][:, 0:1], start=False).then_inc(S["rank_ps"], 1)
            shared_turn(0)
            pe.wait_ge(S["tables"], 1)
            mm(ps[0:E, 5, 130:131], C["tri"][0:E, 0:E], ev[:, 1, 0:1])
            mm(ps[0:1, 5, 352:353], C["ones"][0:E, 0:1], ev[:, 1, 0:1]).then_inc(S["tab_ps"], 1)
            pe.wait_ge(S["rank_sb"], 1)
            for k, t in enumerate((ru, gu)):
                for b in range(TB):
                    last = mm(ps[0:E, 6, k * T + b * P:k * T + (b + 1) * P], t[:, b, 0:E], ident)
            last.then_inc(S["rt_ps"], 1)
            shared_down(0)
            shared_turn(1)
            pe.wait_ge(S["rt_sb"], 1)
            for b in range(TB):
                o = ps[:, 5, 192 + b * XU:192 + (b + 1) * XU]
                mm(o, rte[:, 0, b * P:(b + 1) * P], ev[:, 6, :], stop=False)
                mm(o, C["ones"][0:E, :], ev[:, 7, :], start=False)
                mm(ps[:, 5, 256 + b * XU:256 + (b + 1) * XU], rte[:, 1, b * P:(b + 1) * P], ev[:, 6, :])
            mm(ps[0:1, 5, 320:320 + XU], C["eid"][0:E, :], ev[:, 6, :]).then_inc(S["tab2_ps"], 1)
            shared_down(1)

            def gather(b):
                for q in range(2):
                    for k in range(4):
                        for t in range(TB):
                            last = mm(ps[:, 4 + q, k * P:(k + 1) * P], xp[:, t, 4 * q + k, :],
                                      pm[:, b, t].rearrange("p u s -> p (u s)"), start=(t == 0), stop=(t == TB - 1))
                    last.then_inc(S["gath"], 1)

            def combine(b, t):
                for c in range(2):
                    for y in (y_hi, y_lo):
                        last = mm(ps[:, 2 * t + c, :], oneT[:, b, t * P:(t + 1) * P], y[:, c * 512:(c + 1) * 512],
                                  start=False, stop=False, skip_group_check=True)
                return last

            def pair(i, b, nb, use):
                pe.wait_ge(wgu_in[b], 64 * use)
                pe.wait_ge(S["xg_sb"], 2 * (i + 1))
                pe.wait_ge(S["y0"], i + 1)
                for k in range(DK):
                    for u in range(2):
                        last = mm(ps[CAP * u:CAP * (u + 1), 6, :], xg[:, b, k, CAP * u:CAP * (u + 1)],
                                  unit_w(b, u)[0][:, :, k, :], start=(k == 0), stop=(k == DK - 1))
                last.then_inc(up[b], 1)
                pe.wait_ge(S["onehot"], i + 2)
                gather(nb)
                pe.wait_ge(S["h_ready"], SH + i + 1)
                pe.wait_ge(S["gated"], i + 1)
                pe.wait_ge(S["y1"], i + 1)
                for k in range(FK):
                    nc.tensor.transpose(ps[:, 7, k * P:(k + 1) * P], hb[:, b, k:FF:FK], ident)
                for t in range(TB):
                    last = nc.tensor.transpose(ps[:, 7, FF + t * P:FF + (t + 1) * P],
                                               pg[:, b, t].rearrange("p u s -> p (u s)"), ident)
                last.then_inc(S["tps"], 1)
                combine(nb if nb != b else 1, 0)
                combine(nb if nb != b else 1, 1).then_inc(S["combined"], 1)
                pe.wait_ge(S["tps_sb"], SH + i + 1)
                pe.wait_ge(wd_in[b], 32 * use)
                pe.wait_ge(S["one_sb"], i + 1)
                pe.wait_ge(S["gate_sb"], i + 1)
                for c in range(2):
                    for k in range(FK):
                        for u in range(2):
                            last = mm(ps[CAP * u:CAP * (u + 1), 6 + c, :],
                                      hT[:, b, k * P + CAP * u:k * P + CAP * (u + 1)],
                                      unit_w(b, u)[1][:, k, c * 512:(c + 1) * 512],
                                      start=(k == 0), stop=(k == FK - 1))
                    last.then_inc(S["down_left"] if c == 0 else down[b], 1)

            pe.wait_ge(S["onehot"], 1)
            pe.wait_ge(S["over_ready"], 2)
            gather(0)
            pe.wait_ge(S["zeroed"], 1)
            with pe.Fori(0, STEPS) as s:
                for b in range(2):
                    pair(2 * s + b, b, 1 - b, s + 1)
            over = pe.value_load(cnt[0:1, 0:1], min_val=1, max_val=XU // 2)
            with pe.Fori(0, over) as j:
                pair(j + 2 * STEPS, 0, 0, j + STEPS + 1)
            pe.wait_ge(S["y0"], over + 2 * STEPS + 1)
            pe.wait_ge(S["y1"], over + 2 * STEPS + 1)
            for t in range(TB):
                combine(1, t).then_inc(S["combined"], 1)


def kernel(**inputs):
    import concourse.bacc as bacc
    from concourse.bass_utils import run_bass_kernel_spmd

    a = {k: np.asarray(v) for k, v in inputs.items()}

    def states(re, im):
        return np.ascontiguousarray(np.concatenate([re.transpose(1, 0, 2), im.transpose(1, 0, 2)]))

    def twice(t):
        return np.concatenate([t.T, t.T])

    const, low8 = constants()
    arrays = {"const": const, "low8": low8}
    for name in ("x", "ln_in_g", "ln_in_b", "w_in", "w_uq", "w_ukv", "w_glu", "b_glu", "w_o", "ln1_g", "ln1_b",
                 "w_router", "router_bias", "ws_gate", "ws_up", "ws_down", "ln2_g", "ln2_b"):
        arrays[name] = np.ascontiguousarray(a[name])
    for name in ("w_gate", "w_up", "w_down"):
        arrays[name] = np.ascontiguousarray(a[name][0])
    step = np.broadcast_to(a["log_step"][0][None, :], (P, G))
    arrays["lam"] = np.ascontiguousarray(np.stack([twice(a["lambda_re"][0]), twice(a["lambda_im"][0]), step], 1))
    arrays["bstack"] = states(a["b_re"][0], a["b_im"][0])
    arrays["cstack"] = states(a["c_re"][0].transpose(0, 2, 1), a["c_im"][0].transpose(0, 2, 1))
    rows = [a["q_norm_g"][0], a["kv_norm_g"][0], a["attn_out_g"][0], a["ssm_out_g"][0]]
    vec = np.concatenate([r.reshape(-1, P) for r in rows])
    arrays["vec"] = np.ascontiguousarray(np.concatenate([vec, vec[:4]]).T)
    arrays["dskip"] = np.ascontiguousarray(a["d_skip"][0].T)
    arrays["pos"] = np.ascontiguousarray(a["positions"].reshape(TB, P).T)

    nc = bacc.Bacc("TRN2", target_bir_lowering=False, num_devices=1)
    A, sent = {}, {}
    for name, v in arrays.items():
        sent[f"in_{name}"] = v
        A[name] = nc.dram_tensor(f"in_{name}", v.shape, mybir.dt.from_np(v.dtype), kind="ExternalInput").ap()
    out = nc.dram_tensor("out_x", (1, T, D), F32, kind="ExternalOutput").ap()
    build(nc, A, out)
    r = run_bass_kernel_spmd(nc, [sent], core_ids=[0])
    return r.results[0]["out_x"]
```

```python
from contextlib import ExitStack

import numpy as np

import concourse.bass as bass
from concourse import mybir

F32 = mybir.dt.float32
I32 = mybir.dt.int32
F32R = mybir.dt.float32r
ALU = mybir.AluOpType
ACT = mybir.ActivationFunctionType
AX = mybir.AxisListType

P = 128
T = 256
TB = T // P
D = 1024
DK = D // P
QR, KVR, ROPE, SSM = 256, 128, 32, 512
CW = QR + KVR + ROPE
H, NOPE, VD = 8, 64, 64
QK = NOPE + ROPE
QKX = QK + TB
HALF = ROPE // 2
G, CH, ST = 32, 16, 64
L = 8
NC = T // L
NPW = 2 * L + 1
E, FF = 64, 256
FK = FF // P
CAP = 64
XU = T * 8 // CAP
NU = E + XU
NUP = NU + 2
STEPS = E // 4
GP = 4
GROUPS = E // (2 * GP)
MIDDLE = 2
KEEP, HEADS = 18944, 6208
PAIR_W = 2 * 3 * DK * FF
ALPHA = 2.0 ** 0.25
EPS = 1e-5
SCALE = float(QK) ** -0.5
ROUND = 12582912.0
NEG = -1e30
FAR = 1000.0
TWO_PI = 2 * np.pi
SIN_SCALE = 6.283185
PI_1 = 6.28125
PI_2 = float(np.floor((TWO_PI - PI_1) * 2.0 ** 21) / 2.0 ** 21)
PI_3 = float(TWO_PI - PI_1 - PI_2)

CONST_COLS = dict(ident=P, nj=P, tri=P, ones=P, iota=CAP, invf=HALF, powers=NPW,
                  qmask=4, kmask=4, eid=1, level=3, thresh=3,
                  eps=1, half_pi=1)


def constant_places():
    at, out = 0, {}
    for name, n in CONST_COLS.items():
        out[name] = (at, at + n)
        at += n
    return out, at


def constants():
    place, n = constant_places()
    c = np.zeros((P, n), np.float32)

    def put(name, value):
        a, b = place[name]
        c[:, a:b] = value

    p = np.arange(P)
    put("ident", np.eye(P))
    nj = np.zeros((P, P))
    nj[p[:ST] + ST, p[:ST]] = 1.0
    nj[p[:ST], p[:ST] + ST] = -1.0
    put("nj", nj)
    put("tri", p[:, None] < p[None, :])
    put("ones", 1.0)
    put("iota", np.arange(CAP))
    put("invf", np.float32(10000.0) ** (-np.arange(HALF, dtype=np.float32) / np.float32(HALF)))
    put("powers", list(range(L - 1, -1, -1)) + list(range(L + 1)))
    put("qmask", np.where(p < 64, NEG, 0.0)[:, None] * np.eye(TB).reshape(1, -1))
    put("kmask", (p >= 64)[:, None] * np.eye(TB).reshape(1, -1))
    put("eid", p[:, None])
    put("level", [1.0, 2.0, 3.0])
    put("thresh", [CAP * 1.0, CAP * 2.0, CAP * 3.0])
    put("eps", EPS)
    put("half_pi", np.pi / 2)
    g = np.arange(8)
    low8 = np.broadcast_to((g[None, :] < g[:, None]).reshape(1, 64), (P, 64)).astype(np.float32)
    return c, low8


def build(nc, A, out):
    place, n_const = constant_places()
    ctx = ExitStack()
    with ctx:
        def sb(name, shape, dt=F32):
            return ctx.enter_context(nc.sbuf_tensor(name, shape, dt))

        def sem(name):
            return ctx.enter_context(nc.semaphore(name))

        const = sb("const", [P, n_const])
        C = {k: const[:, a:b] for k, (a, b) in place.items()}
        ident = C["ident"]

        ring = sb("ring", [P, 2 * PAIR_W])
        keep = sb("keep", [P, KEEP])
        with nc.sbuf_tensor("heads", [P, HEADS + 2 * D], F32) as first:
            heads = first[:, :]
        split = sb("split", [P, HEADS + 2 * D], F32R)
        ps = ctx.enter_context(nc.psum_tensor("ps", [P, 8, 512], F32))

        def area(base, off, *shape, rows=P):
            n = int(np.prod(shape))
            v = base[0:rows, off:off + n]
            if len(shape) == 1:
                return v
            names = "abcd"[:len(shape)]
            return v.rearrange(f"p ({' '.join(names)}) -> p {' '.join(names)}",
                               **dict(zip(names[1:], shape[1:])))

        x = area(keep, 0, TB, D)
        lnr = area(keep, 2048, 2, D)
        xT = area(keep, 4096, DK, T)
        wb = area(keep, 6144, G, P)
        wc = area(keep, 10240, G, L + 1, CH)
        toep = area(keep, 14848, G, P)
        qf = area(heads, 0, TB, H, QKX)
        kf = area(heads, 1568, TB, H, QKX)
        vv = area(heads, 3136, TB, H * VD)
        u1 = area(heads, 4160, TB, SSM)
        ug = area(heads, 5184, G, NC)
        uc = area(heads, 0, L, SSM, rows=NC)
        att = area(heads, 0, TB, H * VD)
        yT = area(heads, 5184, 4, T)
        hc = area(keep, 2048, TB, CW)
        brow = area(keep, 2880, SSM)
        bbar = area(keep, 3392, G, CH)
        cT = area(keep, 4096, 3, T)
        qT = xT
        mT = xT
        gate = area(keep, 4096 + 1024, TB, SSM)
        wsg = area(keep, 6144, 2, DK, FF)
        wsd = area(keep, 6144 + 4096, FK, D)
        wr = area(keep, 6144 + 6144, DK, E)
        ru = area(keep, 12288, TB, NUP)
        gu = area(keep, 12288 + TB * NUP, TB, NUP)
        xg = [[area(keep, 12800 + GP * P * k, GP, P) for k in range(DK)],
              [area(keep, GP * P * k, GP, P) for k in range(4)]
              + [area(keep, 2048 + TB * FF + GP * P * k, GP, P) for k in range(3)] + [xT[:, 0:GP, 0:P]]]
        hT = area(keep, 16896, 2, FF)
        hb = area(keep, 17408, 2, FF)
        sg = area(keep, 17920, 2, FF)
        hs = area(keep, 2048, TB, FF)
        rbias = area(keep, 17920, E)
        low8 = area(keep, 17920 + E, 64)
        pg = area(keep, 18432, 2, TB, 2, CAP)
        x_hi = area(split, 0, TB, DK, P)
        x_lo = area(split, 2048, TB, DK, P)
        pm = area(split, 4096, 2, TB, 2 * GP, CAP)
        rt = area(heads, 4096 + 1024, 5, TB, E)
        cmp8 = area(heads, 4096 + 1024 + 640, 2, TB, 64)
        wpre = area(ring, 0, G, L, CH)
        pt1 = area(ring, 0, H, 2, P)
        bt = area(ring, 0, G // 4, P)
        kT = area(ring, 2048, H, T)
        dterm = area(ring, 1024, G, CH, rows=CH)
        kall = area(ring, 4096, G, P, rows=CH)
        wtmp = area(ring, 4096, G, L, CH)
        yc = area(ring, 4096, L, G // 4, CH)
        lr = area(ring, 8192, G, NPW)
        li = area(ring, 8736, G, NPW)
        decay = area(ring, 8192, G, NC)
        cosc = area(ring, 9280, G, NC)
        sinc = area(ring, 10304, G, NC)
        par = area(ring, 11328, 24, G)
        drow = area(ring, 12096, G, rows=CH)
        wo = area(ring, 0, DK, D)
        R1 = PAIR_W
        w_in = area(ring, R1, DK, CW + SSM)
        wuq = area(ring, R1 + 7424, 2, H * QK)
        wukv = area(ring, R1 + 8960, H * (NOPE + VD))
        wglu = area(ring, R1 + 9984, 4, SSM)
        rp = area(ring, R1 + 12032, 8, TB, HALF)
        ucg = area(ring, R1, G, L, CH, rows=NC)
        sb_b = area(ring, R1, G, NC)
        sb_w = area(ring, R1 + 1024, G, NC)
        sb_z = area(ring, R1 + 2048, G, NC)
        sb_s = area(ring, R1 + 3072, G, NC + 1)
        prob = area(ring, R1 + 4128, 3072)
        pt0 = area(ring, R1 + 4128, H, P)
        rtmp = [area(ring, R1 + 6176 + 256 * k, TB, H, HALF) for k in range(4)]
        bs = area(heads, 0, G, CH)
        jbb = area(heads, 1024, G, CH)
        ca = area(heads, 5184, G, CH)
        cb = area(heads, 5696, G, CH)
        ang = area(heads, 2560, G, NPW)
        ang2 = area(heads, 3104, G, NPW)
        mag = area(heads, 3648, G, NPW)
        nbb = area(heads, 4192, G, CH)
        whole = area(keep, 16896, G, NPW)
        cang = area(keep, 14848, G, NC)
        cang2 = area(keep, 14848 + 1024, G, NC)

        y_hi = area(split, HEADS, D)
        y_lo = area(split, HEADS + D, D)
        oneT = sb("oneT", [P, 2, T], F32R)
        gslot = sb("gslot", [P, 1])
        ev = area(heads, HEADS, 12, XU, rows=E)
        rte = area(heads, HEADS + D, 2, T, rows=E)
        vec = sb("vec", [P, 15])
        posi = sb("posi", [P, TB], I32)
        st6 = sb("st6", [P, TB, 2, 6])
        stat = sb("stat", [P, 48])
        sm = sb("sm", [P, 4, TB, 8])
        ids = sb("ids", [1, XU], I32)
        cnt = sb("cnt", [1, 2], I32)
        ut = nc.dram_tensor("u_time", [T, SSM], F32).ap()
        yt = nc.dram_tensor("y_time", [T, SSM], F32).ap()

        names = """ld_const ld_x ld_ln ld_w_in0 ld_w_in1 ld_par ld_attn_w ld_glu ld_wo ld_shared ld_small st_u
            ld_u st_y ld_y st_out j_c j_b j_bbar cbar_done bbar_done bb_signed wc_done wpre_done ln_stat
            ln_rstd x_ready xT_ps xT_sb proj h_sb u_sb kall_ps kall_sb wbt_ps wbt_sb kall_d kall_dma
            toep_zero cn_sq cn_ready cT_ps cT_sb qkv_ps qkv_sb heads_ready hT_ps hT_sb sc_ps smax p_sb
            pT_ps pT_sb pv_ps att_sb ug_ps ug_sb b_ps b_sb nb_ps z_done nz_ps s_done y_ps yg yT_ps yT_sb
            glu_ps glu_in glu_sig ssm_ready mix_ready mT_sb mix_ps x1_ready x_hi_ready x_lo_ready chosen
            gates_ready att_ready x1T_ps x1T_sb router_ps sig_sb rank_ps rank_sb rt_ps rt_sb tab_ps
            tab2_ps tables sh_up sh_silu sh_h sh_tps sh_tps_sb onehot gated gath xg_sb silu
            h_ready tps tps_sb combined down_left y_hi0 y_hi1 y0 y1 ln_shift normed final0 final1 dve act
            pool tabs mags tt_ready rope_sin ucg_ready nbs_sb turns chunks bt_ps bt_sb j_read ld_route
            one_sb gate_sb over_ready attT_ps att_sq ssmT_ps ssm_sq"""
        S = {n: sem("s_" + n) for n in names.split()}
        up = [sem(f"s_up{b}") for b in range(2)]
        up_half = [sem(f"s_up_half{b}") for b in range(2)]
        down = [sem(f"s_down{b}") for b in range(2)]
        wgu_in = [[sem(f"s_wgu_in{b}_{h}") for h in range(2)] for b in range(2)]
        over_gu_in = [sem(f"s_over_gu_in{h}") for h in range(2)]
        wd_in = [sem(f"s_wd_in{b}") for b in range(2)]

        wg, wu, wd = A["w_gate"], A["w_up"], A["w_down"]

        def unit_w(b, u):
            off = b * PAIR_W + u * PAIR_W // 2
            return area(ring, off, 2, DK, FF), area(ring, off + 2 * DK * FF, FK, D)

        block = ctx.enter_context(nc.Block())

        @block.sync
        def _(sp):
            sp.dma_start(const[:, :], A["const"]).then_inc(S["ld_const"], 16)
            sp.dma_start(x[:, 0, :], A["x"][0, 0:P, :]).then_inc(S["ld_x"], 16)
            sp.dma_start(x[:, 1, :], A["x"][0, P:T, :]).then_inc(S["ld_x"], 16)
            for n in range(2):
                sp.dma_start(lnr[:, n, :], A[("ln_in_g", "ln_in_b")[n]][:].partition_broadcast(P)
                             ).then_inc(S["ld_ln"], 16)
            for src, dst in (("lam", par[:, 0:3, :]), ("bstack", bs), ("cstack", ca)):
                sp.dma_start(dst, A[src]).then_inc(S["ld_par"], 16)
            for q in range(2):
                k = slice(q * DK // 2, (q + 1) * DK // 2)
                sp.dma_start(w_in[:, k], A["w_in"][0].rearrange("(k p) n -> p k n", p=P)[:, k]
                             ).then_inc(S[f"ld_w_in{q}"], 16)
            for src, dst in (("vec", vec[:, :]), ("dskip", drow[:, :]),
                             ("pos", posi[:, :])):
                sp.dma_start(dst, A[src]).then_inc(S["ld_small"], 16)
            sp.dma_start(wuq, A["w_uq"][0].rearrange("(k p) h d -> p k (h d)", p=P)).then_inc(S["ld_attn_w"], 16)
            sp.dma_start(wukv, A["w_ukv"][0].rearrange("p h d -> p (h d)")).then_inc(S["ld_attn_w"], 16)
            sp.dma_start(wglu, A["w_glu"][0].rearrange("(k p) n -> p k n", p=P)).then_inc(S["ld_glu"], 16)
            sp.wait_ge(S["x_ready"], 2)
            sp.dma_start(brow, A["b_glu"][0, :].partition_broadcast(P)).then_inc(S["ld_glu"], 16)
            sp.wait_ge(S["u_sb"], 2)
            sp.dma_start(ut.rearrange("(b p) n -> p b n", p=P), u1).then_inc(S["st_u"], 16)
            sp.wait_ge(S["st_u"], 16)
            sp.wait_ge(S["wpre_done"], 1)
            sp.dma_start(uc, ut.rearrange("(c j) n -> c j n", j=L)).then_inc(S["ld_u"], 16)
            sp.wait_ge(S["kall_d"], 1)
            sp.wait_ge(S["toep_zero"], 1)
            for j in range(L):
                sp.dma_start(toep[CH * j:CH * (j + 1), :, CH * j:], kall[:, :, 0:P - CH * j]
                             ).then_inc(S["kall_dma"], 16)
            sp.wait_ge(S["yg"], 2)
            for q in range(4):
                sp.dma_start(yt.rearrange("(c i) (q n) -> q c i n", i=L, q=4)[q],
                             yc[NC * q:NC * (q + 1)].rearrange("c i r o -> c i (r o)")).then_inc(S["st_y"], 16)
            sp.wait_ge(S["st_y"], 64)
            sp.dma_start(u1, yt.rearrange("(b p) n -> p b n", p=P)).then_inc(S["ld_y"], 16)
            sp.wait_ge(S["sc_ps"], 3)
            w_o = A["w_o"][0].rearrange("(k p) n -> p k n", p=P)
            sp.dma_start(wo[:, 2:], w_o[:, 2:]).then_inc(S["ld_wo"], 16)
            sp.wait_ge(S["pv_ps"], 2)
            sp.dma_start(wo[:, 0:2], w_o[:, 0:2]).then_inc(S["ld_wo"], 16)
            sp.wait_ge(S["y_ps"], 2)
            sp.dma_start(rbias, A["router_bias"][0, :].partition_broadcast(P)).then_inc(S["ld_route"], 16)
            sp.dma_start(low8, A["low8"]).then_inc(S["ld_route"], 16)
            for n in range(2):
                sp.dma_start(wsg[:, n, :, :], A[("ws_gate", "ws_up")[n]][0].rearrange("(p k) f -> p k f", k=DK)
                             ).then_inc(S["ld_shared"], 16)
            sp.dma_start(wsd, A["ws_down"][0].rearrange("(p k) n -> p k n", k=FK)).then_inc(S["ld_shared"], 16)
            sp.dma_start(wr, A["w_router"][0].rearrange("(p k) n -> p k n", k=DK)).then_inc(S["ld_shared"], 16)

            def pair_w(b):
                return ring[:, b * PAIR_W:(b + 1) * PAIR_W].rearrange("p (u w) -> p u w", u=2)

            def load_gate_up(b, half, expert):
                k = slice(half * DK // 2, (half + 1) * DK // 2)
                for n, w in enumerate((wg, wu)):
                    dst = pair_w(b)[:, :, n * DK * FF:(n + 1) * DK * FF].rearrange("p u (k f) -> p u k f", k=DK)
                    src = w[bass.ds(expert, 2)].rearrange("a (p k) f -> p a k f", k=DK)
                    sp.dma_start(dst[:, :, k].rearrange("p u k f -> p u (k f)"),
                                 src[:, :, k].rearrange("p a k f -> p a (k f)")).then_inc(wgu_in[b][half], 16)

            def load_down(b, expert):
                sp.dma_start(pair_w(b)[:, :, 2 * DK * FF:],
                             wd[bass.ds(expert, 2)].rearrange("a (p k) n -> p a (k n)", k=FK)
                             ).then_inc(wd_in[b], 16)

            sp.wait_ge(S["glu_in"], 2)
            sp.wait_ge(S["pT_ps"], 3)
            for n in range(2):
                sp.dma_start(lnr[:, n, :], A[("ln1_g", "ln1_b")[n]][0, :].partition_broadcast(P)
                             ).then_inc(S["ld_ln"], 16)
            for half in range(2):
                load_gate_up(1, half, 2)
            load_down(1, 2)
            sp.wait_ge(S["mix_ps"], 4)
            for half in range(2):
                load_gate_up(0, half, 0)
            load_down(0, 0)
            with sp.Fori(1, STEPS) as s:
                for b in range(2):
                    sp.wait_ge(up_half[b], s)
                    load_gate_up(b, 0, s * 4 + 2 * b)
                    sp.wait_ge(up[b], s)
                    load_gate_up(b, 1, s * 4 + 2 * b)
                    sp.wait_ge(down[b], s)
                    load_down(b, s * 4 + 2 * b)
            sp.wait_ge(S["over_ready"], 2)
            over = sp.value_load(cnt[0:1, 0:1], min_val=1, max_val=XU // 2)
            with sp.Fori(0, over) as j:
                experts = [sp.value_load(ids[0:1, bass.ds(2 * j + u, 1)], min_val=0, max_val=E - 1)
                           for u in range(2)]
                for half in range(2):
                    sp.wait_ge((up_half, up)[half][0], j + STEPS)
                    k = slice(half * DK // 2, (half + 1) * DK // 2)
                    for u in range(2):
                        for n, w in enumerate((wg, wu)):
                            sp.dma_start(unit_w(0, u)[0][:, n, k, :],
                                         w[bass.ds(experts[u], 1)].rearrange("a (p k) f -> p (a k) f", k=DK)[:, k]
                                         ).then_inc(over_gu_in[half], 16)
                sp.wait_ge(down[0], j + STEPS)
                for u in range(2):
                    sp.dma_start(unit_w(0, u)[1],
                                 wd[bass.ds(experts[u], 1)].rearrange("a (p k) n -> p (a k) n", k=FK)
                                 ).then_inc(wd_in[0], 16)
            sp.wait_ge(up[1], STEPS)
            for n in range(2):
                sp.dma_start(lnr[:, n, :], A[("ln2_g", "ln2_b")[n]][0, :].partition_broadcast(P)
                             ).then_inc(S["ld_ln"], 16)
            for b in range(TB):
                sp.wait_ge(S[f"final{b}"], 2 - b)
                sp.dma_start(out[0, b * P:(b + 1) * P, :], x[:, b, :]).then_inc(S["st_out"], 16)
            sp.wait_ge(S["st_out"], 16 * TB)

        def unit_cols(t, i, n=2):
            return t[:, :, bass.ds(2 * i, n)].unsqueeze(3).to_broadcast([P, TB, n, CAP])

        def slots(n):
            return C["iota"].unsqueeze(1).unsqueeze(1).to_broadcast([P, TB, n, CAP])

        def wait_from_1(eng, semaphore, n):
            if not (isinstance(n, int) and n < 1):
                eng.wait_ge(semaphore, n)

        @block.gpsimd
        def _(pool):
            n = [0]

            def step(ins):
                n[0] += 1
                ins.then_inc(S["pool"], 1)
                pool.wait_ge(S["pool"], n[0])

            def bc(t, rows, k):
                return t[:, :, rows].unsqueeze(3).to_broadcast([P, G, k, CH])

            def each(t, k):
                return t.unsqueeze(2).to_broadcast([P, G, k, CH])

            pool.wait_ge(S["cbar_done"], 1)
            pool.wait_ge(S["tabs"], 1)
            step(nc.gpsimd.tensor_copy(wc[:, :, 0, :], ca))
            step(nc.gpsimd.tensor_tensor(wc[:, :, 1:, :], bc(lr, slice(L + 1, NPW), L), each(ca, L), ALU.mult))
            step(nc.gpsimd.tensor_tensor(wtmp, bc(li, slice(L + 1, NPW), L), each(cb, L), ALU.mult))
            nc.gpsimd.tensor_tensor(wc[:, :, 1:, :], wc[:, :, 1:, :], wtmp, ALU.add).then_inc(S["wc_done"], 1)
            pool.wait_ge(S["wpre_done"], 1)
            pool.wait_ge(S["chunks"], 1)
            nc.gpsimd.memset(toep, 0.0).then_inc(S["toep_zero"], 1)
            for b in range(TB):
                pool.wait_ge(S["x_hi_ready"], b + 1)
                nc.gpsimd.tensor_tensor(x_lo[:, b], x[:, b, :].rearrange("p (q k) -> p k q", k=DK),
                                        x_hi[:, b].bitcast(F32), ALU.subtract).then_inc(S["x_lo_ready"], 1)

            def gated(i, group, m, buf, b, turned):
                pool.wait_ge(S["onehot"], group + 1)
                wait_from_1(pool, S["tps"], turned)
                nc.gpsimd.tensor_tensor(pg[:, b], pm[:, buf, :, 2 * m:2 * m + 2, :].bitcast(F32), unit_cols(gu, i),
                                        ALU.mult).then_inc(S["gated"], 1)

            def group(n, buf):
                for m in range(GP):
                    i = n * GP + m
                    gated(i, n, m, buf, m % 2, i - 1)

            pool.wait_ge(S["gates_ready"], 1)
            group(0, 0)
            with pool.Fori(0, GROUPS // 2 - 1) as s:
                group(2 * s + 1, 1)
                group(2 * s + 2, 0)
            group(GROUPS - 1, 1)
            pool.wait_ge(S["over_ready"], 2)
            over = pool.value_load(cnt[0:1, 0:1], min_val=1, max_val=XU // 2)
            with pool.Fori(0, over) as j:
                gated(j + 2 * STEPS, j + GROUPS, 0, 0, 0, j + 2 * STEPS)
            pool.wait_ge(S["ld_ln"], 96)
            for c in range(2):
                half = slice(c * 512, (c + 1) * 512)
                pool.wait_ge(S["normed"], c + 1)
                step(nc.gpsimd.tensor_tensor(x[:, 0, half], x[:, 0, half], lnr[:, 0, half], ALU.mult))
                nc.gpsimd.tensor_tensor(x[:, 0, half], x[:, 0, half], lnr[:, 1, half], ALU.add).then_inc(S["final0"], 1)

        @block.scalar
        def _(act):
            n = [0]

            def step(ins):
                n[0] += 1
                ins.then_inc(S["act"], 1)
                act.wait_ge(S["act"], n[0])

            def f(out_, in_, func, **k):
                return nc.scalar.activation(out_, in_, func, **k)

            act.wait_ge(S["ld_const"], 16)
            for b in range(TB):
                act.wait_ge(S["ln_stat"], b + 1)
                f(stat[:, 4 + b:5 + b], stat[:, 2 * b + 1:2 * b + 2], ACT.Sqrt, bias=C["eps"]).then_inc(S["ln_rstd"], 1)
            act.wait_ge(S["ld_par"], 48)
            f(par[:, 3, :], par[:, 2, :], ACT.Exp).then_inc(S["mags"], 1)
            act.wait_ge(S["j_b"], 1)
            f(nbb.rearrange("p g c -> p (g c)"), ps[:, 6, :], ACT.Copy).then_inc(S["nbs_sb"], 1)
            for b in range(TB):
                for q in range(2):
                    act.wait_ge(S["xT_ps"], 2 * b + q + 1)
                    f(xT[:, 4 * q:4 * q + 4, b * P:(b + 1) * P],
                      ps[:, 2 * b + q, :].rearrange("p (k t) -> p k t", k=4), ACT.Copy).then_inc(S["xT_sb"], 1)
            act.wait_ge(S["j_c"], 1)
            f(cb.rearrange("p g c -> p (g c)"), ps[:, 7, :], ACT.Copy).then_inc(S["cbar_done"], 1)
            act.wait_ge(S["tt_ready"], 1)
            step(f(par[:, 6, :], par[:, 4, :], ACT.Exp))
            step(f(mag, ang2, ACT.Exp))
            step(f(par[:, 8, :], par[:, 5, :], ACT.Sin))
            f(par[:, 9, :], par[:, 7, :], ACT.Sin, bias=C["half_pi"]).then_inc(S["mags"], 1)
            act.wait_ge(S["turns"], 1)
            step(f(li, ang, ACT.Sin, scale=SIN_SCALE))
            step(f(ang2, ang, ACT.Abs))
            f(lr, ang2, ACT.Sin, scale=-SIN_SCALE, bias=C["half_pi"]).then_inc(S["mags"], 1)
            act.wait_ge(S["turns"], 2)
            step(f(rp[:, 1], rp[:, 0], ACT.Sin))
            step(f(rp[:, 2], rp[:, 0], ACT.Abs))
            f(rp[:, 3], rp[:, 2], ACT.Sin, scale=-1.0, bias=C["half_pi"]).then_inc(S["rope_sin"], 1)
            act.wait_ge(S["proj"], 4)
            act.wait_ge(S["mags"], 3)
            act.wait_ge(S["tabs"], 1)
            for b in range(TB):
                f(hc[:, b, :], ps[:, 4 + 2 * b, 0:CW], ACT.Copy).then_inc(S["h_sb"], 1)
                f(u1[:, b, :], ps[:, 5 + 2 * b, :], ACT.Copy).then_inc(S["u_sb"], 1)
            act.wait_ge(S["u_sb"], 2)
            for b in range(TB):
                act.wait_ge(S["h_sb"], b + 1)
                step(f(ps[:, 7, 0:QR], hc[:, b, 0:QR], ACT.Square, scale=QR ** -0.5,
                       accum_out=stat[:, 8 + 2 * b:9 + 2 * b]))
                step(f(ps[:, 7, 0:KVR], hc[:, b, QR:QR + KVR], ACT.Square, scale=KVR ** -0.5,
                       accum_out=stat[:, 9 + 2 * b:10 + 2 * b]))
            f(stat[:, 12:16], stat[:, 8:12], ACT.Sqrt, bias=C["eps"]).then_inc(S["cn_sq"], 1)
            def wbt_out(r):
                act.wait_ge(S["wbt_ps"], r + 1)
                f(wb[:, 4 * r:4 * r + 4, :], ps[:, r % 4, :].rearrange("p (g n) -> p g n", g=4),
                  ACT.Copy).then_inc(S["wbt_sb"], 1)

            for r in range(4):
                wbt_out(r)
            act.wait_ge(S["cT_ps"], 1)
            act.wait_ge(S["ld_small"], 48)
            for k in range(3):
                f(cT[:, k, :], ps[:, 4 + k, 0:T], ACT.Copy, scale=vec[:, k:k + 1]).then_inc(S["cT_sb"], 1)
            for r in range(4, 8):
                wbt_out(r)
            def qkv_out(b):
                if b == 0:
                    act.wait_ge(S["ucg_ready"], 1)
                act.wait_ge(S["qkv_ps"], 2 * b + 1)
                f(qf[:, b, :, 0:QK].rearrange("p (a h) d -> p a h d", a=2),
                  ps[:, 4:6, 0:4 * QK].rearrange("p a (h d) -> p a h d", h=4), ACT.Copy).then_inc(S["qkv_sb"], 1)
                act.wait_ge(S["qkv_ps"], 2 * b + 2)
                kv = ps[:, 6:8, :].rearrange("p a (h d) -> p (a h) d", h=4)
                f(kf[:, b, :, 0:NOPE], kv[:, :, 0:NOPE], ACT.Copy).then_inc(S["qkv_sb"], 1)
                f(vv[:, b, :].rearrange("p (h d) -> p h d", h=H), kv[:, :, NOPE:], ACT.Copy).then_inc(S["qkv_sb"], 1)

            qkv_out(0)
            act.wait_ge(S["wc_done"], 1)
            for r in range(2):
                act.wait_ge(S["ug_ps"], r + 1)
                f(ug[:, 16 * r:16 * r + 16, :], ps[:, r, :].rearrange("p (g c) -> p g c", g=16),
                  ACT.Copy).then_inc(S["ug_sb"], 1)
            act.wait_ge(S["turns"], 3)
            step(f(sinc, cang, ACT.Sin, scale=SIN_SCALE))
            step(f(cang2, cang, ACT.Abs))
            f(cosc, cang2, ACT.Sin, scale=-SIN_SCALE, bias=C["half_pi"]).then_inc(S["chunks"], 1)
            qkv_out(1)
            for r in range(2):
                act.wait_ge(S["bt_ps"], r + 1)
                f(bt[:, 4 * r:4 * r + 4, :], ps[:, 2 + r, :].rearrange("p (r n) -> p r n", r=4),
                  ACT.Copy).then_inc(S["bt_sb"], 1)
            for r in range(2):
                act.wait_ge(S["b_ps"], r + 1)
                f(sb_b.rearrange("p (q r) c -> p r q c", q=4)[:, 4 * r:4 * r + 4],
                  ps[:, r, :].rearrange("p (r q c) -> p r q c", r=4, q=4), ACT.Copy).then_inc(S["b_sb"], 1)
            act.wait_ge(S["kall_ps"], 1)
            for q in range(4):
                f(kall[:, 8 * q:8 * q + 8, :], ps[NC * q:NC * q + CH, 2:4, :].rearrange("p a (g n) -> p (a g) n", g=4),
                  ACT.Copy).then_inc(S["kall_sb"], 1)
            for t in range(2):
                dst = (qT, kT)[t]
                act.wait_ge(S["hT_ps"], t + 1)
                f(dst[0:QKX, :, :], ps[0:QKX, 4:8, :].rearrange("p a (h t) -> p (a h) t", h=2),
                  ACT.Copy).then_inc(S["hT_sb"], 1)
            def exps(r):
                act.wait_ge(S["smax"], r + 1)
                if r == 0:
                    w, heads, off = P, range(8), 0
                else:
                    w, heads, off = T, range(4 * (r - 1), 4 * r), 1024 + 1024 * (r - 1)
                bank = (4, 6, 2)[r]
                for m, h in enumerate(heads):
                    col = 16 + 8 * min(r, 1) + h
                    src = ps[:, bank:bank + 2, :].rearrange("p a n -> p (a n)")[:, m * w:(m + 1) * w]
                    last = f(prob[:, off + m * w:off + (m + 1) * w], src, ACT.Exp, scale=SCALE,
                             bias=stat[:, col:col + 1], accum_out=stat[:, col + 16:col + 17])
                    if m < len(heads) - 1:
                        last.then_inc(S["act"], 1)
                        n[0] += 1
                last.then_inc(S["p_sb"], 1)
                act.wait_ge(S["act"], n[0])

            for r in range(3):
                exps(r)
            for r in range(2):
                act.wait_ge(S["y_ps"], r + 1)
                f(yc[:, :, 4 * r:4 * r + 4, :], ps[:, r, :].rearrange("p (r i o) -> p i r o", r=4, i=L),
                  ACT.Gelu_apprx_tanh).then_inc(S["yg"], 1)
            act.wait_ge(S["yT_ps"], 1)
            f(yT, ps[:, 0:2, :].rearrange("p a (k t) -> p (a k) t", k=2), ACT.Copy).then_inc(S["yT_sb"], 1)
            for b in range(TB):
                act.wait_ge(S["att_sb"], b + 1)
                act.wait_ge(S["pT_sb"], 3)
                step(f(ps[:, 7, :], att[:, b, :], ACT.Square, scale=SSM ** -0.5, accum_out=stat[:, 8 + b:9 + b]))
            f(stat[:, 12:14], stat[:, 8:10], ACT.Sqrt, bias=C["eps"]).then_inc(S["att_sq"], 1)
            for k in range(4):
                act.wait_ge(S["attT_ps"], k // 2 + 1)
                f(mT[:, k, :], ps[:, 6 + k // 2, (k % 2) * T:(k % 2 + 1) * T], ACT.Copy,
                  scale=vec[:, 3 + k:4 + k]).then_inc(S["mT_sb"], 1)
            for b in range(TB):
                act.wait_ge(S["glu_in"], b + 1)
                f(gate[:, b, :], gate[:, b, :], ACT.Sigmoid).then_inc(S["glu_sig"], 1)
            act.wait_ge(S["glu_sig"], 2)
            for b in range(TB):
                act.wait_ge(S["ssm_ready"], b + 1)
                step(f(ps[:, 2 + b, :], u1[:, b, :], ACT.Square, scale=SSM ** -0.5, accum_out=stat[:, 10 + b:11 + b]))
            f(stat[:, 14:16], stat[:, 10:12], ACT.Sqrt, bias=C["eps"]).then_inc(S["ssm_sq"], 1)
            for k in range(4, 8):
                act.wait_ge(S["ssmT_ps"], k // 2 - 1)
                f(mT[:, k, :], ps[:, k // 2 - 2, (k % 2) * T:(k % 2 + 1) * T], ACT.Copy,
                  scale=vec[:, 3 + k:4 + k]).then_inc(S["mT_sb"], 1)

            def x1_rstd(b):
                act.wait_ge(S["ln_stat"], 3 + b)
                f(stat[:, 4 + b:5 + b], stat[:, 2 * b + 1:2 * b + 2], ACT.Sqrt, bias=C["eps"]).then_inc(S["ln_rstd"], 1)

            x1_rstd(0)
            for b in range(TB):
                for q in range(2):
                    act.wait_ge(S["x1T_ps"], 2 * b + q + 1)
                    f(xT[:, 4 * q:4 * q + 4, b * P:(b + 1) * P],
                      ps[:, 2 * b + q, :].rearrange("p (k t) -> p k t", k=4), ACT.Copy).then_inc(S["x1T_sb"], 1)
                if b == 0:
                    x1_rstd(1)
                act.wait_ge(S["router_ps"], b + 1)
                f(rt[:, 0, b, :], ps[:, 5 - b, 0:E], ACT.Sigmoid).then_inc(S["sig_sb"], 1)
            for b in range(TB):
                act.wait_ge(S["x1_ready"], b + 1)
                f(x_hi[:, b], x[:, b, :].rearrange("p (q k) -> p k q", k=DK), ACT.Copy).then_inc(S["x_hi_ready"], 1)

            def shared_silu(b):
                act.wait_ge(S["sh_up"], b + 1)
                f(hs[:, b], ps[:, 6, 0:FF], ACT.Silu).then_inc(S["sh_silu"], 1)

            def evac_gather(dst, count):
                for q in range(2):
                    act.wait_ge(S["gath"], count + q + 1)
                    f(dst(q), ps[:, 4 + q, :].rearrange("p (m s) -> p m s", m=GP), ACT.Copy).then_inc(S["xg_sb"], 1)

            def part(n, buf, r):
                evac_gather(lambda q: xg[buf][2 * r + q], 2 * GP * n + 2 * r)

            def over_part(j, q):
                act.wait_ge(S["gath"], 2 * j + (2 * GP * GROUPS + q + 1))
                f(area(keep, 12800, DK, GP * P)[:, 4 * q:4 * q + 4, 0:P], ps[:, 4 + q, :].rearrange("p (k s) -> p k s", k=4),
                  ACT.Copy).then_inc(S["xg_sb"], 1)

            def pair(i, b, use, sg_read, then):
                act.wait_ge(up[b], use)
                wait_from_1(act, S["h_ready"], sg_read)
                f(sg[:, b], ps[:, 6, 0:FF], ACT.Silu).then_inc(S["silu"], 1)
                then()
                act.wait_ge(S["gate_sb"], i + 1)
                act.wait_ge(S["down_left"], i + 1)
                f(y_hi[:, 0:512], ps[:, 6, :], ACT.Copy, scale=gslot[:, 0:1]).then_inc(S["y_hi0"], 1)
                act.wait_ge(down[b], use)
                f(y_hi[:, 512:D], ps[:, 7, :], ACT.Copy, scale=gslot[:, 0:1]).then_inc(S["y_hi1"], 1)

            def group(n, buf):
                for m in range(GP):
                    i = n * GP + m
                    pair(i, m % 2, n * 2 + m // 2 + 1, i - 1, lambda: part(n + 1, 1 - buf, m))

            shared_silu(0)
            for r in range(GP):
                part(0, 0, r)
            act.wait_ge(S["ld_route"], 32)
            act.wait_ge(S["gates_ready"], 1)
            act.wait_ge(S["x_lo_ready"], 2)
            group(0, 0)
            with act.Fori(0, MIDDLE) as s:
                group(2 * s + 1, 1)
                group(2 * s + 2, 0)
            shared_silu(1)
            with act.Fori(MIDDLE, GROUPS // 2 - 1) as s:
                group(2 * s + 1, 1)
                group(2 * s + 2, 0)
            for m in range(GP):
                i = (GROUPS - 1) * GP + m
                pair(i, m % 2, i // 2 + 1, i - 1, (lambda: over_part(0, m)) if m < 2 else (lambda: None))
            act.wait_ge(S["over_ready"], 2)
            over = act.value_load(cnt[0:1, 0:1], min_val=1, max_val=XU // 2)
            with act.Fori(0, over) as j:
                i = j + 2 * STEPS
                pair(i, 0, j + STEPS + 1, i, lambda: over_part(j + 1, 0))
                over_part(j + 1, 1)
            act.wait_ge(S["ln_stat"], 5)
            f(stat[:, 4:5], stat[:, 1:2], ACT.Sqrt, bias=C["eps"]).then_inc(S["ln_rstd"], 1)
            act.wait_ge(S["ln_shift"], 1)
            for c in range(2):
                half = slice(c * 512, (c + 1) * 512)
                f(x[:, 0, half], x[:, 0, half], ACT.Identity, scale=stat[:, 6:7], bias=stat[:, 8:9]).then_inc(S["normed"], 1)
            act.wait_ge(S["ln_stat"], 6)
            f(stat[:, 5:6], stat[:, 3:4], ACT.Sqrt, bias=C["eps"]).then_inc(S["ln_rstd"], 1)

        @block.vector
        def _(dve):
            n = [0]

            def step(ins):
                n[0] += 1
                ins.then_inc(S["dve"], 1)
                dve.wait_ge(S["dve"], n[0])

            def ts(o, i, a, b, op0, op1=ALU.bypass):
                if b is None:
                    return nc.vector.tensor_scalar(o, i, a, None, op0)
                return nc.vector.tensor_scalar(o, i, a, b, op0, op1)

            def tt2(o, a, b, op):
                return nc.vector.tensor_tensor(o, a, b, op)

            def layer_norm(b):
                for q in range(2):
                    step(nc.vector.bn_stats(st6[:, b, q, :], x[:, b, 512 * q:512 * q + 512]))
                nc.vector.bn_aggr(stat[:, 2 * b:2 * b + 2], st6[:, b, :, :]).then_inc(S["ln_stat"], 1)

            def layer_norm_end(b, k, ready):
                dve.wait_ge(S["ln_rstd"], k + 1)
                step(nc.vector.reciprocal(stat[:, 6 + b:7 + b], stat[:, 4 + b:5 + b]))
                step(nc.vector.scalar_tensor_tensor(x[:, b, :], x[:, b, :], stat[:, 2 * b:2 * b + 1], lnr[:, 0, :],
                                                    ALU.subtract, ALU.mult))
                nc.vector.scalar_tensor_tensor(x[:, b, :], x[:, b, :], stat[:, 6 + b:7 + b], lnr[:, 1, :],
                                               ALU.mult, ALU.add).then_inc(ready, 1)

            dve.wait_ge(S["ld_x"], 32)
            for b in range(TB):
                layer_norm(b)
            dve.wait_ge(S["ld_ln"], 32)
            for b in range(TB):
                layer_norm_end(b, b, S["x_ready"])
            dve.wait_ge(S["ld_par"], 48)
            ts(ca[ST:P], ca[ST:P], -1.0, None, ALU.mult).then_inc(S["bb_signed"], 1)

            pr = lambda k: par[:, k, :]
            dve.wait_ge(S["ld_par"], 48)
            dve.wait_ge(S["mags"], 1)
            step(ts(pr(0), pr(0), -1e-4, None, ALU.min))
            step(tt2(pr(4), pr(0), pr(3), ALU.mult))
            step(tt2(pr(10), pr(1), pr(3), ALU.mult))
            step(ts(pr(11), pr(10), 1.0 / TWO_PI, ROUND, ALU.mult, ALU.add))
            step(ts(pr(11), pr(11), ROUND, None, ALU.subtract))
            for c in (PI_1, PI_2, PI_3):
                step(nc.vector.scalar_tensor_tensor(pr(10), pr(11), -c, pr(10), ALU.mult, ALU.add))
            step(ts(pr(5), pr(10), 3.1415925, -3.1415925, ALU.min, ALU.max))
            step(nc.vector.scalar_tensor_tensor(pr(7), pr(5), -1.0, pr(5), ALU.mult, ALU.min))
            powers = C["powers"].unsqueeze(1).to_broadcast([P, G, NPW])
            tt2(ang2, pr(4).unsqueeze(2).to_broadcast([P, G, NPW]), powers, ALU.mult).then_inc(S["tt_ready"], 1)
            dve.wait_ge(S["mags"], 2)
            re, im = pr(0), pr(1)
            step(tt2(pr(16), pr(6), pr(9), ALU.mult))
            step(ts(pr(16), pr(16), -1.0, None, ALU.add))
            step(tt2(pr(17), pr(6), pr(8), ALU.mult))
            step(tt2(pr(18), re, re, ALU.mult))
            step(tt2(pr(19), im, im, ALU.mult))
            step(tt2(pr(18), pr(18), pr(19), ALU.add))
            step(nc.vector.reciprocal(pr(18), pr(18)))
            step(tt2(pr(19), pr(16), re, ALU.mult))
            step(tt2(pr(20), pr(17), im, ALU.mult))
            step(tt2(pr(19), pr(19), pr(20), ALU.add))
            step(tt2(pr(19), pr(19), pr(18), ALU.mult))
            step(tt2(pr(20), pr(17), re, ALU.mult))
            step(tt2(pr(21), pr(16), im, ALU.mult))
            step(tt2(pr(20), pr(20), pr(21), ALU.subtract))
            step(tt2(pr(20), pr(20), pr(18), ALU.mult))
            dve.wait_ge(S["nbs_sb"], 1)
            col = lambda k: pr(k).unsqueeze(2).to_broadcast([P, G, CH])
            step(tt2(bbar, col(19), bs, ALU.mult))
            step(tt2(jbb, col(20), nbb, ALU.mult))
            tt2(bbar, bbar, jbb, ALU.subtract).then_inc(S["bbar_done"], 1)
            dve.wait_ge(S["bbar_done"], 1)
            step(ts(pr(12), pr(10), 1.0 / TWO_PI, None, ALU.mult))
            step(tt2(ang, pr(12).unsqueeze(2).to_broadcast([P, G, NPW]), powers, ALU.mult))
            step(ts(whole, ang, ROUND, ROUND, ALU.add, ALU.subtract))
            tt2(ang, ang, whole, ALU.subtract).then_inc(S["turns"], 1)
            dve.wait_ge(S["ld_small"], 48)
            step(nc.vector.tensor_copy(stat[:, 46:48], posi[:, :]))
            for b in range(TB):
                step(ts(rp[:, 4, b, :], C["invf"], stat[:, 46 + b:47 + b], None, ALU.mult))
            step(ts(rp[:, 5], rp[:, 4], 1.0 / TWO_PI, ROUND, ALU.mult, ALU.add))
            step(ts(rp[:, 5], rp[:, 5], ROUND, None, ALU.subtract))
            for c in (PI_1, PI_2, PI_3):
                step(nc.vector.scalar_tensor_tensor(rp[:, 4], rp[:, 5], -c, rp[:, 4], ALU.mult, ALU.add))
            ts(rp[:, 0], rp[:, 4], 3.1415925, -3.1415925, ALU.min, ALU.max).then_inc(S["turns"], 1)
            dve.wait_ge(S["mags"], 3)
            step(nc.vector.tensor_copy(pr(22), mag[:, :, NPW - 1]))
            step(tt2(lr, lr, mag, ALU.mult))
            tt2(li, li, mag, ALU.mult).then_inc(S["tabs"], 1)
            dve.wait_ge(S["tabs"], 1)
            dve.wait_ge(S["j_bbar"], 1)
            nc.vector.tensor_copy(jbb, ps[:, 0, :].rearrange("p (g c) -> p g c", g=G)).then_inc(S["j_read"], 1)
            dve.wait_ge(S["j_read"], 1)
            pb = lambda t: t[:, :, 0:L].unsqueeze(3).to_broadcast([P, G, L, CH])
            step(tt2(wpre, pb(lr), bbar.unsqueeze(2).to_broadcast([P, G, L, CH]), ALU.mult))
            t4 = toep.rearrange("p g (j c) -> p g j c", j=L)
            step(tt2(t4, pb(li), jbb.unsqueeze(2).to_broadcast([P, G, L, CH]), ALU.mult))
            tt2(wpre, wpre, t4, ALU.subtract).then_inc(S["wpre_done"], 1)
            dve.wait_ge(S["wpre_done"], 1)
            step(ts(pr(13), pr(12), float(L), None, ALU.mult))
            step(ts(pr(14), pr(13), ROUND, ROUND, ALU.add, ALU.subtract))
            step(tt2(pr(13), pr(13), pr(14), ALU.subtract))
            step(ts(pr(14), pr(13), 4096.0, ROUND, ALU.mult, ALU.add))
            step(ts(pr(14), pr(14), ROUND, 1.0 / 4096.0, ALU.subtract, ALU.mult))
            step(tt2(pr(15), pr(13), pr(14), ALU.subtract))
            chunks = C["iota"][:, 0:NC].unsqueeze(1).to_broadcast([P, G, NC])
            wide = lambda k: pr(k).unsqueeze(2).to_broadcast([P, G, NC])
            step(tt2(cang, wide(14), chunks, ALU.mult))
            dve.wait_ge(S["cn_sq"], 1)
            step(nc.vector.reciprocal(stat[:, 12:16], stat[:, 12:16]))
            for b in range(TB):
                step(ts(hc[:, b, 0:QR], hc[:, b, 0:QR], stat[:, 12 + 2 * b:13 + 2 * b], None, ALU.mult))
                ts(hc[:, b, QR:QR + KVR], hc[:, b, QR:QR + KVR], stat[:, 13 + 2 * b:14 + 2 * b], None,
                   ALU.mult).then_inc(S["cn_ready"], 1)
            dve.wait_ge(S["ld_u"], 16)
            nc.vector.tensor_copy(ucg, uc.rearrange("p j (g c) -> p g j c", g=G)).then_inc(S["ucg_ready"], 1)
            step(ts(cang2, cang, ROUND, ROUND, ALU.add, ALU.subtract))
            step(tt2(cang, cang, cang2, ALU.subtract))
            step(tt2(cang2, wide(15), chunks, ALU.mult))
            step(tt2(cang, cang, cang2, ALU.add))
            step(ts(cang2, cang, ROUND, ROUND, ALU.add, ALU.subtract))
            tt2(cang, cang, cang2, ALU.subtract).then_inc(S["turns"], 1)
            dve.wait_ge(S["wc_done"], 1)
            step(nc.vector.tensor_copy(decay, pr(22).unsqueeze(2).to_broadcast([P, G, NC])))
            step(nc.vector.memset(decay[:, :, 0:1], 0.0))
            dve.wait_ge(S["wbt_ps"], 8)
            step(tt2(dterm, ident[0:CH, 0:CH].unsqueeze(1).to_broadcast([CH, G, CH]),
                     drow[:, :].unsqueeze(2).to_broadcast([CH, G, CH]), ALU.mult))

            dve.wait_ge(S["rope_sin"], 1)
            def rotate(x1, x2, c, s, t):
                step(tt2(t[0], x1, s, ALU.mult))
                step(tt2(t[1], x2, s, ALU.mult))
                step(tt2(t[2], x2, c, ALU.mult))
                step(tt2(t[3], x1, c, ALU.mult))
                step(tt2(x1, t[3], t[1], ALU.subtract))
                step(tt2(x2, t[2], t[0], ALU.add))

            rotate(hc[:, :, QR + KVR:QR + KVR + HALF], hc[:, :, QR + KVR + HALF:CW], rp[:, 3], rp[:, 1],
                   [rp[:, k] for k in (4, 5, 6, 7)])
            dve.wait_ge(S["qkv_sb"], 6)
            spread = lambda t: t.unsqueeze(2).to_broadcast([P, TB, H, HALF])
            rotate(qf[:, :, :, NOPE:NOPE + HALF], qf[:, :, :, NOPE + HALF:QK], spread(rp[:, 3]), spread(rp[:, 1]), rtmp)
            for b in range(TB):
                step(nc.vector.tensor_copy(kf[:, b, :, NOPE:QK],
                                           hc[:, b, QR + KVR:CW].unsqueeze(1).to_broadcast([P, H, ROPE])))
            for t, m in ((qf, "qmask"), (kf, "kmask")):
                last = nc.vector.tensor_copy(t[:, :, :, QK:QKX], C[m].rearrange("p (b m) -> p b m", b=TB)
                                             .unsqueeze(2).to_broadcast([P, TB, H, TB]))
                if t is qf:
                    step(last)
            last.then_inc(S["heads_ready"], 1)

            dve.wait_ge(S["nb_ps"], 2)
            dve.wait_ge(S["b_sb"], 2)
            dve.wait_ge(S["chunks"], 1)
            flat = lambda t: t.rearrange("p g c -> p (g c)")
            two = ps[:, 0:2, :].rearrange("p a n -> p (a n)")
            step(tt2(flat(sb_w), flat(sinc), two, ALU.mult))
            step(tt2(sb_z, cosc, sb_b, ALU.mult))
            step(tt2(sb_w, sb_w, sb_z, ALU.add))
            dve.wait_ge(S["kall_sb"], 4)
            tt2(kall[:, :, 0:CH], kall[:, :, 0:CH], dterm, ALU.add).then_inc(S["kall_d"], 1)
            nc.vector.tensor_tensor_scan(flat(sb_z), flat(decay), flat(sb_w), 0.0, ALU.mult, ALU.add).then_inc(S["z_done"], 1)
            dve.wait_ge(S["z_done"], 1)
            step(tt2(sb_b, cosc, sb_z, ALU.mult))
            step(nc.vector.memset(sb_s[:, :, 0:1], 0.0))
            dve.wait_ge(S["nz_ps"], 2)
            two = ps[:, 2:4, :].rearrange("p a n -> p (a n)")
            step(tt2(flat(sb_w), flat(sinc), two, ALU.mult))
            tt2(sb_s[:, :, 1:], sb_b, sb_w, ALU.subtract).then_inc(S["s_done"], 1)

            for r in range(3):
                dve.wait_ge(S["sc_ps"], r + 1)
                w, m, c = ((P, 8, 16), (T, 4, 24), (T, 4, 28))[r]
                bank = (4, 6, 2)[r]
                src = ps[:, bank:bank + 2, :].rearrange("p a n -> p (a n)").rearrange("p (h k) -> p h k", h=m)
                step(nc.vector.tensor_reduce(stat[:, c:c + m], src, AX.X, ALU.max))
                ts(stat[:, c:c + m], stat[:, c:c + m], -SCALE, None, ALU.mult).then_inc(S["smax"], 1)
            dve.wait_ge(S["pT_ps"], 1)
            nc.vector.tensor_copy(pt0.rearrange("p h q -> p (h q)"), ps[:, 6:8, :].rearrange("p a n -> p (a n)")).then_inc(S["pT_sb"], 1)
            for r in range(2):
                dve.wait_ge(S["pT_ps"], 2 + r)
                bank = (4, 6)[r]
                nc.vector.tensor_copy(pt1[:, 4 * r:4 * r + 4].rearrange("p h k q -> p (h k q)"),
                                      ps[:, bank:bank + 2, :].rearrange("p a n -> p (a n)")).then_inc(S["pT_sb"], 1)
            step(nc.vector.reciprocal(stat[:, 32:48], stat[:, 32:48]))
            for b in range(TB):
                dve.wait_ge(S["pv_ps"], b + 1)
                tt2(att[:, b, :].rearrange("p (h d) -> p h d", h=H), ps[:, 4 + b, :].rearrange("p (h d) -> p h d", h=H),
                    stat[:, 32 + 8 * b:40 + 8 * b].unsqueeze(2).to_broadcast([P, H, VD]), ALU.mult).then_inc(S["att_sb"], 1)
            dve.wait_ge(S["att_sq"], 1)
            step(nc.vector.reciprocal(stat[:, 12:14], stat[:, 12:14]))
            for b in range(TB):
                ts(att[:, b, :], att[:, b, :], stat[:, 12 + b:13 + b], None, ALU.mult).then_inc(S["att_ready"], 1)
            dve.wait_ge(S["ld_y"], 16)
            dve.wait_ge(S["ld_glu"], 32)
            for b in range(TB):
                dve.wait_ge(S["glu_ps"], b + 1)
                tt2(gate[:, b, :], ps[:, 2 + b, :], brow, ALU.add).then_inc(S["glu_in"], 1)
            for b in range(TB):
                dve.wait_ge(S["glu_sig"], b + 1)
                tt2(u1[:, b, :], u1[:, b, :], gate[:, b, :], ALU.mult).then_inc(S["ssm_ready"], 1)
            dve.wait_ge(S["ssm_sq"], 1)
            step(nc.vector.reciprocal(stat[:, 14:16], stat[:, 14:16]))
            for b in range(TB):
                ts(u1[:, b, :], u1[:, b, :], stat[:, 14 + b:15 + b], None, ALU.mult).then_inc(S["mix_ready"], 1)
            for b in range(TB):
                for c in range(2):
                    dve.wait_ge(S["mix_ps"], 2 * b + c + 1)
                    half = slice(c * 512, (c + 1) * 512)
                    step(nc.vector.scalar_tensor_tensor(x[:, b, half], x[:, b, half], ALPHA, ps[:, 4 + 2 * b + c, :],
                                                        ALU.mult, ALU.add))
                    step(nc.vector.bn_stats(st6[:, b, c, :], x[:, b, half]))
                nc.vector.bn_aggr(stat[:, 2 * b:2 * b + 2], st6[:, b, :, :]).then_inc(S["ln_stat"], 1)
                dve.wait_ge(S["ld_ln"], 64)
                layer_norm_end(b, 2 + b, S["x1_ready"])

            r_ = lambda k: rt[:, k, :, :]
            for b in range(TB):
                score, biased, best, picked, chosen = [rt[:, k, b, :] for k in (0, 1, 2, 4, 3)]
                grouped = lambda t: t.rearrange("p (g k) -> p g k", g=8)
                gs, gn, kept, shut = [sm[:, k, b, :] for k in range(4)]
                better, equal = cmp8[:, 0, b, :], cmp8[:, 1, b, :]
                if b == 0:
                    dve.wait_ge(S["ld_route"], 32)
                dve.wait_ge(S["sig_sb"], b + 1)
                step(tt2(biased, score, rbias, ALU.add))
                for g in range(8):
                    nc.vector.max(best[:, 8 * g:8 * g + 8], biased[:, 8 * g:8 * g + 8]).then_inc(S["dve"], 1)
                n[0] += 8
                dve.wait_ge(S["dve"], n[0])
                step(tt2(gs, grouped(best)[:, :, 0], grouped(best)[:, :, 1], ALU.add))
                mine = gs.unsqueeze(2).to_broadcast([P, 8, 8])
                other = gs.unsqueeze(1).to_broadcast([P, 8, 8])
                step(tt2(grouped(better), other, mine, ALU.is_gt))
                step(tt2(grouped(equal), other, mine, ALU.is_equal))
                step(tt2(equal, equal, low8, ALU.mult))
                step(tt2(better, better, equal, ALU.add))
                step(nc.vector.tensor_reduce(gn, grouped(better), AX.X, ALU.add))
                step(ts(kept, gn, 4.0, None, ALU.is_lt))
                step(ts(shut, kept, -NEG, NEG, ALU.mult, ALU.add))
                spread8 = lambda t: t.unsqueeze(2).to_broadcast([P, 8, 8])
                step(tt2(grouped(biased), grouped(biased), spread8(kept), ALU.mult))
                step(tt2(grouped(biased), grouped(biased), spread8(shut), ALU.add))
                step(nc.vector.max(gs, biased))
                step(nc.vector.match_replace(best, gs, biased, 3 * NEG))
                ts(chosen, best, 2 * NEG, None, ALU.is_lt).then_inc(S["chosen"], 1)
                dve.wait_ge(S["chosen"], b + 1)
                step(ts(best, chosen, -FAR, FAR, ALU.mult, ALU.add))
            dve.wait_ge(S["rank_ps"], 1)
            tt2(ru[:, :, 0:E], r_(2), ps[:, 7, 0:TB * E].rearrange("p (b e) -> p b e", b=TB), ALU.add).then_inc(S["rank_sb"], 1)
            dve.wait_ge(S["rank_sb"], 1)
            tt2(pm[:, 0], slots(2 * GP), unit_cols(ru, 0, 2 * GP), ALU.is_equal).then_inc(S["onehot"], 1)
            ex = lambda k, w=XU: ev[:, k, 0:w]
            step(tt2(ex(0, 3), ps[0:E, 7, 128:129].to_broadcast([E, 3]), C["thresh"][0:E], ALU.is_gt))
            nc.vector.tensor_reduce(ex(1, 1), ex(0, 3), AX.X, ALU.add).then_inc(S["tables"], 1)
            step(tt2(r_(4), r_(0), r_(3), ALU.mult))
            gsum, ginv = sm[:, 1, :, 0], sm[:, 1, :, 1]
            step(nc.vector.tensor_reduce(gsum, r_(4), AX.X, ALU.add))
            step(nc.vector.reciprocal(ginv, gsum))
            for b in range(TB):
                step(ts(gu[:, b, 0:E], rt[:, 4, b, :], sm[:, 1, b, 1:2], 2.5, ALU.mult, ALU.mult))
            step(nc.vector.memset(ru[:, :, NU:], FAR))
            nc.vector.memset(gu[:, :, NU:], 0.0).then_inc(S["gates_ready"], 1)

            def shared_hidden(b):
                dve.wait_ge(S["sh_silu"], b + 1)
                tt2(hs[:, b], hs[:, b], ps[:, 6, FF:2 * FF], ALU.mult).then_inc(S["sh_h"], 1)

            def shared_transposed():
                dve.wait_ge(S["sh_tps"], 2)
                nc.vector.tensor_copy(hT[:, :], ps[:, 7, :].rearrange("p (b f) -> p b f", b=TB)
                                      ).then_inc(S["sh_tps_sb"], 1)

            def one_hots(n, buf):
                tt2(pm[:, buf], slots(2 * GP), unit_cols(ru, n * GP, 2 * GP), ALU.is_equal).then_inc(S["onehot"], 1)

            def over_one_hot(j):
                tt2(pm[:, 0, :, 0:2, :], slots(2), unit_cols(ru, j + 2 * STEPS), ALU.is_equal).then_inc(S["onehot"], 1)

            shared_hidden(0)
            dve.wait_ge(S["rt_ps"], 1)
            step(nc.vector.tensor_copy(rte[:, :, :], ps[0:E, 2, :].rearrange("p (a t) -> p a t", a=2)))
            dve.wait_ge(S["tab_ps"], 1)
            step(tt2(ex(2, 3), C["level"][0:E], ps[0:E, 7, 130:131].to_broadcast([E, 3]), ALU.add))
            step(tt2(ex(2, 3), ex(2, 3), ex(0, 3), ALU.mult))
            step(ts(ex(2, 3), ex(2, 3), -1.0, None, ALU.add))
            for l in range(3):
                step(ts(ex(3 + l), C["iota"][0:E, 0:XU], ev[:, 2, l:l + 1], None, ALU.is_equal))
            step(tt2(ex(6), ex(3), ex(4), ALU.add))
            step(tt2(ex(6), ex(6), ex(5), ALU.add))
            step(ts(ex(7), ex(6), -FAR, None, ALU.mult))
            for l in range(2):
                step(nc.vector.scalar_tensor_tensor(ex(7), ex(3 + l), -float(CAP * (l + 1)), ex(7), ALU.mult, ALU.add))
            nc.vector.scalar_tensor_tensor(ex(7), ex(5), -3.0 * CAP, ex(7), ALU.mult, ALU.add).then_inc(S["rt_sb"], 1)
            dve.wait_ge(S["tab2_ps"], 1)
            step(ts(ru[:, :, E:NU], ps[:, 7, 192:192 + TB * XU].rearrange("p (b j) -> p b j", b=TB), FAR, None, ALU.add))
            step(nc.vector.tensor_copy(gu[:, :, E:NU], ps[:, 7, 256:256 + TB * XU].rearrange("p (b j) -> p b j", b=TB)))
            nc.vector.tensor_copy(ids[:, :], ps[0:1, 7, 320:320 + XU]).then_inc(S["over_ready"], 1)
            step(ts(ev[0:1, 9, 0:1], ps[0:1, 7, 352:353], 0.5, 0.25, ALU.mult, ALU.add))
            step(ts(ev[0:1, 9, 0:1], ev[0:1, 9, 0:1], ROUND, ROUND, ALU.add, ALU.subtract))
            step(ts(ev[0:1, 9, 0:1], ev[0:1, 9, 0:1], 1.0, None, ALU.max))
            nc.vector.tensor_copy(cnt[:, 0:1], ev[0:1, 9, 0:1]).then_inc(S["over_ready"], 1)

            def pair(i, b, turned, hb_read, one_read):
                dve.wait_ge(S["silu"], i + 1)
                wait_from_1(dve, S["tps"], hb_read)
                tt2(hb[:, b], sg[:, b], ps[:, 6, FF:2 * FF], ALU.mult).then_inc(S["h_ready"], 1)
                dve.wait_ge(S["tps"], i + 1)
                nc.vector.tensor_copy(hT[:, b], ps[:, 7, 0:FF]).then_inc(S["tps_sb"], 1)
                wait_from_1(dve, S["combined"], one_read)
                ts(oneT[:, turned], ps[:, 7, FF:], 0.0, None, ALU.is_gt).then_inc(S["one_sb"], 1)
                nc.vector.tensor_reduce(gslot[:, :], ps[:, 7, FF:], AX.X, ALU.add).then_inc(S["gate_sb"], 1)
                dve.wait_ge(S["gate_sb"], i + 1)
                for c in range(2):
                    half = slice(c * 512, (c + 1) * 512)
                    dve.wait_ge(S[f"y_hi{c}"], i + 1)
                    nc.vector.scalar_tensor_tensor(y_lo[:, half], ps[:, 6 + c, :], gslot[:, 0:1],
                                                   y_hi[:, half].bitcast(F32), ALU.mult, ALU.subtract
                                                   ).then_inc(S[f"y{c}"], 1)

            def group(n, next_one_hots):
                wait_from_1(dve, S["gath"], n * (2 * GP))
                wait_from_1(dve, S["gated"], n * GP)
                next_one_hots()
                for m in range(GP):
                    i = n * GP + m
                    pair(i, m % 2, m % 2, i - 1, i - 2)

            one_hots(1, 1)
            for m in range(GP):
                pair(m, m % 2, m % 2, m - 1, m - 2)
            with dve.Fori(0, MIDDLE) as s:
                group(2 * s + 1, lambda: one_hots(2 * s + 2, 0))
                group(2 * s + 2, lambda: one_hots(2 * s + 3, 1))
            shared_hidden(1)
            shared_transposed()
            with dve.Fori(MIDDLE, GROUPS // 2 - 1) as s:
                group(2 * s + 1, lambda: one_hots(2 * s + 2, 0))
                group(2 * s + 2, lambda: one_hots(2 * s + 3, 1))
            group(GROUPS - 1, lambda: over_one_hot(0))
            dve.wait_ge(up[1], STEPS)
            for b in range(TB):
                step(tt2(x[:, b, :].rearrange("p (q k) -> p k q", k=DK), x_hi[:, b].bitcast(F32), x_lo[:, b].bitcast(F32),
                         ALU.add))
            over = dve.value_load(cnt[0:1, 0:1], min_val=1, max_val=XU // 2)
            with dve.Fori(0, over) as j:
                dve.wait_ge(S["gath"], 2 * j + (2 * GP * GROUPS + 2))
                dve.wait_ge(S["gated"], j + 2 * STEPS + 1)
                over_one_hot(j + 1)
                pair(j + 2 * STEPS, 0, 1, j + 2 * STEPS, j + 2 * STEPS)
            for b in range(TB):
                dve.wait_ge(S["combined"], over + 2 * STEPS + b)
                step(nc.vector.scalar_tensor_tensor(x[:, b, :], x[:, b, :], ALPHA,
                                                    ps[:, 2 * b:2 * b + 2, :].rearrange("p a n -> p (a n)"),
                                                    ALU.mult, ALU.add))
                layer_norm(b)
                if b == 0:
                    dve.wait_ge(S["ln_rstd"], 5)
                    step(nc.vector.reciprocal(stat[:, 6:7], stat[:, 4:5]))
                    nc.vector.scalar_tensor_tensor(stat[:, 8:9], stat[:, 0:1], -1.0, stat[:, 6:7],
                                                   ALU.mult, ALU.mult).then_inc(S["ln_shift"], 1)
            dve.wait_ge(S["ld_ln"], 96)
            layer_norm_end(1, 5, S["final1"])

        @block.tensor
        def _(pe):
            def mm(o, l, r, start=True, stop=True, **k):
                return nc.tensor.matmul(o, l, r, start=start, stop=stop, **k)

            fl = lambda t: t.rearrange("p g c -> p (g c)")
            nj = C["nj"]
            pe.wait_ge(S["ld_const"], 16)
            pe.wait_ge(S["ld_par"], 48)
            mm(ps[:, 6, :], nj, fl(bs)).then_inc(S["j_b"], 1)
            for b in range(TB):
                pe.wait_ge(S["x_ready"], b + 1)
                for q in range(2):
                    for k in range(4):
                        c = (4 * q + k) * P
                        last = nc.tensor.transpose(ps[:, 2 * b + q, k * P:(k + 1) * P], x[:, b, c:c + P], ident)
                    last.then_inc(S["xT_ps"], 1)
            for b in range(TB):
                pe.wait_ge(S["xT_sb"], 2 * b + 2)
                if b:
                    pe.wait_ge(S["bbar_done"], 1)
                    mm(ps[:, 0, :], nj, fl(bbar)).then_inc(S["j_bbar"], 1)
                    pe.wait_ge(S["cbar_done"], 1)
                    pe.wait_ge(S["nbs_sb"], 1)
                for k in range(DK):
                    if b == 0 and k % (DK // 2) == 0:
                        pe.wait_ge(S[f"ld_w_in{2 * k // DK}"], 16)
                    if b == 0 and k == 1:
                        pe.wait_ge(S["bb_signed"], 1)
                        mm(ps[:, 7, :], nj, fl(ca)).then_inc(S["j_c"], 1)
                    l = xT[:, k, b * P:(b + 1) * P]
                    m0 = mm(ps[:, 4 + 2 * b, 0:CW], l, w_in[:, k, 0:CW], start=(k == 0), stop=(k == DK - 1))
                    m1 = mm(ps[:, 5 + 2 * b, :], l, w_in[:, k, CW:], start=(k == 0), stop=(k == DK - 1))
                m0.then_inc(S["proj"], 1)
                m1.then_inc(S["proj"], 1)
            def wbt(r):
                if r >= 4:
                    pe.wait_ge(S["wbt_sb"], r - 3)
                for g in range(4):
                    last = nc.tensor.transpose(ps[:, r % 4, g * P:(g + 1) * P],
                                               wpre[:, 4 * r + g, :, :].rearrange("p j c -> p (j c)"), ident)
                last.then_inc(S["wbt_ps"], 1)

            pe.wait_ge(S["wpre_done"], 1)
            pe.wait_ge(S["j_read"], 1)
            for r in range(4):
                wbt(r)
            pe.wait_ge(S["cn_ready"], 2)
            pe.wait_ge(S["u_sb"], 2)
            pe.wait_ge(S["h_sb"], 2)
            for k in range(3):
                for b in range(TB):
                    last = nc.tensor.transpose(ps[:, 4 + k, b * P:(b + 1) * P], hc[:, b, k * P:(k + 1) * P], ident)
            last.then_inc(S["cT_ps"], 1)
            for r in range(4, 8):
                wbt(r)
            pe.wait_ge(S["cT_sb"], 3)
            pe.wait_ge(S["ld_attn_w"], 32)

            def qkv(b):
                if b:
                    pe.wait_ge(S["qkv_sb"], 3)
                for a in range(2):
                    for k in range(2):
                        last = mm(ps[:, 4 + a, 0:4 * QK], cT[:, k, :][:, b * P:(b + 1) * P],
                                  wuq[:, k, a * 4 * QK:(a + 1) * 4 * QK], start=(k == 0), stop=(k == 1))
                last.then_inc(S["qkv_ps"], 1)
                for a in range(2):
                    last = mm(ps[:, 6 + a, :], cT[:, 2, :][:, b * P:(b + 1) * P], wukv[:, a * 512:(a + 1) * 512])
                last.then_inc(S["qkv_ps"], 1)

            qkv(0)
            pe.wait_ge(S["ucg_ready"], 1)
            pe.wait_ge(S["wbt_sb"], 8)
            for r in range(2):
                for g in range(16):
                    last = nc.tensor.transpose(ps[:, r, g * NC:(g + 1) * NC],
                                               ucg[:, 16 * r + g].rearrange("p j c -> p (j c)"), ident[0:NC, 0:NC])
                last.then_inc(S["ug_ps"], 1)
            qkv(1)
            pe.wait_ge(S["ug_sb"], 2)
            for r in range(G // 4):
                for q in range(4):
                    g = q * (G // 4) + r
                    last = mm(ps[NC * q:NC * (q + 1), 2 + r // 4, (r % 4) * P:(r % 4 + 1) * P], ug[:, g, :], wb[:, g, :])
                if r % 4 == 3:
                    last.then_inc(S["bt_ps"], 1)
            for r in range(G // 4):
                pe.wait_ge(S["bt_sb"], r // 4 + 1)
                last = nc.tensor.transpose(ps[:, r // 4, (r % 4) * P:(r % 4 + 1) * P], bt[:, r, :], ident)
                if r % 4 == 3:
                    last.then_inc(S["b_ps"], 1)

            pe.wait_ge(S["wc_done"], 1)
            for r in range(G // 4):
                for q in range(4):
                    g = q * (G // 4) + r
                    last = mm(ps[NC * q:NC * q + CH, 2 + r // 4, (r % 4) * P:(r % 4 + 1) * P], bbar[:, g, :],
                              wc[:, g, 0:L, :].rearrange("p i c -> p (i c)"))
            last.then_inc(S["kall_ps"], 1)
            pe.wait_ge(S["b_sb"], 2)
            for r in range(2):
                mm(ps[:, r, :], nj, sb_b[:, 16 * r:16 * r + 16, :].rearrange("p g c -> p (g c)")).then_inc(S["nb_ps"], 1)
            pe.wait_ge(S["heads_ready"], 1)
            pe.wait_ge(S["qkv_sb"], 6)
            for t in range(2):
                if t:
                    pe.wait_ge(S["hT_sb"], 1)
                for h in range(H):
                    for b in range(TB):
                        c = (h % 2) * T + b * P
                        last = nc.tensor.transpose(ps[0:QKX, 4 + h // 2, c:c + P], (qf, kf)[t][:, b, h, :], ident)
                last.then_inc(S["hT_ps"], 1)
            pe.wait_ge(S["z_done"], 1)
            pe.wait_ge(S["kall_sb"], 4)
            for r in range(2):
                mm(ps[:, 2 + r, :], nj, sb_z[:, 16 * r:16 * r + 16, :].rearrange("p g c -> p (g c)")).then_inc(S["nz_ps"], 1)
            pe.wait_ge(S["hT_sb"], 2)

            def scores(r):
                heads = range(8) if r == 0 else range(4 * (r - 1), 4 * r)
                bank = (4, 6, 2)[r]
                w = P if r == 0 else T
                flat = ps[:, bank:bank + 2, :].rearrange("p a n -> p (a n)")
                for m, h in enumerate(heads):
                    q0 = 0 if r == 0 else P
                    last = mm(flat[:, m * w:(m + 1) * w], qT[0:QKX, h, q0:q0 + P], kT[0:QKX, h, 0:w])
                last.then_inc(S["sc_ps"], 1)

            scores(0)
            scores(1)
            pe.wait_ge(S["s_done"], 1)
            scores(2)
            pe.wait_ge(S["kall_dma"], 16 * L)
            for r in range(G // 4):
                spot = [ps[NC * q:NC * (q + 1), r // 4, (r % 4) * P:(r % 4 + 1) * P] for q in range(4)]
                for q in range(4):
                    mm(spot[q], ug[:, q * (G // 4) + r, :], toep[:, q * (G // 4) + r, :], stop=False)
                for q in range(4):
                    g = q * (G // 4) + r
                    last = mm(spot[q], sb_s[:, g, 0:NC], wc[:, g, 1:, :].rearrange("p i c -> p (i c)"), start=False)
                if r % 4 == 3:
                    last.then_inc(S["y_ps"], 1)
            pe.wait_ge(S["p_sb"], 2)
            for h in range(H):
                last = nc.tensor.transpose(ps[:, 6 + h // 4, (h % 4) * P:(h % 4 + 1) * P], prob[:, h * P:(h + 1) * P], ident)
            last.then_inc(S["pT_ps"], 1)
            for r in range(2):
                if r:
                    pe.wait_ge(S["p_sb"], 3)
                    pe.wait_ge(S["pT_sb"], 1)
                for m in range(4):
                    for k in range(2):
                        c = 1024 + (4 * r + m) * T + k * P
                        j = 2 * m + k
                        last = nc.tensor.transpose(ps[:, (4, 6)[r] + j // 4, (j % 4) * P:(j % 4 + 1) * P],
                                                   prob[:, c:c + P], ident)
                last.then_inc(S["pT_ps"], 1)
            pe.wait_ge(S["pT_sb"], 3)
            def transpose_y():
                pe.wait_ge(S["ld_y"], 16)
                pe.wait_ge(S["yg"], 2)
                for k in range(4):
                    for b in range(TB):
                        c = (k % 2) * T + b * P
                        last = nc.tensor.transpose(ps[:, k // 2, c:c + P], u1[:, b, k * P:(k + 1) * P], ident)
                last.then_inc(S["yT_ps"], 1)

            for b in range(TB):
                for h in range(H):
                    if b == 1 and h == 7:
                        transpose_y()
                    for k in range(b + 1):
                        l = pt0[:, h, :] if b == 0 else pt1[:, h, k, :]
                        last = mm(ps[:, 4 + b, h * VD:(h + 1) * VD], l, vv[:, k, h * VD:(h + 1) * VD],
                                  start=(k == 0), stop=(k == b))
                last.then_inc(S["pv_ps"], 1)
            pe.wait_ge(S["yT_sb"], 1)
            pe.wait_ge(S["ld_glu"], 32)
            for b in range(TB):
                for k in range(4):
                    last = mm(ps[:, 2 + b, :], yT[:, k, b * P:(b + 1) * P], wglu[:, k, :], start=(k == 0), stop=(k == 3))
                last.then_inc(S["glu_ps"], 1)
                if b == 0:
                    pe.wait_ge(S["att_ready"], 2)
                    for q in range(2):
                        for k in range(2 * q, 2 * q + 2):
                            for t in range(TB):
                                c = (k % 2) * T + t * P
                                last = nc.tensor.transpose(ps[:, 6 + q, c:c + P], att[:, t, k * P:(k + 1) * P], ident)
                        last.then_inc(S["attT_ps"], 1)

            def project(half, b):
                pe.wait_ge(S["mT_sb"], 4 * half + 4)
                for c in range(2):
                    for k in range(4 * half, 4 * half + 4):
                        last = mm(ps[:, 4 + 2 * b + c, :], mT[:, k, b * P:(b + 1) * P], wo[:, k, c * 512:(c + 1) * 512],
                                  start=(k == 0), stop=(k == 7))
                    if half:
                        last.then_inc(S["mix_ps"], 1)

            pe.wait_ge(S["ld_wo"], 32)
            project(0, 0)
            pe.wait_ge(S["mix_ready"], 2)
            for q in range(2):
                for k in range(2 * q, 2 * q + 2):
                    for b in range(TB):
                        c = (k % 2) * T + b * P
                        last = nc.tensor.transpose(ps[:, q, c:c + P], u1[:, b, k * P:(k + 1) * P], ident)
                last.then_inc(S["ssmT_ps"], 1)
            project(0, 1)
            project(1, 0)
            project(1, 1)
            for b in range(TB):
                pe.wait_ge(S["x1_ready"], b + 1)
                for q in range(2):
                    for k in range(4):
                        last = nc.tensor.transpose(ps[:, 2 * b + q, k * P:(k + 1) * P],
                                                   x[:, b, 4 * q + k:D:DK], ident)
                    last.then_inc(S["x1T_ps"], 1)
                pe.wait_ge(S["x1T_sb"], 2 * b + 2)
                pe.wait_ge(S["ld_shared"], 64)
                for k in range(DK):
                    last = mm(ps[:, 5 - b, 0:E], xT[:, k, b * P:(b + 1) * P], wr[:, k, :],
                              start=(k == 0), stop=(k == DK - 1))
                last.then_inc(S["router_ps"], 1)

            def shared_up(b, ks):
                for k in ks:
                    last = mm(ps[:, 6, :], xT[:, k, b * P:(b + 1) * P], wsg[:, :, k, :], start=(k == 0), stop=(k == DK - 1))
                if k == DK - 1:
                    last.then_inc(S["sh_up"], 1)

            def shared_rest():
                pe.wait_ge(S["y0"], (2 * MIDDLE + 1) * GP)
                shared_up(1, range(DK))
                pe.wait_ge(S["y1"], (2 * MIDDLE + 1) * GP)
                pe.wait_ge(S["sh_h"], 2)
                for b in range(TB):
                    for k in range(FK):
                        last = nc.tensor.transpose(ps[:, 7, b * FF + k * P:b * FF + (k + 1) * P], hs[:, b, k:FF:FK], ident)
                    last.then_inc(S["sh_tps"], 1)
                pe.wait_ge(S["sh_tps_sb"], 1)
                for b in range(TB):
                    for c in range(2):
                        for k in range(FK):
                            mm(ps[:, 2 * b + c, :], hT[:, b, k * P:(k + 1) * P], wsd[:, k, c * 512:(c + 1) * 512],
                                      start=False, stop=False, skip_group_check=True)

            def gather_bank(bank, cols, ks, hot):
                for k in ks:
                    for t in range(TB):
                        for x_part in (x_hi, x_lo):
                            last = mm(ps[:, bank, cols(k)], x_part[:, t, k, :], hot[:, t],
                                      start=(t == 0 and x_part is x_hi), stop=(t == TB - 1 and x_part is x_lo))
                last.then_inc(S["gath"], 1)

            def part(n, buf, r):
                hot = pm[:, buf].rearrange("p t u s -> p t (u s)")
                for q in range(2):
                    wait_from_1(pe, S["xg_sb"], n * (2 * GP) + 2 * r + q - 1)
                    gather_bank(4 + q, lambda k: slice(0, 512), (2 * r + q,), hot)

            def over_part(j, q):
                pe.wait_ge(S["onehot"], j + GROUPS + 1)
                pe.wait_ge(S["xg_sb"], 2 * j + (2 * GP * GROUPS + q - 1))
                hot = pm[:, 0, :, 0:2, :].rearrange("p t u s -> p t (u s)")
                gather_bank(4 + q, lambda k: slice((k % 4) * P, (k % 4 + 1) * P), range(4 * q, 4 * q + 4), hot)

            def combine(b, t, start=False):
                for c in range(2):
                    for y in (y_hi, y_lo):
                        last = mm(ps[:, 2 * t + c, :], oneT[:, b, t * P:(t + 1) * P], y[:, c * 512:(c + 1) * 512],
                                  start=start and y is y_hi, stop=False, skip_group_check=True)
                return last

            def pair(i, b, loads, weights, gathered, tokens, beside, before, combine_first=False):
                def combine_before():
                    start = isinstance(i, int) and i == 1
                    combine(before, 0, start)
                    combine(before, 1, start).then_inc(S["combined"], 1)

                pe.wait_ge(S["xg_sb"], gathered)
                wait_from_1(pe, S["y0"], i)
                for k in range(DK):
                    weights(k)
                    for u in range(2):
                        last = mm(ps[CAP * u:CAP * (u + 1), 6, :], tokens(k, u),
                                  unit_w(b, u)[0][:, :, k, :], start=(k == 0), stop=(k == DK - 1))
                    if k == DK // 2 - 1:
                        last.then_inc(up_half[b], 1)
                        if combine_first:
                            pe.wait_ge(S["y1"], i)
                            combine_before()
                last.then_inc(up[b], 1)
                if not combine_first:
                    beside()
                pe.wait_ge(S["h_ready"], i + 1)
                pe.wait_ge(S["gated"], i + 1)
                wait_from_1(pe, S["y1"], i)
                for k in range(FK):
                    nc.tensor.transpose(ps[:, 7, k * P:(k + 1) * P], hb[:, b, k:FF:FK], ident)
                for t in range(TB):
                    last = nc.tensor.transpose(ps[:, 7, FF + t * P:FF + (t + 1) * P],
                                               pg[:, b, t].rearrange("p u s -> p (u s)"), ident)
                last.then_inc(S["tps"], 1)
                if combine_first:
                    beside()
                elif not (isinstance(i, int) and i == 0):
                    combine_before()
                pe.wait_ge(S["tps_sb"], i + 1)
                pe.wait_ge(wd_in[b], 16 * loads)
                pe.wait_ge(S["one_sb"], i + 1)
                pe.wait_ge(S["gate_sb"], i + 1)
                for c in range(2):
                    for k in range(FK):
                        for u in range(2):
                            last = mm(ps[CAP * u:CAP * (u + 1), 6 + c, :],
                                      hT[:, b, k * P + CAP * u:k * P + CAP * (u + 1)],
                                      unit_w(b, u)[1][:, k, c * 512:(c + 1) * 512],
                                      start=(k == 0), stop=(k == FK - 1))
                    last.then_inc(S["down_left"] if c == 0 else down[b], 1)

            def group_pair(n, m, buf, beside):
                loads = n * (GP // 2) + m // 2 + 1

                def weights(k):
                    if k % (DK // 2) == 0:
                        pe.wait_ge(wgu_in[m % 2][2 * k // DK], 32 * loads)

                pair(n * GP + m, m % 2, loads, weights, n * (2 * GP) + 2 * GP,
                     lambda k, u: xg[buf][k][:, m, CAP * u:CAP * (u + 1)], beside, 1 - m % 2)

            def group(n, buf):
                pe.wait_ge(S["onehot"], n + 2)
                for m in range(GP):
                    group_pair(n, m, buf, lambda: part(n + 1, 1 - buf, m))

            shared_up(0, range(4))
            pe.wait_ge(S["chosen"], 2)
            ch = rt[:, 3, :, :]
            mm(ps[:, 7, 0:E], C["tri"], ch[:, 0, :])
            mm(ps[:, 7, E:2 * E], C["ones"], ch[:, 0, :], stop=False)
            mm(ps[:, 7, E:2 * E], C["tri"], ch[:, 1, :], start=False)
            mm(ps[0:E, 7, 128:129], ch[:, 0, :], C["ones"][:, 0:1], stop=False)
            mm(ps[0:E, 7, 128:129], ch[:, 1, :], C["ones"][:, 0:1], start=False).then_inc(S["rank_ps"], 1)
            shared_up(0, range(4, 6))
            pe.wait_ge(S["onehot"], 1)
            pe.wait_ge(S["x_lo_ready"], 2)
            pe.wait_ge(S["x_hi_ready"], 2)
            part(0, 0, 0)
            shared_up(0, range(6, DK))
            pe.wait_ge(S["tables"], 1)
            mm(ps[0:E, 7, 130:131], C["tri"][0:E, 0:E], ev[:, 1, 0:1])
            mm(ps[0:1, 7, 352:353], C["ones"][0:E, 0:1], ev[:, 1, 0:1]).then_inc(S["tab_ps"], 1)
            pe.wait_ge(S["gates_ready"], 1)
            for k, t in enumerate((ru, gu)):
                for b in range(TB):
                    last = mm(ps[0:E, 2, k * T + b * P:k * T + (b + 1) * P], t[:, b, 0:E], ident)
            last.then_inc(S["rt_ps"], 1)
            for r in range(1, GP):
                part(0, 0, r)

            def tables():
                pe.wait_ge(S["rt_sb"], 1)
                for b in range(TB):
                    o = ps[:, 7, 192 + b * XU:192 + (b + 1) * XU]
                    mm(o, rte[:, 0, b * P:(b + 1) * P], ev[:, 6, :], stop=False)
                    mm(o, C["ones"][0:E, :], ev[:, 7, :], start=False)
                    mm(ps[:, 7, 256 + b * XU:256 + (b + 1) * XU], rte[:, 1, b * P:(b + 1) * P], ev[:, 6, :])
                mm(ps[0:1, 7, 320:320 + XU], C["eid"][0:E, :], ev[:, 6, :]).then_inc(S["tab2_ps"], 1)
                pe.wait_ge(S["over_ready"], 2)
                pe.wait_ge(S["onehot"], 2)

            pe.wait_ge(S["sh_h"], 1)
            for m in range(GP):
                group_pair(0, m, 0, lambda: (tables() if m == 0 else None, part(1, 1, m)))
            with pe.Fori(0, MIDDLE) as s:
                group(2 * s + 1, 1)
                group(2 * s + 2, 0)
            shared_rest()
            with pe.Fori(MIDDLE, GROUPS // 2 - 1) as s:
                group(2 * s + 1, 1)
                group(2 * s + 2, 0)
            for m in range(GP):
                group_pair(GROUPS - 1, m, 1, (lambda: over_part(0, m)) if m < 2 else (lambda: None))
            over = pe.value_load(cnt[0:1, 0:1], min_val=1, max_val=XU // 2)
            with pe.Fori(0, over) as j:
                def weights(k):
                    if k % (DK // 2) == 0:
                        pe.wait_ge(over_gu_in[2 * k // DK], 64 * (j + 1))

                pair(j + 2 * STEPS, 0, 2 * j + (STEPS + 2), weights, 2 * j + (2 * GP * GROUPS + 2),
                     lambda k, u: xg[0][k][:, 0, CAP * u:CAP * (u + 1)], lambda: over_part(j + 1, 0), 1, True)
                over_part(j + 1, 1)
            pe.wait_ge(S["y0"], over + 2 * STEPS)
            pe.wait_ge(S["y1"], over + 2 * STEPS)
            for t in range(TB):
                combine(1, t).then_inc(S["combined"], 1)


def kernel(**inputs):
    import concourse.bacc as bacc
    from concourse.bass_utils import run_bass_kernel_spmd

    a = {k: np.asarray(v) for k, v in inputs.items()}

    def states(re, im):
        return np.ascontiguousarray(np.concatenate([re.transpose(1, 0, 2), im.transpose(1, 0, 2)]))

    def twice(t):
        return np.concatenate([t.T, t.T])

    const, low8 = constants()
    arrays = {"const": const, "low8": low8}
    for name in ("x", "ln_in_g", "ln_in_b", "w_in", "w_uq", "w_ukv", "w_glu", "b_glu", "w_o", "ln1_g", "ln1_b",
                 "w_router", "router_bias", "ws_gate", "ws_up", "ws_down", "ln2_g", "ln2_b"):
        arrays[name] = np.ascontiguousarray(a[name])
    for name in ("w_gate", "w_up", "w_down"):
        arrays[name] = np.ascontiguousarray(a[name][0])
    step = np.broadcast_to(a["log_step"][0][None, :], (P, G))
    arrays["lam"] = np.ascontiguousarray(np.stack([twice(a["lambda_re"][0]), twice(a["lambda_im"][0]), step], 1))
    arrays["bstack"] = states(a["b_re"][0], a["b_im"][0])
    arrays["cstack"] = states(a["c_re"][0].transpose(0, 2, 1), a["c_im"][0].transpose(0, 2, 1))
    rows = [a["q_norm_g"][0], a["kv_norm_g"][0], a["attn_out_g"][0], a["ssm_out_g"][0]]
    vec = np.concatenate([r.reshape(-1, P) for r in rows])
    arrays["vec"] = np.ascontiguousarray(np.concatenate([vec, vec[:4]]).T)
    arrays["dskip"] = np.ascontiguousarray(a["d_skip"][0].T)
    arrays["pos"] = np.ascontiguousarray(a["positions"].reshape(TB, P).T)

    nc = bacc.Bacc("TRN2", target_bir_lowering=False, num_devices=1)
    A, sent = {}, {}
    for name, v in arrays.items():
        sent[f"in_{name}"] = v
        A[name] = nc.dram_tensor(f"in_{name}", v.shape, mybir.dt.from_np(v.dtype), kind="ExternalInput").ap()
    out = nc.dram_tensor("out_x", (1, T, D), F32, kind="ExternalOutput").ap()
    build(nc, A, out)
    r = run_bass_kernel_spmd(nc, [sent], core_ids=[0])
    return r.results[0]["out_x"]
```
